# Optimizing a Trainium2 kernel written in Bass

```python
import math
import jax, jax.numpy as jnp
from jax import lax
import numpy as np

D_MODEL = 1024
BATCH = 1
SEQ = 512
DEPTH = 1
DEC_BATCH = 1
DEC_SEQ = 1024
PAST_LEN = 128

HEAD_DIM = 64
RWKV_WIDTH = D_MODEL // 2
RWKV_HEADS = RWKV_WIDTH // HEAD_DIM
ATTN_WIDTH = D_MODEL - RWKV_WIDTH
ATTN_HEADS = ATTN_WIDTH // HEAD_DIM
KV_HEADS = 2
KV_WIDTH = KV_HEADS * HEAD_DIM
Q_PER_KV = ATTN_HEADS // KV_HEADS
DECAY_LORA = 32
ICLR_LORA = 32
GATE_LORA = 64
D_FF = int(math.ceil(8 * D_MODEL / 3 / 256)) * 256
N_META = 16
GRID_W = 64
ROPE_THETA = 10000.0
ROPE_FREQS = HEAD_DIM // 4
BLOCK_Q = 128
DEEPNORM_ALPHA = (2.0 * DEPTH) ** 0.25
DEEPNORM_BETA = (8.0 * DEPTH) ** -0.25
LN_EPS = 1e-5
GN_EPS = 64e-5
QK_EPS = 1e-6
R_END = RWKV_WIDTH
K_END = 2 * RWKV_WIDTH
V_END = 3 * RWKV_WIDTH
WLO_END = V_END + DECAY_LORA
ALO_END = WLO_END + ICLR_LORA
RWKV_IN_WIDTH = ALO_END + GATE_LORA
Q_END = RWKV_IN_WIDTH + ATTN_WIDTH
AK_END = Q_END + KV_WIDTH
IN_WIDTH = AK_END + KV_WIDTH

kernel_name = "hymba_rwkv7_axial_gqa_deepnorm_encoder"

F32 = jnp.float32

def _heads(t):
    return t.reshape(t.shape[:-1] + (-1, HEAD_DIM))

def layer_norm(x, g, b):
    xf = x.astype(F32)
    mu = jnp.mean(xf, axis=-1, keepdims=True)
    var = jnp.mean(jnp.square(xf - mu), axis=-1, keepdims=True)
    y = (xf - mu) * lax.rsqrt(var + LN_EPS) * g.astype(F32) + b.astype(F32)
    return y.astype(x.dtype)

def token_shift_centred(p, mu_prev, mu_next):
    prev = jnp.pad(p[:, :-1], ((0, 0), (1, 0), (0, 0)))
    nxt = jnp.pad(p[:, 1:], ((0, 0), (0, 1), (0, 0)))
    return p + mu_prev * (prev - p) + mu_next * (nxt - p)

def _wkv_step(S, xs):
    r_t, w_t, k_t, v_t, kk_t, a_t = xs
    sa = jnp.einsum('zbhvk,zbhk->zbhv', S, -kk_t)
    S = (S * w_t[..., None, :]
         + sa[..., :, None] * (kk_t * a_t)[..., None, :]
         + v_t[..., :, None] * k_t[..., None, :])
    o = jnp.einsum('zbhvk,zbhk->zbhv', S, r_t)
    return S, o

def rwkv7_bidir(p, mu, w0, w_up, a0, a_up, g_up, k_k, k_a, r_k, gn_g, gn_b):
    dtype = p.dtype
    p = p.astype(F32)
    B, T, _ = p.shape
    mu = mu.astype(F32)
    p = token_shift_centred(p, mu[0], mu[1])
    r, k, v, w_lo, a_lo, g_lo = jnp.split(p, [R_END, K_END, V_END, WLO_END, ALO_END], axis=-1)
    w = w0.astype(F32)[:, None, None, :] + jnp.einsum('btr,zrc->zbtc', jnp.tanh(w_lo), w_up.astype(F32))
    decay = jnp.exp(-jnp.exp(-jax.nn.softplus(-w) - 0.5))
    a = jax.nn.sigmoid(a0.astype(F32)[:, None, None, :]
                       + jnp.einsum('btr,zrc->zbtc', a_lo, a_up.astype(F32)))
    g = jax.nn.sigmoid(g_lo) @ g_up.astype(F32)
    kk = _heads(k * k_k.astype(F32))
    kk = kk / jnp.maximum(jnp.sqrt(jnp.sum(kk * kk, axis=-1, keepdims=True)), 1e-12)
    k_dir = k[None] * (1.0 + (a - 1.0) * k_a.astype(F32))
    rh, vh = _heads(r), _heads(v)

    def both(t):
        return jnp.broadcast_to(t[None], (2,) + t.shape)

    seqs = (both(rh), _heads(decay), _heads(k_dir), both(vh), both(kk), _heads(a))
    seqs = tuple(jnp.moveaxis(jnp.stack([t[0], jnp.flip(t[1], axis=1)]), 2, 0) for t in seqs)
    S0 = jnp.zeros((2, B, RWKV_HEADS, HEAD_DIM, HEAD_DIM), F32)
    _, o = lax.scan(_wkv_step, S0, seqs)
    o = jnp.moveaxis(o, 0, 2)
    o = o[0] + jnp.flip(o[1], axis=1)
    mo = jnp.mean(o, axis=-1, keepdims=True)
    vo = jnp.mean(jnp.square(o - mo), axis=-1, keepdims=True)
    o = (o - mo) * lax.rsqrt(vo + GN_EPS) * _heads(gn_g.astype(F32)) + _heads(gn_b.astype(F32))
    bonus = jnp.sum(rh * _heads(k_dir[0] + k_dir[1]) * r_k.astype(F32), axis=-1, keepdims=True) * vh
    out = (o + bonus).reshape(B, T, RWKV_WIDTH) * g
    return out.astype(dtype)

def axial_rope_tables(n_tokens):
    rows = n_tokens // GRID_W
    row_idx = jnp.repeat(jnp.arange(rows), GRID_W)
    col_idx = jnp.tile(jnp.arange(GRID_W), rows)
    pos = jnp.stack([row_idx, col_idx], axis=-1).astype(F32)
    inv_freq = ROPE_THETA ** (-jnp.arange(ROPE_FREQS, dtype=F32) / ROPE_FREQS)
    ang = pos[:, :, None] * inv_freq
    ang = jnp.concatenate([jnp.zeros((N_META, 2, ROPE_FREQS), F32), ang], axis=0)
    return jnp.cos(ang), jnp.sin(ang)

def apply_axial_rope(x, cos, sin):
    xr = x.reshape(x.shape[:-1] + (2, 2, ROPE_FREQS))
    x1, x2 = xr[..., 0, :], xr[..., 1, :]
    c = cos[None, :, None]
    s = sin[None, :, None]
    out = jnp.stack([x1 * c - x2 * s, x2 * c + x1 * s], axis=-2)
    return out.reshape(x.shape)

def rms_heads(x, g):
    return x * lax.rsqrt(jnp.mean(x * x, axis=-1, keepdims=True) + QK_EPS) * g.astype(F32)

def attend_block(qb, k, v):
    s = jnp.einsum('bqhgd,bkhd->bhgqk', qb, k) * (HEAD_DIM ** -0.5)
    pr = jax.nn.softmax(s, axis=-1)
    return jnp.einsum('bhgqk,bkhd->bqhgd', pr, v)

def axial_gqa(pq, pk, pv, q_gain, k_gain, cos, sin):
    dtype = pq.dtype
    B, T, _ = pq.shape
    q = apply_axial_rope(rms_heads(_heads(pq.astype(F32)), q_gain), cos, sin)
    k = apply_axial_rope(rms_heads(_heads(pk.astype(F32)), k_gain), cos, sin)
    v = _heads(pv.astype(F32))
    q = q.reshape(B, T, KV_HEADS, Q_PER_KV, HEAD_DIM)
    meta_out = attend_block(q[:, :N_META], k, v)
    n_blk = (T - N_META) // BLOCK_Q
    qr = q[:, N_META:].reshape(B, n_blk, BLOCK_Q, KV_HEADS, Q_PER_KV, HEAD_DIM)
    qr = jnp.moveaxis(qr, 1, 0)
    real_out = lax.map(lambda qb: attend_block(qb, k, v), qr)
    real_out = jnp.moveaxis(real_out, 0, 1).reshape(B, T - N_META, KV_HEADS, Q_PER_KV, HEAD_DIM)
    out = jnp.concatenate([meta_out, real_out], axis=1)
    return out.reshape(B, T, ATTN_WIDTH).astype(dtype)

def encoder_layer(x, lp, cos, sin):
    proj = x @ lp['w_in']
    y_rwkv = rwkv7_bidir(proj[..., :RWKV_IN_WIDTH], lp['shift_mu'], lp['decay_w0'], lp['decay_up'],
                         lp['iclr_a0'], lp['iclr_up'], lp['gate_up'], lp['k_k'], lp['k_a'],
                         lp['r_k'], lp['gn_g'], lp['gn_b'])
    y_attn = axial_gqa(proj[..., RWKV_IN_WIDTH:Q_END], proj[..., Q_END:AK_END], proj[..., AK_END:],
                       lp['q_gain'], lp['k_gain'], cos, sin)
    mix = jnp.concatenate([y_rwkv, y_attn], axis=-1) @ lp['w_out']
    x = layer_norm(DEEPNORM_ALPHA * x + mix, lp['ln1_g'], lp['ln1_b'])
    gate, up = jnp.split(x @ lp['w_ffn_in'], 2, axis=-1)
    ffn = (jax.nn.silu(gate) * up) @ lp['w_ffn_out']
    return layer_norm(DEEPNORM_ALPHA * x + ffn, lp['ln2_g'], lp['ln2_b'])

def run_trunk(x, meta_tokens, ln_in_g, ln_in_b, params):
    B, n_tok, _ = x.shape
    cos, sin = axial_rope_tables(n_tok)
    meta = jnp.broadcast_to(meta_tokens[None].astype(x.dtype), (B, N_META, D_MODEL))
    h = layer_norm(jnp.concatenate([meta, x], axis=1), ln_in_g, ln_in_b)
    for l in range(DEPTH):
        lp = {name: arr[l] for name, arr in params.items()}
        h = encoder_layer(h, lp, cos, sin)
    return h[:, N_META:]

def setup_inputs(seed: int = 0) -> dict:
    key = jax.random.key(seed)
    ks = jax.random.split(key, 32)
    nrm = jax.random.normal
    L = DEPTH
    return {
        "x_prompt": nrm(ks[0], (BATCH, SEQ, D_MODEL), F32),
        "x_sample": nrm(ks[1], (DEC_BATCH, DEC_SEQ, D_MODEL), F32),
        "meta_tokens": nrm(ks[2], (N_META, D_MODEL), F32),
        "ln_in_g": 1.0 + 0.02 * nrm(ks[3], (D_MODEL,), F32),
        "ln_in_b": 0.02 * nrm(ks[4], (D_MODEL,), F32),
        "w_in": nrm(ks[5], (L, D_MODEL, IN_WIDTH), F32) * D_MODEL ** -0.5,
        "shift_mu": jax.random.uniform(ks[6], (L, 2, RWKV_IN_WIDTH), F32, 0.0, 0.5),
        "decay_w0": jax.random.uniform(ks[7], (L, 2, RWKV_WIDTH), F32, -6.0, 0.0),
        "decay_up": nrm(ks[8], (L, 2, DECAY_LORA, RWKV_WIDTH), F32) * DECAY_LORA ** -0.5,
        "iclr_a0": 0.1 * nrm(ks[9], (L, 2, RWKV_WIDTH), F32),
        "iclr_up": nrm(ks[10], (L, 2, ICLR_LORA, RWKV_WIDTH), F32) * ICLR_LORA ** -0.5,
        "gate_up": nrm(ks[11], (L, GATE_LORA, RWKV_WIDTH), F32) * GATE_LORA ** -0.5,
        "k_k": 0.85 + 0.05 * nrm(ks[12], (L, RWKV_WIDTH), F32),
        "k_a": 1.0 + 0.05 * nrm(ks[13], (L, RWKV_WIDTH), F32),
        "r_k": 0.1 * nrm(ks[14], (L, RWKV_HEADS, HEAD_DIM), F32),
        "gn_g": 1.0 + 0.02 * nrm(ks[15], (L, RWKV_WIDTH), F32),
        "gn_b": 0.02 * nrm(ks[16], (L, RWKV_WIDTH), F32),
        "q_gain": 1.0 + 0.02 * nrm(ks[17], (L, HEAD_DIM), F32),
        "k_gain": 1.0 + 0.02 * nrm(ks[18], (L, HEAD_DIM), F32),
        "w_out": nrm(ks[19], (L, D_MODEL, D_MODEL), F32) * (D_MODEL ** -0.5 * DEEPNORM_BETA),
        "ln1_g": 1.0 + 0.02 * nrm(ks[20], (L, D_MODEL), F32),
        "ln1_b": 0.02 * nrm(ks[21], (L, D_MODEL), F32),
        "w_ffn_in": nrm(ks[22], (L, D_MODEL, 2 * D_FF), F32) * D_MODEL ** -0.5,
        "w_ffn_out": nrm(ks[23], (L, D_FF, D_MODEL), F32) * (D_FF ** -0.5 * DEEPNORM_BETA),
        "ln2_g": 1.0 + 0.02 * nrm(ks[24], (L, D_MODEL), F32),
        "ln2_b": 0.02 * nrm(ks[25], (L, D_MODEL), F32),
    }

def reference(x_prompt, x_sample, meta_tokens, ln_in_g, ln_in_b, w_in, shift_mu, decay_w0, decay_up,
              iclr_a0, iclr_up, gate_up, k_k, k_a, r_k, gn_g, gn_b, q_gain, k_gain, w_out,
              ln1_g, ln1_b, w_ffn_in, w_ffn_out, ln2_g, ln2_b):
    params = dict(w_in=w_in, shift_mu=shift_mu, decay_w0=decay_w0, decay_up=decay_up,
                  iclr_a0=iclr_a0, iclr_up=iclr_up, gate_up=gate_up, k_k=k_k, k_a=k_a, r_k=r_k,
                  gn_g=gn_g, gn_b=gn_b, q_gain=q_gain, k_gain=k_gain, w_out=w_out,
                  ln1_g=ln1_g, ln1_b=ln1_b, w_ffn_in=w_ffn_in, w_ffn_out=w_ffn_out,
                  ln2_g=ln2_g, ln2_b=ln2_b)
    y_prompt = run_trunk(x_prompt, meta_tokens, ln_in_g, ln_in_b, params)
    y_sample = run_trunk(x_sample, meta_tokens, ln_in_g, ln_in_b, params)
    return (y_prompt, y_sample)


_drawn_inputs = setup_inputs


def setup_inputs(seed=0):
    import zlib

    import numpy as np

    out = dict(_drawn_inputs(seed))
    spreads = {}
    factors = {'ln_in_g': 2.772,
     'decay_up': 6.244,
     'iclr_a0': 8.0,
     'k_k': 125.769,
     'k_a': 5.2,
     'gn_g': 56.47,
     'gn_b': 58.453,
     'q_gain': 30.868,
     'k_gain': 31.384,
     'ln1_g': 2.831,
     'ln2_g': 23.156,
     'ln2_b': 22.814,
     'ln1_b': 6.295}
    for name, (base, spread) in spreads.items():
        noise = np.random.default_rng([zlib.crc32(name.encode()), seed]).standard_normal(out[name].shape)
        drawn = base * np.exp(spread * noise) if base else spread * noise
        out[name] = __import__('jax').numpy.asarray(drawn.astype(out[name].dtype))
    for name, factor in factors.items():
        out[name] = (out[name] * factor).astype(out[name].dtype)
    return out
```

```python
from contextlib import ExitStack

import concourse.bass as bass
from concourse import mybir

ALU = mybir.AluOpType
ACT = mybir.ActivationFunctionType
F32 = mybir.dt.float32
F32R = mybir.dt.float32r
AX = mybir.AxisListType

P = 128
D = 1024
KT = D // P
N_META = 16
SEQS = (512, 1024)
T_REAL = sum(SEQS)
NT = T_REAL // P
META_COL = T_REAL
HEAD = 64
RW = 512
RH = RW // HEAD
RWKV_IN = 1664
MB = RWKV_IN // P
IN_WIDTH = 2432
QKV = IN_WIDTH - RWKV_IN
ATT_H = 8
KV_H = 2
CHUNK = 64
D_FF = 2816
LN_EPS = 1e-5
GN_EPS = 64e-5
QK_EPS = 1e-6
ALPHA = 2.0 ** 0.25
DECAY = 0.6065306597126334
ROW0 = 1
SEG = [(1, 17, 512), (531, 547, 1024)]
ST = 1572


class Tally:

    def __init__(self, sem):
        self.sem, self.base, self.k = sem, 0, 0

    def enter(self, base):
        self.base, self.k = base, 0

    def inc(self, ins):
        ins.then_inc(self.sem, 1)
        self.k += 1
        return self.base + self.k

    def now(self):
        return self.base + self.k


def wait(eng, sem, value):
    if isinstance(value, int) and value <= 0:
        return
    eng.wait_ge(sem, value)


def hold(eng, sem, value, passed):
    if isinstance(value, int) and value <= 0:
        return
    eng.wait_ge(sem, value)
    eng.sem_inc(passed, 1)


def alloc(ctx, nc):
    def sb(name, shape, dt=F32):
        return ctx.enter_context(nc.sbuf_tensor(name, shape, dt))

    def ps(name, shape, dt=F32):
        return ctx.enter_context(nc.psum_tensor(name, shape, dt))

    sems = []

    def sem(name):
        sems.append(nc.alloc_semaphore(name))
        return sems[-1]

    def clear():
        nc.clear_and_free_semaphores(sems)
        nc.all_engine_barrier()

    ctx.callback(clear)
    return sb, ps, sem


def project(nc, d, hT):
    h_hi, h_lo = hT
    with ExitStack() as ctx:
        sb, ps, sem = alloc(ctx, nc)
        ident = sb("pj_ident", [P, P])
        gain = sb("pj_gain", [P, D])
        bias = sb("pj_bias", [P, D])
        neg_half = sb("pj_neg_half", [P, 1])
        x_in = sb("pj_x", [P, 2, D])
        hn = sb("pj_hn", [P, 2, D])
        stats = sb("pj_stats", [P, 2, 12])
        mv = sb("pj_mv", [P, 2, 2])
        rstd = sb("pj_rstd", [P, 2, 1])
        nmr = sb("pj_nmr", [P, 2, 1])
        tp = ps("pj_tp", [P, 4, 512])
        mm = ps("pj_mm", [P, 4, 512])
        x_loaded = [sem("pj_x0"), sem("pj_x1")]
        const_loaded = sem("pj_const")
        ident_made = sem("pj_ident_made")
        stats_done = sem("pj_stats_done")
        rstd_done = sem("pj_rstd_done")
        nmr_done = sem("pj_nmr_done")
        normed = sem("pj_normed")
        gained = sem("pj_gained")
        hn_done = sem("pj_hn_done")
        tp_done = sem("pj_tp_done")
        hi_done = sem("pj_hi_done")
        lo_done = sem("pj_lo_done")
        h_stored = [sem("pj_h_stored0"), sem("pj_h_stored1")]
        vec = sem("pj_vec")
        passed = sem("pj_passed")

        n = NT + 1
        with nc.Block() as block:
            @block.sync
            def _(sp):
                sp.dma_start(ident[:, :], d["ident"]).then_inc(const_loaded, 16)
                sp.dma_start(gain[:, :], d["ln_in_g"].partition_broadcast(P)).then_inc(const_loaded, 16)
                sp.dma_start(bias[:, :], d["ln_in_b"].partition_broadcast(P)).then_inc(const_loaded, 16)

                def load(t, q, turn):
                    wait(sp, normed, t - 1)
                    sp.dma_start(x_in[:, q, :], d["x"][bass.ds(t * P, P), :]).then_inc(x_loaded[q], 16)

                def store(t, q):
                    wait(sp, hn_done, t + 1)
                    sp.dma_start(d["h"][bass.ds(t * P, P), :], hn[:, q, :]).then_inc(h_stored[q], 16)

                load(0, 0, 0)
                load(1, 1, 0)
                with sp.Fori(0, NT // 2 - 1) as i:
                    for q in range(2):
                        load(2 * i + q + 2, q, 0)
                        store(2 * i + q, q)
                load(NT, 0, 0)
                store(NT - 2, 0)
                store(NT - 1, 1)
                sp.wait_ge(h_stored[0], 16 * (NT // 2))
                sp.wait_ge(h_stored[1], 16 * (NT // 2))

            @block.gpsimd
            def _(pool):
                nc.gpsimd.memset(neg_half[:, :], -0.5).then_inc(ident_made, 1)
                pool.wait_ge(ident_made, 1)
                pool.wait_ge(const_loaded, 48)

                def tile(t, q):
                    pool.wait_ge(stats_done, t + 1)
                    nc.gpsimd.tensor_tensor(rstd[:, q, :], mv[:, q, 1:2], neg_half[:, :], ALU.pow).then_inc(rstd_done, 1)
                    pool.wait_ge(gained, t + 1)
                    nc.gpsimd.tensor_tensor(hn[:, q, :], hn[:, q, :], bias[:, :], ALU.add).then_inc(hn_done, 1)

                with pool.Fori(0, NT // 2) as i:
                    tile(2 * i, 0)
                    tile(2 * i + 1, 1)
                tile(NT, 0)

            @block.scalar
            def _(act):
                def tile(t, q, stored):
                    act.wait_ge(nmr_done, t + 1)
                    act.wait_ge(rstd_done, t + 1)
                    wait(act, tp_done, 2 * (t - 1))
                    wait(act, h_stored[q], stored)
                    nc.scalar.activation(hn[:, q, :], x_in[:, q, :], ACT.Identity, bias=nmr[:, q, :], scale=rstd[:, q, :]).then_inc(normed, 1)
                    for b in range(2):
                        act.wait_ge(tp_done, 2 * t + b + 1)
                        nc.scalar.activation(h_hi[:, 4 * b:4 * b + 4, bass.ds(t * P, P)],
                                             tp[:, 2 * q + b, :].rearrange("p (k c) -> p k c", k=4), ACT.Copy).then_inc(hi_done, 1)

                tile(0, 0, 0)
                tile(1, 1, 0)
                with act.Fori(1, NT // 2) as i:
                    tile(2 * i, 0, i * 16)
                    tile(2 * i + 1, 1, i * 16)
                tile(NT, 0, NT // 2 * 16)

            @block.vector
            def _(dve):
                dve.wait_ge(const_loaded, 48)
                step = Tally(vec)

                def stat(t, q, turn):
                    dve.wait_ge(x_loaded[q], 16 * (turn + 1))
                    nc.vector.bn_stats(stats[:, q, 0:6], x_in[:, q, 0:512])
                    v = step.inc(nc.vector.bn_stats(stats[:, q, 6:12], x_in[:, q, 512:1024]))
                    wait(dve, normed, t - 1)
                    hold(dve, vec, v, passed)
                    v = step.inc(nc.vector.bn_aggr(mv[:, q, :], stats[:, q, :]))
                    dve.wait_ge(vec, v)
                    nc.vector.tensor_scalar(mv[:, q, 1:2], mv[:, q, 1:2], LN_EPS, None, ALU.add).then_inc(stats_done, 1)

                def norm(t, q):
                    dve.wait_ge(rstd_done, t + 1)
                    nc.vector.scalar_tensor_tensor(out=nmr[:, q, :], in0=mv[:, q, 0:1], scalar=-1.0, in1=rstd[:, q, :],
                                                   op0=ALU.mult, op1=ALU.mult).then_inc(nmr_done, 1)
                    dve.wait_ge(normed, t + 1)
                    nc.vector.tensor_tensor(hn[:, q, :], hn[:, q, :], gain[:, :], ALU.mult).then_inc(gained, 1)
                    for b in range(2):
                        dve.wait_ge(hi_done, 2 * t + b + 1)
                        hi = h_hi[:, 4 * b:4 * b + 4, bass.ds(t * P, P)]
                        nc.vector.tensor_tensor(h_lo[:, 4 * b:4 * b + 4, bass.ds(t * P, P)],
                                                tp[:, 2 * q + b, :].rearrange("p (k c) -> p k c", k=4),
                                                hi.bitcast(F32), ALU.subtract).then_inc(lo_done, 1)

                stat(0, 0, 0)
                per = 4
                first = step.now()

                def pair(i):
                    step.enter(first + i * per)
                    stat(2 * i + 1, 1, i)
                    norm(2 * i, 0)
                    stat(2 * i + 2, 0, i + 1)
                    norm(2 * i + 1, 1)
                    assert step.k == per

                pair(0)
                with dve.Fori(1, NT // 2) as i:
                    pair(i)
                norm(NT, 0)

            @block.tensor
            def _(pe):
                pe.wait_ge(const_loaded, 48)

                def tile(t, q):
                    pe.wait_ge(hn_done, t + 1)
                    wait(pe, lo_done, 2 * (t - 1))
                    for b in range(2):
                        for k in range(4):
                            last = nc.tensor.transpose(tp[:, 2 * q + b, k * P:(k + 1) * P],
                                                       hn[:, q, (4 * b + k) * P:(4 * b + k + 1) * P], ident[:, :])
                        last.then_inc(tp_done, 1)

                tile(0, 0)
                tile(1, 1)
                with pe.Fori(1, NT // 2) as i:
                    tile(2 * i, 0)
                    tile(2 * i + 1, 1)
                tile(NT, 0)


def columns(nc, d, hT):
    h_hi, h_lo = hT
    with ExitStack() as ctx:
        sb, ps, sem = alloc(ctx, nc)
        ident = sb("co_ident", [P, P])
        mu = sb("co_mu", [P, 2, MB])
        keep = sb("co_keep", [P, MB])
        w_in = sb("co_w", [P, 2, KT, P])
        w_hi = sb("co_w_hi", [P, 2, KT, P], F32R)
        w_lo = sb("co_w_lo", [P, 2, KT, P], F32R)
        raw = sb("co_raw", [P, 2, ST])
        sh = sb("co_sh", [P, ST])
        tm = sb("co_tm", [P, 2, NT, P])
        tm_meta = sb("co_tm_meta", [N_META, 2, 2, P])
        lora = sb("co_lora", [P, ST])
        mm = ps("co_mm", [P, 4, 512])
        tp = ps("co_tp", [P, 4, 512])
        const_loaded = sem("co_const")
        consts_made = sem("co_consts_made")
        w_loaded = [sem("co_w0"), sem("co_w1")]
        hi_done = sem("co_hi_done")
        lo_done = sem("co_lo_done")
        group_done = sem("co_group_done")
        raw_done = sem("co_raw_done")
        vec = sem("co_vec")
        sh_done = sem("co_sh_done")
        tp_done = sem("co_tp_done")
        tm_done = sem("co_tm_done")
        tm_stored = [sem("co_tm_stored0"), sem("co_tm_stored1")]
        lora_done = sem("co_lora_done")
        gate_half = sem("co_gate_half")
        lora_stored = sem("co_lora_stored")
        w_view = d["w_in"].rearrange("(k p) n -> p k n", p=P)

        with nc.Block() as block:
            @block.sync
            def _(sp):
                sp.dma_start(ident[:, :], d["ident"]).then_inc(const_loaded, 16)
                sp.dma_start(mu[:, :, :], d["mu"]).then_inc(const_loaded, 16)

                def load(m, q):
                    wait(sp, lo_done, m - 1)
                    sp.dma_start(w_in[:, q, :, :], w_view[:, :, bass.ds(m * P, P)]).then_inc(w_loaded[q], 16)

                def store(m, q):
                    sp.wait_ge(tm_done, m + 1)
                    sp.dma_start(d["rkv"][0:T_REAL, bass.ds(m * P, P)].rearrange("(t p) f -> p t f", p=P),
                                 tm[:, q, :, :]).then_inc(tm_stored[q], 16)
                    sp.dma_start(d["rkv"][T_REAL:T_REAL + 2 * N_META, bass.ds(m * P, P)].rearrange("(s p) f -> p s f", p=N_META),
                                 tm_meta[:, q, :, :]).then_inc(tm_stored[q], 16)

                load(0, 0)
                load(1, 1)
                load(2, 0)
                with sp.Fori(0, (MB - 3) // 2) as i:
                    load(2 * i + 3, 1)
                    store(2 * i, 0)
                    load(2 * i + 4, 0)
                    store(2 * i + 1, 1)
                store(MB - 3, 0)
                store(MB - 2, 1)
                sp.wait_ge(lora_done, 2)
                sp.wait_ge(gate_half, 1)
                out = d["lora"]
                sp.dma_start(out[:, 0:512], lora[:, 17:529]).then_inc(lora_stored, 16)
                sp.dma_start(out[:, 512:1536], lora[:, 547:1571]).then_inc(lora_stored, 16)
                sp.dma_start(out[:, 1536:1552], lora[:, 1:17]).then_inc(lora_stored, 16)
                sp.dma_start(out[:, 1552:1568], lora[:, 531:547]).then_inc(lora_stored, 16)
                sp.wait_ge(lora_stored, 64)
                for q in range(2):
                    sp.wait_ge(tm_stored[q], 32 * ((MB - 1) // 2))

            @block.gpsimd
            def _(pool):
                for q in range(2):
                    for a in (0, 529, 530, 1571):
                        nc.gpsimd.memset(raw[:, q, a:a + 1], 0.0).then_inc(consts_made, 1)

                def split(m, q, turn):
                    pool.wait_ge(hi_done, m + 1)
                    nc.gpsimd.tensor_tensor(w_lo[:, q, :, :], w_in[:, q, :, :], w_hi[:, q, :, :].bitcast(F32),
                                            ALU.subtract).then_inc(lo_done, 1)

                split(0, 0, 0)
                with pool.Fori(0, (MB - 1) // 2) as i:
                    split(2 * i + 1, 1, i)
                    split(2 * i + 2, 0, i + 1)

            @block.scalar
            def _(act):
                def split(m, q, turn):
                    act.wait_ge(w_loaded[q], 16 * (turn + 1))
                    wait(act, group_done, 3 * (m - 1))
                    nc.scalar.activation(w_hi[:, q, :, :], w_in[:, q, :, :], ACT.Copy).then_inc(hi_done, 1)

                def evict(m, q):
                    wait(act, sh_done, m - 1)
                    for g, to in ((0, 17), (1, 547), (2, 1059)):
                        act.wait_ge(group_done, 3 * m + g + 1)
                        if g == 2:
                            for at in (1, 531):
                                nc.scalar.activation(raw[:, q, at:at + N_META], mm[:, 3, 0:N_META], ACT.Copy).then_inc(raw_done, 1)
                        nc.scalar.activation(raw[:, q, to:to + 512], mm[:, g, :], ACT.Copy).then_inc(raw_done, 1)

                split(0, 0, 0)
                split(1, 1, 0)
                evict(0, 0)

                def pair(i):
                    split(2 * i + 2, 0, i + 1)
                    evict(2 * i + 1, 1)
                    split(2 * i + 3, 1, i + 1)
                    evict(2 * i + 2, 0)

                pair(0)
                with act.Fori(1, (MB - 3) // 2) as i:
                    pair(i)
                split(MB - 1, 0, MB // 2)
                evict(MB - 2, 1)
                evict(MB - 1, 0)
                act.wait_ge(sh_done, MB)
                nc.scalar.activation(lora[0:32, 1:1571], sh[0:32, 1:1571], ACT.Tanh).then_inc(lora_done, 1)
                nc.scalar.activation(lora[64:128, 1:1571], sh[64:128, 1:1571], ACT.Tanh, scale=0.5).then_inc(lora_done, 1)

            @block.vector
            def _(dve):
                dve.wait_ge(const_loaded, 32)
                dve.wait_ge(consts_made, 8)
                step = Tally(vec)
                v = step.inc(nc.vector.tensor_scalar(keep[:, :], mu[:, 0, :], -1.0, 1.0, ALU.mult, ALU.add))
                dve.wait_ge(vec, v)
                v = step.inc(nc.vector.tensor_tensor(keep[:, :], keep[:, :], mu[:, 1, :], ALU.subtract))
                dve.wait_ge(vec, v)

                def shift(m, q):
                    dve.wait_ge(raw_done, 5 * (m + 1))
                    n = ST - 2
                    v = step.inc(nc.vector.tensor_scalar(sh[:, 1:1 + n], raw[:, q, 1:1 + n], keep[:, bass.ds(m, 1)], None, ALU.mult))
                    dve.wait_ge(vec, v)
                    v = step.inc(nc.vector.scalar_tensor_tensor(out=sh[:, 1:1 + n], in0=raw[:, q, 0:n], scalar=mu[:, 0, bass.ds(m, 1)],
                                                                in1=sh[:, 1:1 + n], op0=ALU.mult, op1=ALU.add))
                    dve.wait_ge(vec, v)
                    nc.vector.scalar_tensor_tensor(out=sh[:, 1:1 + n], in0=raw[:, q, 2:2 + n], scalar=mu[:, 1, bass.ds(m, 1)],
                                                   in1=sh[:, 1:1 + n], op0=ALU.mult, op1=ALU.add).then_inc(sh_done, 1)

                def turned(m, q, turn):
                    wait(dve, tm_stored[q], 32 * turn)
                    for b in range(3):
                        dve.wait_ge(tp_done, 4 * m + b + 1)
                        nc.vector.tensor_copy(tm[:, q, 4 * b:4 * b + 4, :], tp[:, b, :].rearrange("p (t f) -> p t f", t=4))
                    dve.wait_ge(tp_done, 4 * m + 4)
                    nc.vector.tensor_copy(tm_meta[:, q, :, :], tp[0:N_META, 3, 0:2 * P].rearrange("p (s f) -> p s f", s=2)).then_inc(tm_done, 1)

                shift(0, 0)
                first = step.now()

                def pair(i):
                    step.enter(first + i * 4)
                    turned(2 * i, 0, i)
                    shift(2 * i + 1, 1)
                    turned(2 * i + 1, 1, i)
                    shift(2 * i + 2, 0)
                    assert step.k == 4

                pair(0)
                with dve.Fori(1, (MB - 1) // 2) as i:
                    pair(i)
                step.enter(first + 4 * ((MB - 1) // 2))
                dve.wait_ge(lora_done, 2)
                nc.vector.tensor_copy(lora[32:64, 1:1571], sh[32:64, 1:1571])
                nc.vector.tensor_scalar(lora[64:128, 1:1571], lora[64:128, 1:1571], 0.5, 0.5, ALU.mult, ALU.add).then_inc(gate_half, 1)

            @block.tensor
            def _(pe):
                pe.wait_ge(const_loaded, 32)

                def product(m, q):
                    pe.wait_ge(lo_done, m + 1)
                    pe.wait_ge(hi_done, m + 1)
                    for g in range(3):
                        wait(pe, raw_done, 5 * (m - 1) + (1, 2, 5)[g])
                        parts = [(w, x, k) for k in range(KT) for w, x in ((w_hi, h_hi), (w_lo, h_hi), (w_hi, h_lo))]
                        for j, (w, x, k) in enumerate(parts):
                            last = nc.tensor.matmul(mm[:, g, :], w[:, q, k, :], x[:, k, g * 512:(g + 1) * 512],
                                                    start=(j == 0), stop=(j == len(parts) - 1))
                            if g == 2:
                                last = nc.tensor.matmul(mm[:, 3, 0:N_META], w[:, q, k, :], x[:, k, META_COL:META_COL + N_META],
                                                        start=(j == 0), stop=(j == len(parts) - 1))
                        last.then_inc(group_done, 1)

                def turn(m):
                    pe.wait_ge(sh_done, m + 1)
                    wait(pe, tm_done, m)
                    for b in range(3):
                        for t in range(4 * b, 4 * b + 4):
                            at = 17 + t * P if t < 4 else 547 + (t - 4) * P
                            last = nc.tensor.transpose(tp[:, b, (t % 4) * P:(t % 4 + 1) * P], sh[:, at:at + P], ident[:, :])
                        last.then_inc(tp_done, 1)
                    for s, at in enumerate((1, 531)):
                        last = nc.tensor.transpose(tp[0:N_META, 3, s * P:(s + 1) * P], sh[:, at:at + N_META], ident[:, :])
                    last.then_inc(tp_done, 1)

                def pair(i):
                    product(2 * i + 1, 1)
                    turn(2 * i)
                    product(2 * i + 2, 0)
                    turn(2 * i + 1)

                product(0, 0)
                pair(0)
                with pe.Fori(1, (MB - 1) // 2) as i:
                    pair(i)


def qkv(nc, d, hT):
    h_hi, h_lo = hT
    NQK = 640
    with ExitStack() as ctx:
        sb, ps, sem = alloc(ctx, nc)
        w_in = sb("qk_w", [P, 2, QKV])
        w_hi = sb("qk_w_hi", [P, KT, QKV], F32R)
        w_lo = sb("qk_w_lo", [P, KT, QKV], F32R)
        cos = sb("qk_cos", [P, NT + 1, HEAD])
        sin = sb("qk_sin", [P, NT + 1, HEAD])
        gain = sb("qk_gain", [P, 2, HEAD])
        neg_half = sb("qk_neg_half", [P, 10])
        square = sb("qk_square", [P, NQK])
        ssq = sb("qk_ssq", [P, 2, 10])
        rstd = sb("qk_rstd", [P, 2, 10])
        normed = sb("qk_normed", [P, 2, NQK])
        turned = sb("qk_turned", [P, 2, NQK])
        out = sb("qk_out", [P, 2, QKV])
        mm = ps("qk_mm", [P, 2, 2, 512])
        const_loaded = sem("qk_const")
        half_made = sem("qk_half_made")
        w_loaded = [sem("qk_w0"), sem("qk_w1")]
        hi_done = sem("qk_hi_done")
        lo_done = sem("qk_lo_done")
        product_done = sem("qk_product_done")
        squared = sem("qk_squared")
        ssq_done = sem("qk_ssq_done")
        rstd_done = sem("qk_rstd_done")
        norm_done = sem("qk_norm_done")
        swap_done = sem("qk_swap_done")
        v_done = sem("qk_v_done")
        out_done = sem("qk_out_done")
        stored = [sem("qk_stored0"), sem("qk_stored1")]
        vec = sem("qk_vec")
        last_tile = NT
        with nc.Block() as block:
            @block.sync
            def _(sp):
                for k in range(KT):
                    wait(sp, lo_done, k - 1)
                    sp.dma_start(w_in[:, k % 2, :], d["w_in"][k * P:(k + 1) * P, RWKV_IN:IN_WIDTH]).then_inc(w_loaded[k % 2], 16)
                    if k == 1:
                        sp.dma_start(cos[:, :, :], d["cos"].rearrange("t p c -> p t c")).then_inc(const_loaded, 16)
                        sp.dma_start(sin[:, :, :], d["sin"].rearrange("t p c -> p t c")).then_inc(const_loaded, 16)
                        sp.dma_start(gain[:, 0, :], d["q_gain"].partition_broadcast(P)).then_inc(const_loaded, 16)
                        sp.dma_start(gain[:, 1, :], d["k_gain"].partition_broadcast(P)).then_inc(const_loaded, 16)

                def store(t, q):
                    sp.wait_ge(out_done, t + 1)
                    sp.dma_start(d["qkv"][bass.ds(t * P, P), :], out[:, q, :]).then_inc(stored[q], 16)

                with sp.Fori(0, NT // 2) as i:
                    store(2 * i, 0)
                    store(2 * i + 1, 1)
                store(last_tile, 0)
                sp.wait_ge(stored[0], 16 * (NT // 2 + 1))
                sp.wait_ge(stored[1], 16 * (NT // 2))

            @block.gpsimd
            def _(pool):
                nc.gpsimd.memset(neg_half[:, :], -0.5).then_inc(half_made, 1)
                pool.wait_ge(half_made, 1)
                pool.wait_ge(const_loaded, 64)

                def tile(t, q):
                    pool.wait_ge(ssq_done, t + 1)
                    nc.gpsimd.tensor_tensor(rstd[:, q, :], ssq[:, q, :], neg_half[:, :], ALU.pow).then_inc(rstd_done, 1)
                    pool.wait_ge(norm_done, t + 1)
                    wait(pool, out_done, t - 1)
                    x = normed[:, q, :].rearrange("p (h a s f) -> p h a s f", a=2, s=2, f=16)
                    o = turned[:, q, :].rearrange("p (h a s f) -> p h a s f", a=2, s=2, f=16)
                    tab = sin[:, bass.ds(t, 1), :].rearrange("p o (a s f) -> p o a s f", a=2, s=2)
                    for s in range(2):
                        nc.gpsimd.tensor_tensor(o[:, :, :, s, :], x[:, :, :, 1 - s, :],
                                                tab[:, :, :, s, :].broadcast_to([P, 10, 2, 16]), ALU.mult).then_inc(swap_done, 1)

                tile(0, 0)
                tile(1, 1)
                with pool.Fori(1, NT // 2) as i:
                    tile(2 * i, 0)
                    tile(2 * i + 1, 1)
                tile(last_tile, 0)

            @block.scalar
            def _(act):
                for k in range(KT):
                    act.wait_ge(w_loaded[k % 2], 16 * (k // 2 + 1))
                    nc.scalar.activation(w_hi[:, k, :], w_in[:, k % 2, :], ACT.Copy).then_inc(hi_done, 1)

                def tile(t, q, turn):
                    act.wait_ge(product_done, t + 1)
                    wait(act, ssq_done, t)
                    nc.scalar.activation(square[:, 0:512], mm[:, q, 0, :], ACT.Square)
                    nc.scalar.activation(square[:, 512:NQK], mm[:, q, 1, 0:P], ACT.Square).then_inc(squared, 1)
                    wait(act, stored[q], 16 * turn)
                    nc.scalar.activation(out[:, q, NQK:QKV], mm[:, q, 1, P:2 * P], ACT.Copy).then_inc(v_done, 1)

                tile(0, 0, 0)
                tile(1, 1, 0)
                with act.Fori(1, NT // 2) as i:
                    tile(2 * i, 0, i)
                    tile(2 * i + 1, 1, i)
                tile(last_tile, 0, NT // 2)

            @block.vector
            def _(dve):
                for k in range(KT):
                    dve.wait_ge(hi_done, k + 1)
                    nc.vector.tensor_tensor(w_lo[:, k, :], w_in[:, k % 2, :], w_hi[:, k, :].bitcast(F32), ALU.subtract).then_inc(lo_done, 1)
                dve.wait_ge(const_loaded, 64)
                step = Tally(vec)

                def tile(t, q):
                    heads = lambda ap: ap.rearrange("p (h c) -> p h c", c=HEAD)
                    dve.wait_ge(squared, t + 1)
                    wait(dve, rstd_done, t - 1)
                    v = step.inc(nc.vector.tensor_reduce(ssq[:, q, :], heads(square[:, :]), AX.X, ALU.add))
                    dve.wait_ge(vec, v)
                    nc.vector.tensor_scalar(ssq[:, q, :], ssq[:, q, :], 1.0 / HEAD, QK_EPS, ALU.mult, ALU.add).then_inc(ssq_done, 1)
                    dve.wait_ge(rstd_done, t + 1)
                    wait(dve, swap_done, 2 * (t - 1))
                    dve.wait_ge(v_done, t + 1)
                    r = rstd[:, q, :].unsqueeze(2)
                    nc.vector.tensor_tensor(heads(normed[:, q, 0:512]), heads(mm[:, q, 0, :]), r[:, 0:8, :].broadcast_to([P, 8, HEAD]), ALU.mult)
                    v = step.inc(nc.vector.tensor_tensor(heads(normed[:, q, 512:NQK]), heads(mm[:, q, 1, 0:P]),
                                                         r[:, 8:10, :].broadcast_to([P, 2, HEAD]), ALU.mult))
                    dve.wait_ge(vec, v)
                    nc.vector.tensor_tensor(heads(normed[:, q, 0:512]), heads(normed[:, q, 0:512]),
                                            gain[:, 0:1, :].broadcast_to([P, 8, HEAD]), ALU.mult)
                    nc.vector.tensor_tensor(heads(normed[:, q, 512:NQK]), heads(normed[:, q, 512:NQK]),
                                            gain[:, 1:2, :].broadcast_to([P, 2, HEAD]), ALU.mult).then_inc(norm_done, 1)
                    dve.wait_ge(norm_done, t + 1)
                    c = cos[:, bass.ds(t, 1), :]
                    x = normed[:, q, 0:512].rearrange("p (g j c) -> p g j c", g=2, j=4)
                    y = out[:, q, 0:512].rearrange("p (j g c) -> p g j c", g=2, j=4)
                    s = turned[:, q, 0:512].rearrange("p (g j c) -> p g j c", g=2, j=4)
                    nc.vector.tensor_tensor(y[:, 0], x[:, 0], c.broadcast_to([P, 4, HEAD]), ALU.mult)
                    nc.vector.tensor_tensor(y[:, 1], x[:, 1], c.broadcast_to([P, 4, HEAD]), ALU.mult)
                    v = step.inc(nc.vector.tensor_tensor(heads(out[:, q, 512:NQK]), heads(normed[:, q, 512:NQK]), c.broadcast_to([P, 2, HEAD]), ALU.mult))
                    dve.wait_ge(vec, v)
                    dve.wait_ge(swap_done, 2 * t + 2)
                    nc.vector.tensor_tensor(y, y, s, ALU.add)
                    nc.vector.tensor_tensor(out[:, q, 512:NQK], out[:, q, 512:NQK], turned[:, q, 512:NQK], ALU.add).then_inc(out_done, 1)

                tile(0, 0)
                tile(1, 1)
                with dve.Fori(1, NT // 2) as i:
                    step.enter(i * 6)
                    tile(2 * i, 0)
                    tile(2 * i + 1, 1)
                    assert step.k == 6
                step.enter(6 * (NT // 2))
                tile(last_tile, 0)

            @block.tensor
            def _(pe):
                def tile(t, q, cols):
                    wait(pe, norm_done, t - 1)
                    wait(pe, v_done, t - 1)
                    for c, width in ((0, 512), (1, 256)):
                        parts = [(x, w, k) for k in range(KT) for x, w in ((h_hi, w_hi), (h_hi, w_lo), (h_lo, w_hi))]
                        for j, (x, w, k) in enumerate(parts):
                            last = nc.tensor.matmul(mm[:, q, c, 0:width], x[:, k, cols], w[:, k, c * 512:c * 512 + width],
                                                    start=(j == 0), stop=(j == len(parts) - 1))
                    last.then_inc(product_done, 1)

                pe.wait_ge(lo_done, KT)
                for t in range(NT + 1):
                    tile(t, t % 2, slice(t * P, (t + 1) * P))


def attend(nc, d):
    SCALE = HEAD ** -0.5
    with ExitStack() as ctx:
        sb, ps, sem = alloc(ctx, nc)
        ident = sb("at_ident", [P, P])
        kv = sb("at_kv", [P, NT + 1, 256])
        v_meta = sb("at_v_meta", [P, ATT_H * HEAD])
        kT = sb("at_kT", [P, (NT + 1) * P])
        k_meta = sb("at_k_meta", [P, KV_H * N_META])
        q_in = sb("at_q", [P, 2, 512])
        qT = sb("at_qT", [P, 2, 4, P])
        probs = sb("at_probs", [P, 2, 1024])
        probsT = sb("at_probsT", [P, 2, 1024])
        top = sb("at_top", [P, 2])
        neg_top = sb("at_neg_top", [P, 2, ATT_H])
        total = sb("at_total", [P, 2, ATT_H])
        m_score = sb("at_m_score", [P, ATT_H * N_META])
        m_top = sb("at_m_top", [P, ATT_H])
        m_arg = sb("at_m_arg", [P, ATT_H * N_META])
        m_prob = sb("at_m_prob", [P, ATT_H * N_META])
        m_probT = sb("at_m_probT", [P, P])
        m_sum = sb("at_m_sum", [P, ATT_H])
        inv = sb("at_inv", [P, ATT_H])
        out = sb("at_out", [P, 2, 512])
        S = ps("at_S", [P, 2, 2, 512])
        PT = ps("at_PT", [P, 2, 512])
        M = ps("at_M", [P, 512])
        O = ps("at_O", [P, 512])
        loaded = sem("at_loaded")
        zeroed = sem("at_zeroed")
        k_zeroed = sem("at_k_zeroed")
        vm_loaded = sem("at_vm_loaded")
        kT_done = sem("at_kT_done")
        kT_copied = sem("at_kT_copied")
        q_loaded = [sem("at_q0"), sem("at_q1")]
        qT_done = sem("at_qT_done")
        qT_copied = sem("at_qT_copied")
        ms_done = sem("at_ms_done")
        ms_copied = sem("at_ms_copied")
        s_done = sem("at_s_done")
        top_done = sem("at_top_done")
        exp_done = sem("at_exp_done")
        t_done = sem("at_t_done")
        t_by_vec = sem("at_t_by_vec")
        t_by_act = sem("at_t_by_act")
        pv_done = sem("at_pv_done")
        m_arg_done = sem("at_m_arg_done")
        m_exp_done = sem("at_m_exp_done")
        mT_done = sem("at_mT_done")
        mT_copied = sem("at_mT_copied")
        o_done = sem("at_o_done")
        out_done = sem("at_out_done")
        out_stored = [sem("at_out0"), sem("at_out1")]
        vec = sem("at_vec")
        sp_passed = sem("at_sp_passed")

        def over(eng, pair):
            pair(0, 0, 4)
            pair(1, 0, 4)
            with eng.Fori(2, NT // 2) as i:
                pair(i, 4, 8)

        with nc.Block() as block:
            @block.sync
            def _(sp):
                sp.dma_start(ident[:, :], d["ident"]).then_inc(loaded, 16)
                sp.dma_start(kv[:, :, :], d["qkv"][:, 512:QKV].rearrange("(t p) c -> p t c", p=P)).then_inc(loaded, 16)
                sp.wait_ge(zeroed, 1)
                for h in range(ATT_H):
                    g = h // 4
                    sp.dma_start(v_meta[h * N_META:(h + 1) * N_META, h * HEAD:(h + 1) * HEAD],
                                 d["qkv"][NT * P:NT * P + N_META, 640 + g * HEAD:640 + (g + 1) * HEAD]).then_inc(vm_loaded, 16)

                def load(t, q):
                    hold(sp, qT_done, t - 1, sp_passed)
                    sp.dma_start(q_in[:, q, :], d["qkv"][bass.ds(t * P, P), 0:512]).then_inc(q_loaded[q], 16)

                def store(t, q):
                    hold(sp, out_done, t + 1, sp_passed)
                    sp.dma_start(d["mix"][bass.ds(t * P, P), RW:D], out[:, q, :]).then_inc(out_stored[q], 16)

                load(0, 0)
                load(1, 1)
                with sp.Fori(0, NT // 2 - 1) as i:
                    for q in range(2):
                        load(2 * i + q + 2, q)
                        store(2 * i + q, q)
                store(NT - 2, 0)
                store(NT - 1, 1)
                for q in range(2):
                    sp.wait_ge(out_stored[q], 16 * (NT // 2))

            @block.gpsimd
            def _(pool):
                nc.gpsimd.memset(v_meta[:, :], 0.0).then_inc(zeroed, 1)
                nc.gpsimd.memset(k_meta[:, :], 0.0).then_inc(k_zeroed, 1)

            @block.scalar
            def _(act):
                def pair(i, first, n):
                    half = n // 2 * P
                    for q in range(2):
                        t = 2 * i + q
                        for h in range(ATT_H):
                            u = t * ATT_H + h
                            act.wait_ge(top_done, u + 1)
                            wait(act, t_done, 2 * (u - 1))
                            nc.scalar.activation(probs[:, h % 2, 0:n * P], S[:, h % 2].rearrange("p b c -> p (b c)")[:, 0:n * P], ACT.Exp,
                                                 bias=neg_top[:, q, h:h + 1], scale=SCALE, accum_out=total[:, q, h:h + 1]).then_inc(exp_done, 1)
                            act.wait_ge(t_done, 2 * u + 2)
                            wait(act, pv_done, u - 1)
                            nc.scalar.activation(probsT[:, h % 2, half:2 * half], PT[:, 1, 0:half], ACT.Copy).then_inc(t_by_act, 1)
                        act.wait_ge(m_arg_done, t + 1)
                        wait(act, mT_done, t)
                        nc.scalar.activation(m_prob[:, :], m_arg[:, :], ACT.Exp).then_inc(m_exp_done, 1)

                over(act, pair)

            @block.vector
            def _(dve):
                for b in range(4):
                    n = 4 if b < 3 else 1
                    dve.wait_ge(kT_done, b + 1)
                    nc.vector.tensor_copy(kT[:, b * 512:b * 512 + n * P], S[:, b // 2, b % 2, 0:n * P]).then_inc(kT_copied, 1)
                dve.wait_ge(k_zeroed, 1)
                dve.wait_ge(kT_copied, 4)
                for g in range(KV_H):
                    nc.vector.tensor_copy(k_meta[g * HEAD:(g + 1) * HEAD, g * N_META:(g + 1) * N_META],
                                          kT[g * HEAD:(g + 1) * HEAD, META_COL:META_COL + N_META]).then_inc(kT_copied, 1)
                step = Tally(vec)
                per = 4
                heads = lambda ap, c: ap.rearrange("p (h c) -> p h c", c=c)

                def query(t, q):
                    dve.wait_ge(qT_done, t + 1)
                    nc.vector.tensor_copy(qT[:, q, :, :], M[:, :].rearrange("p (j c) -> p j c", j=4)).then_inc(qT_copied, 1)
                    dve.wait_ge(ms_done, t + 1)
                    v = step.inc(nc.vector.tensor_copy(m_score[:, :].rearrange("p (g j c) -> p g j c", g=2, j=4),
                                                       M[:, 0:P].rearrange("p (j g c) -> p g j c", g=2, j=4)))
                    dve.wait_ge(vec, v)
                    nc.vector.tensor_reduce(m_top[:, :], heads(m_score[:, :], N_META), AX.X, ALU.max).then_inc(ms_copied, 1)
                    dve.wait_ge(ms_copied, t + 1)

                def pair(i, first, n):
                    half = n // 2 * P
                    for q in range(2):
                        t = 2 * i + q
                        step.enter(t * (ATT_H + per))
                        query(t, q)
                        for h in range(ATT_H):
                            u = t * ATT_H + h
                            dve.wait_ge(s_done, u + 1)
                            v = step.inc(nc.vector.tensor_reduce(top[:, h % 2:h % 2 + 1], S[:, h % 2].rearrange("p b c -> p (b c)")[:, 0:n * P], AX.X, ALU.max))
                            dve.wait_ge(vec, v)
                            nc.vector.tensor_scalar(neg_top[:, q, h:h + 1], top[:, h % 2:h % 2 + 1], m_top[:, h:h + 1], -SCALE,
                                                    ALU.max, ALU.mult).then_inc(top_done, 1)
                            if h > 0:
                                turned(u - 1, h - 1, half)
                        turned(t * ATT_H + ATT_H - 1, ATT_H - 1, half)
                        dve.wait_ge(top_done, (t + 1) * ATT_H)
                        nc.vector.scalar_tensor_tensor(out=heads(m_arg[:, :], N_META), in0=heads(m_score[:, :], N_META), scalar=SCALE,
                                                       in1=neg_top[:, q, :].unsqueeze(2).broadcast_to([P, ATT_H, N_META]),
                                                       op0=ALU.mult, op1=ALU.add).then_inc(m_arg_done, 1)
                        dve.wait_ge(m_exp_done, t + 1)
                        v = step.inc(nc.vector.tensor_reduce(m_sum[:, :], heads(m_prob[:, :], N_META), AX.X, ALU.add))
                        dve.wait_ge(vec, v)
                        v = step.inc(nc.vector.tensor_tensor(m_sum[:, :], m_sum[:, :], total[:, q, :], ALU.add))
                        dve.wait_ge(vec, v)
                        v = step.inc(nc.vector.reciprocal(inv[:, :], m_sum[:, :]))
                        dve.wait_ge(mT_done, t + 1)
                        nc.vector.tensor_copy(m_probT[:, :], M[:, 0:P]).then_inc(mT_copied, 1)
                        dve.wait_ge(vec, v)
                        dve.wait_ge(o_done, t + 1)
                        wait(dve, out_stored[q], i * 16)
                        nc.vector.tensor_tensor(heads(out[:, q, :], HEAD), heads(O[:, :], HEAD),
                                                inv[:, :].unsqueeze(2).broadcast_to([P, ATT_H, HEAD]), ALU.mult).then_inc(out_done, 1)
                        assert step.k == ATT_H + per

                def turned(u, h, half):
                    dve.wait_ge(t_done, 2 * u + 1)
                    wait(dve, pv_done, u - 1)
                    nc.vector.tensor_copy(probsT[:, h % 2, 0:half], PT[:, 0, 0:half]).then_inc(t_by_vec, 1)

                over(dve, pair)

            @block.tensor
            def _(pe):
                pe.wait_ge(loaded, 32)
                for t in range(NT + 1):
                    last = nc.tensor.transpose(S[:, t // 8, t // 4 % 2, t % 4 * P:(t % 4 + 1) * P], kv[:, t, 0:P], ident[:, :])
                    if t % 4 == 3 or t == NT:
                        last.then_inc(kT_done, 1)
                pe.wait_ge(vm_loaded, 16 * ATT_H)
                pe.wait_ge(kT_copied, 6)

                def rows(h):
                    g = h // 4
                    return slice(g * HEAD, (g + 1) * HEAD)

                def query(t, q):
                    wait(pe, mT_copied, t)
                    pe.wait_ge(q_loaded[q], 16 * ((t - q) // 2 + 1) if isinstance(t, int) else 16 * turn_of[0] + 16)
                    for j in range(4):
                        last = nc.tensor.transpose(M[:, j * P:(j + 1) * P], q_in[:, q, j * P:(j + 1) * P], ident[:, :])
                    last.then_inc(qT_done, 1)
                    pe.wait_ge(qT_copied, t + 1)
                    for j in range(4):
                        last = nc.tensor.matmul(M[:, j * 32:(j + 1) * 32], qT[:, q, j, :], k_meta[:, :], start=True, stop=True)
                    last.then_inc(ms_done, 1)

                def score(t, q, h, first, n):
                    u = t * ATT_H + h
                    wait(pe, exp_done, u - 1)
                    for b in range(n // 4):
                        c = (first + 4 * b) * P
                        last = nc.tensor.matmul(S[:, h % 2, b, :], qT[rows(h), q, h % 4, :], kT[rows(h), c:c + 512], start=True, stop=True)
                    last.then_inc(s_done, 1)

                def turn(t, h, n):
                    u = t * ATT_H + h
                    pe.wait_ge(exp_done, u + 1)
                    for b in range(2):
                        wait(pe, (t_by_vec, t_by_act)[b], u)
                        for k in range(n // 2):
                            at = (b * (n // 2) + k) * P
                            last = nc.tensor.transpose(PT[:, b, k * P:(k + 1) * P], probs[:, h % 2, at:at + P], ident[:, :])
                        last.then_inc(t_done, 1)

                def value(t, h, first, n):
                    u = t * ATT_H + h
                    pe.wait_ge(t_by_vec, u + 1)
                    pe.wait_ge(t_by_act, u + 1)
                    if h == 0:
                        wait(pe, out_done, t)
                    for k in range(n):
                        g = h // 4
                        last = nc.tensor.matmul(O[:, h * HEAD:(h + 1) * HEAD], probsT[:, h % 2, k * P:(k + 1) * P],
                                                kv[:, first + k, P + g * HEAD:P + (g + 1) * HEAD], start=(h == 0 and k == 0), stop=False,
                                                skip_group_check=True)
                    last.then_inc(pv_done, 1)

                turn_of = [0]

                def pair(i, first, n):
                    turn_of[0] = i
                    for q in range(2):
                        t = 2 * i + q
                        query(t, q)
                        score(t, q, 0, first, n)
                        for h in range(ATT_H):
                            if h + 1 < ATT_H:
                                score(t, q, h + 1, first, n)
                            if h > 0:
                                value(t, h - 1, first, n)
                            turn(t, h, n)
                        value(t, ATT_H - 1, first, n)
                        pe.wait_ge(m_exp_done, t + 1)
                        nc.tensor.transpose(M[:, 0:P], m_prob[:, :], ident[:, :]).then_inc(mT_done, 1)
                        pe.wait_ge(mT_copied, t + 1)
                        nc.tensor.matmul(O[:, :], m_probT[:, :], v_meta[:, :], start=False, stop=True, skip_group_check=True).then_inc(o_done, 1)

                over(pe, pair)


W_LOGIT, A_LOGIT, CUM, CHUNK_SUM, T_K, T_R, T_B, T_D = range(8)
GRAM = 8
D_V = 12
Y_SLOT = (13, 15, 18, 21, 24, 27)
X_SLOT = (None, 16, 19, 22, 25, None)
XT_SLOT = (14, 17, 20, 23, 26, 28)
SLOTS = 29
PER_BANK = [len(range(b, SLOTS, 3)) for b in range(3)]
LEVELS = 6
STEPS = NT
BACK = ("carry0", "solve0", "state0", "carry1", "solve1", "state1", "emit")


def scan_order():
    front = [("F", "lora"), ("F", "decay"), ("F", "turn"), ("B", "lora"), ("F", "gram"), ("B", "decay"), ("F", "dv"), ("B", "turn")]
    f = [("F", x, l) for l in range(LEVELS) for x in ("y", "x")]
    b = [("B", "gram"), ("B", "dv")] + [("B", x, l) for l in range(LEVELS) for x in ("y", "x")]
    for k in range(len(b)):
        if k < len(f):
            front.append(f[k])
        front.append(b[k])
    back = [("back", s, k) for k in range(len(BACK)) for s in "FB"]
    order, at = [], 0
    for k, stage in enumerate(back):
        order.append(stage)
        if k == 0:
            continue
        to = len(front) * k // (len(back) - 1)
        order += front[at:to]
        at = to
    return order


def scan(nc, d):
    S2 = {"F": 0, "B": 1}
    with ExitStack() as ctx:
        sb, ps, sem = alloc(ctx, nc)
        ident = sb("sc_ident", [P, P])
        eye = sb("sc_eye", [P, CHUNK])
        tri = sb("sc_tri", [P, 2, P])
        halves = sb("sc_halves", [P, 2])
        gram_mask = sb("sc_gram_mask", [P, 2, 2, CHUNK])
        level_mask = sb("sc_level_mask", [P, 2, LEVELS, CHUNK])
        keep = sb("sc_keep", [P, 3, STEPS])
        k_k = sb("sc_k_k", [P, RW])
        k_a = sb("sc_k_a", [P, RW])
        r_k = sb("sc_r_k", [P, RW])
        up = sb("sc_up", [33, 2, 2, RW])
        neg_half = sb("sc_neg_half", [P, RH])

        rk = sb("sc_rk", [P, 2, 2 * RW])
        lo = sb("sc_lo", [33, 2, 2, P])
        V = sb("sc_V", [P, 2, 2, RW])
        sgm = sb("sc_sgm", [P, RW])
        av = sb("sc_av", [P, RW])
        kkr = sb("sc_kkr", [P, RW])
        sq = sb("sc_sq", [P, RW])
        ssq = sb("sc_ssq", [P, RH])
        inv = sb("sc_inv", [P, RH])
        cx = sb("sc_cx", [P, RW])
        Wd = sb("sc_W", [P, RW])
        Wi = sb("sc_Wi", [P, RW])
        We = sb("sc_We", [P, RW])
        kd = sb("sc_kd", [P, RW])
        Bt = sb("sc_Bt", [P, 2, 2, RW])
        Ct = sb("sc_Ct", [P, 2, 2, RW])
        bonus = sb("sc_bonus", [P, 2, 2, RH])
        WC = sb("sc_WC", [P, 2, 2, 8])
        KRT = sb("sc_KRT", [P, 2, 2, 4, 2, 2, CHUNK])
        BCT = sb("sc_BCT", [P, 2, 4, 2, 2, CHUNK])
        AT = sb("sc_AT", [P, 2, RH, P])
        ET = sb("sc_ET", [P, 2, 2, RH, P])
        FT = sb("sc_FT", [P, 2, 2, RH, P])
        YD = sb("sc_YD", [P, 2, RH, P])
        XTd = sb("sc_XTd", [P, 2, 2, RH, P])
        Y = sb("sc_Y", [P, 2, RW])
        X = sb("sc_X", [P, 2, RW])
        XT = sb("sc_XT", [P, 2, RW])
        DV = sb("sc_DV", [P, 2, 2, RW])
        H = sb("sc_H", [P, 2, 4, P])
        H_meta = sb("sc_H_meta", [P, 4, P])
        H_add = sb("sc_H_add", [P, 4, P])
        U1 = sb("sc_U1", [P, 2, RW])
        U = sb("sc_U", [P, 2, RW])
        RHt = sb("sc_RH", [P, 2, RW])
        out = sb("sc_out", [P, 2, RW + RH])
        bank = ps("sc_bank", [P, 8, 512])

        const_loaded = sem("sc_const")
        zeroed = sem("sc_zeroed")
        ones_made = sem("sc_ones_made")
        in_loaded = [sem("sc_in0"), sem("sc_in1")]
        v_loaded = [[sem(f"sc_v{s}{p}") for p in range(2)] for s in range(2)]
        meta_loaded = sem("sc_meta_loaded")
        full = [[sem(f"sc_full{s}{b}") for b in range(3)] for s in range(2)]
        free = [[sem(f"sc_free{s}{b}") for b in range(3)] for s in range(2)]
        bd = [sem("sc_bd0"), sem("sc_bd1")]
        x1_done = [sem("sc_x1_0"), sem("sc_x1_1")]
        sg_raw = sem("sc_sg_raw")
        a_raw = sem("sc_a_raw")
        sg_ok = sem("sc_sg_ok")
        a_ok = sem("sc_a_ok")
        kk_raw = sem("sc_kk_raw")
        sq_ok = sem("sc_sq_ok")
        ssq_ok = sem("sc_ssq_ok")
        inv_ok = sem("sc_inv_ok")
        kk_ok = sem("sc_kk_ok")
        cx_ok = sem("sc_cx_ok")
        w_ok = sem("sc_w_ok")
        kd_ok = sem("sc_kd_ok")
        bb_ok = sem("sc_bb_ok")
        tilde = sem("sc_tilde")
        bonus_pre = sem("sc_bonus_pre")
        bonus_ok = sem("sc_bonus_ok")
        bonus_half = sem("sc_bonus_half")
        bfull = [sem("sc_bfull0"), sem("sc_bfull1")]
        bvec = [sem("sc_bvec0"), sem("sc_bvec1")]
        rh_ok = [sem("sc_rh0"), sem("sc_rh1")]
        m_full = sem("sc_m_full")
        m_vec = sem("sc_m_vec")
        out_stored = [sem("sc_out0"), sem("sc_out1")]
        vec = sem("sc_vec")
        sp_passed = sem("sc_sp_passed")
        pe_passed = sem("sc_pe_passed")

        heads = lambda ap, c=HEAD: ap.rearrange("p (h c) -> p h c", c=c)
        half = lambda c: slice(c * CHUNK, (c + 1) * CHUNK)

        class Step:

            def __init__(self, s, g, par, turn=0):
                self.s, self.g, self.par, self.turn = s, g, par, turn
                self.n = g + 1 if s == 0 else g
                self.q = 0 if isinstance(g, int) and g < 0 else 2 * g + 1 + s

            def full(self, slot):
                return self.n * PER_BANK[slot % 3] + slot // 3 + 1

            def taken(self, slot):
                return self.n * PER_BANK[slot % 3] + slot // 3 + 1

            def before(self, slot):
                return self.n * PER_BANK[slot % 3] + slot // 3

            def bank(self, slot):
                return 3 * self.s + slot % 3

        def inputs_in(eng, st):
            if isinstance(st.q, int) and st.q == 0:
                eng.wait_ge(meta_loaded, 16 * 8)
            else:
                eng.wait_ge(in_loaded[st.s], 16 * 3 * (st.g + 1))

        def order(c, s):
            return c if s == 0 else 1 - c

        def window(front, back, g, q, i):
            for stage in scan_order():
                if stage[0] == "back":
                    s = S2[stage[1]]
                    back(Step(s, g, (q + 1) % 2), stage[2])
                else:
                    s = S2[stage[0]]
                    front(Step(s, g + 1, q, i + q + 1), *stage[1:])

        FRONT = ["lora", "decay", "turn", "gram", "dv"]

        def program(eng, front, back, meta, enter=lambda *a: None):
            def whole(st):
                for name in FRONT:
                    front(st, name)
                for l in range(LEVELS):
                    front(st, "y", l)
                    front(st, "x", l)

            enter("meta", 0)
            first = Step(0, -1, 0)
            whole(first)
            meta()
            enter("first", 0)
            for s in range(2):
                whole(Step(s, 0, 1, 1))

            def pair(i):
                for q in range(2):
                    enter("window", 2 * i + q)
                    window(front, back, 2 * i + q, q, i)

            pair(0)
            with eng.Fori(1, STEPS // 2 - 1) as i:
                pair(i)
            enter("window", STEPS - 2)
            window(front, back, STEPS - 2, 0, STEPS // 2 - 1)
            enter("last", STEPS - 1)
            for k in range(len(BACK)):
                for s in range(2):
                    back(Step(s, STEPS - 1, 0), k)

        with nc.Block() as block:
            @block.sync
            def _(sp):
                consts = [(ident[:, :], d["ident"]), (eye[:, :], d["eye"]), (tri[:, :, :], d["tri"]), (halves[:, :], d["halves"]),
                          (gram_mask[:, :, :, :], d["gram_mask"]), (level_mask[:, :, :, :], d["level_mask"]), (keep[:, :, :], d["keep"]),
                          (k_k[:, :], d["k_k"].partition_broadcast(P)), (k_a[:, :], d["k_a"].partition_broadcast(P)),
                          (r_k[:, :], d["r_k"].partition_broadcast(P)), (up[:, :, :, :], d["lora_up"])]
                for to, of in consts:
                    sp.dma_start(to, of).then_inc(const_loaded, 16)
                sp.wait_ge(zeroed, 3)
                for c in range(2):
                    rows = slice(c * CHUNK + CHUNK - N_META, (c + 1) * CHUNK)
                    at = T_REAL + c * N_META
                    sp.dma_start(rk[rows, 0, :], d["rkv"][at:at + N_META, 0:2 * RW]).then_inc(meta_loaded, 16)
                    for x in range(2):
                        sp.dma_start(lo[0:32, 0, x, rows], d["lora"][32 * x:32 * x + 32, at:at + N_META]).then_inc(meta_loaded, 16)
                    sp.dma_start(V[rows, 0, 0, :], d["rkv"][at:at + N_META, 2 * RW:3 * RW]).then_inc(meta_loaded, 16)

                def load(g, par, s):
                    st = Step(s, g, par)
                    t = g if s == 0 else STEPS - 1 - g
                    if not (isinstance(g, int) and g == 0 and s == 1):
                        q = st.q - 2 if not (isinstance(g, int) and g == 0) else 0
                        hold(sp, bonus_pre, q + 1, sp_passed)
                        hold(sp, tilde, 4 * (q + 1), sp_passed)
                    sp.dma_start(rk[:, s, :], d["rkv"][bass.ds(t * P, P), 0:2 * RW]).then_inc(in_loaded[s], 16)
                    for x in range(2):
                        sp.dma_start(lo[0:32, s, x, :], d["lora"][32 * x:32 * x + 32, bass.ds(t * P, P)]).then_inc(in_loaded[s], 16)
                    hold(sp, bfull[s], 7 * (g - 1), sp_passed)
                    sp.dma_start(V[:, s, par, :], d["rkv"][bass.ds(t * P, P), 2 * RW:3 * RW]).then_inc(v_loaded[s][par], 16)

                def store(g, s):
                    t = g if s == 0 else STEPS - 1 - g
                    hold(sp, bvec[s], 7 * (g + 1), sp_passed)
                    sp.dma_start(d["scan"][s, bass.ds(t * P, P), :], out[:, s, :]).then_inc(out_stored[s], 16)

                load(0, 1, 1)
                load(0, 1, 0)
                for s in range(2):
                    load(1, 0, s)
                with sp.Fori(1, STEPS // 2) as i:
                    for q in range(2):
                        for s in range(2):
                            load(2 * i + q, (q + 1) % 2, s)
                        for s in range(2):
                            store(2 * i + q - 2, s)
                for g in (STEPS - 2, STEPS - 1):
                    for s in range(2):
                        store(g, s)
                for s in range(2):
                    sp.wait_ge(out_stored[s], 16 * STEPS)

            @block.gpsimd
            def _(pool):
                for part in (rk[:, 0, :], V[:, 0, 0, :], lo[0:32, 0, :, :]):
                    nc.gpsimd.memset(part, 0.0).then_inc(zeroed, 1)
                pool.wait_ge(zeroed, 3)
                nc.gpsimd.memset(lo[32:33, :, :, :], 1.0).then_inc(ones_made, 1)
                pool.wait_ge(ones_made, 1)
                nc.gpsimd.memset(neg_half[:, :], -0.5)
                for part in (AT[:, :, :, :], YD[:, :, :, :], H[:, :, :, :], H_meta[:, :, :]):
                    nc.gpsimd.memset(part, 0.0)
                for p in range(2):
                    for t in (ET, FT, XTd):
                        nc.gpsimd.memset(t[:, :, p], 0.0)
                nc.gpsimd.memset(out[:, :, RW:RW + RH], 0.0).then_inc(zeroed, 1)
                pool.wait_ge(zeroed, 4)
                pool.wait_ge(const_loaded, 16 * 11)

                def front(st, name, level=None):
                    s, q = st.s, st.q
                    if name == "lora":
                        inputs_in(pool, st)
                        wait(pool, tilde, 4 * q - 3)
                        wait(pool, bb_ok, q)
                        nc.gpsimd.tensor_tensor(kkr[:, :], rk[:, s, RW:2 * RW], k_k[:, :], ALU.mult).then_inc(kk_raw, 1)
                        pool.wait_ge(ssq_ok, q + 1)
                        nc.gpsimd.tensor_tensor(inv[:, :], ssq[:, :], neg_half[:, :], ALU.pow).then_inc(inv_ok, 1)
                        pool.wait_ge(inv_ok, q + 1)
                        pool.wait_ge(sq_ok, q + 1)
                        nc.gpsimd.tensor_tensor(heads(kkr[:, :]), heads(kkr[:, :]), inv[:, :].unsqueeze(2).broadcast_to([P, RH, HEAD]),
                                                ALU.mult).then_inc(kk_ok, 1)
                    if name == "decay":
                        pool.wait_ge(kd_ok, q + 1)
                        pool.wait_ge(kk_ok, q + 1)
                        nc.gpsimd.tensor_tensor(av[:, :], kkr[:, :], av[:, :], ALU.mult).then_inc(bb_ok, 1)
                        nc.gpsimd.tensor_tensor(sq[:, :], rk[:, s, 0:RW], kd[:, :], ALU.mult).then_inc(bonus_half, 1)
                        pool.wait_ge(bonus_half, q + 1)
                        nc.gpsimd.tensor_tensor(sq[:, :], sq[:, :], r_k[:, :], ALU.mult).then_inc(bonus_pre, 1)

                program(pool, front, lambda st, k: None, lambda: None)

            @block.scalar
            def _(act):
                act.wait_ge(const_loaded, 16 * 11)
                act.wait_ge(zeroed, 4)

                def front(st, name, level=None):
                    s, q, par = st.s, st.q, st.par

                    def take(slot, ins=None):
                        act.wait_ge(full[s][slot % 3], st.full(slot))

                    def copy(slot, to, func=ACT.Copy, scale=1.0, cols=slice(0, 512)):
                        take(slot)
                        nc.scalar.activation(to, bank[:, st.bank(slot), cols], func, scale=scale).then_inc(free[s][slot % 3], 1)

                    if name == "lora":
                        wait(act, cx_ok, q)
                        take(W_LOGIT)
                        nc.scalar.activation(sgm[:, :], bank[:, st.bank(W_LOGIT), :], ACT.Tanh, scale=0.5).then_inc(free[s][0], 1)
                        wait(act, tilde, 4 * q)
                        take(A_LOGIT)
                        nc.scalar.activation(av[:, :], bank[:, st.bank(A_LOGIT), :], ACT.Tanh, scale=0.5).then_inc(free[s][1], 1)
                        act.wait_ge(kk_raw, q + 1)
                        wait(act, bonus_ok, q)
                        nc.scalar.activation(sq[:, :], kkr[:, :], ACT.Square).then_inc(sq_ok, 1)
                    if name == "decay":
                        act.wait_ge(cx_ok, q + 1)
                        wait(act, tilde, 4 * q)
                        b = bank[:, st.bank(CUM), :]
                        take(CUM)
                        nc.scalar.activation(Wi[:, :], b, ACT.Exp, scale=DECAY)
                        nc.scalar.activation(Wd[:, :], b, ACT.Exp, scale=-DECAY).then_inc(free[s][2], 1)
                        nc.scalar.activation(We[:, :], cx[:, :], ACT.Exp, scale=-DECAY).then_inc(w_ok, 1)
                        take(CHUNK_SUM)
                        nc.scalar.activation(WC[:, s, par, :], bank[:, st.bank(CHUNK_SUM), 0:8], ACT.Exp, scale=-DECAY).then_inc(free[s][0], 1)
                    if name == "turn":
                        for slot in (T_K, T_R, T_B, T_D):
                            x = (slot - T_K) % 2
                            to = KRT[:, s, par, :, :, x, :] if slot < T_B else BCT[:, s, :, :, x, :]
                            take(slot)
                            nc.scalar.activation(to.rearrange("p j c t -> p (j c) t"), heads(bank[:, st.bank(slot), :]), ACT.Copy).then_inc(free[s][slot % 3], 1)
                    if name == "dv":
                        copy(D_V, DV[:, s, par, :])
                    if name == "y":
                        slot = Y_SLOT[level]
                        act.wait_ge(free[s][slot % 3], st.taken(slot))
                        for c in range(2):
                            last = nc.scalar.activation(YD[half(c), s, :, half(c)], heads(Y[half(c), s, :]), ACT.Copy)
                        last.then_inc(bd[s], 1)
                    if name == "x":
                        slot = XT_SLOT[level]
                        act.wait_ge(free[s][slot % 3], st.taken(slot))
                        for c in range(2):
                            last = nc.scalar.activation(XTd[half(c), s, par, :, half(c)], heads(XT[half(c), s, :]), ACT.Copy)
                        last.then_inc(bd[s], 1)

                def back(st, k):
                    if k not in (0, 3):
                        return
                    s = st.s
                    act.wait_ge(bfull[s], 7 * st.g + k + 1)
                    wait(act, bvec[s], 7 * st.g)
                    c = order(k // 3, s)
                    nc.scalar.activation(RHt[half(c), s, :], bank[64:128, 6 + s, :], ACT.Copy).then_inc(rh_ok[s], 1)

                program(act, front, back, lambda: None)

            @block.vector
            def _(dve):
                dve.wait_ge(const_loaded, 16 * 11)
                dve.wait_ge(zeroed, 4)
                step = Tally(vec)

                def then(ins):
                    dve.wait_ge(vec, step.inc(ins))

                def front(st, name, level=None):
                    s, q, par = st.s, st.q, st.par

                    def take(slot):
                        dve.wait_ge(full[s][slot % 3], st.full(slot))
                        return bank[:, st.bank(slot), :]

                    def freed(slot, ins):
                        ins.then_inc(free[s][slot % 3], 1)

                    if name == "lora":
                        dve.wait_ge(sq_ok, q + 1)
                        wait(dve, inv_ok, q)
                        then(nc.vector.tensor_reduce(ssq[:, :], heads(sq[:, :]), AX.X, ALU.add))
                        nc.vector.tensor_scalar(ssq[:, :], ssq[:, :], 1e-24, None, ALU.max).then_inc(ssq_ok, 1)
                        dve.wait_ge(free[s][0], st.taken(W_LOGIT))
                        nc.vector.tensor_scalar(sgm[:, :], sgm[:, :], 0.5, 0.5, ALU.mult, ALU.add).then_inc(sg_ok, 1)
                        dve.wait_ge(free[s][1], st.taken(A_LOGIT))
                        nc.vector.tensor_scalar(av[:, :], av[:, :], 0.5, 0.5, ALU.mult, ALU.add).then_inc(a_ok, 1)
                        dve.wait_ge(a_ok, q + 1)
                        wait(dve, bonus_pre, q)
                        inputs_in(dve, st)
                        then(nc.vector.scalar_tensor_tensor(out=kd[:, :], in0=av[:, :], scalar=1.0, in1=k_a[:, :], op0=ALU.subtract, op1=ALU.mult))
                        nc.vector.scalar_tensor_tensor(out=kd[:, :], in0=kd[:, :], scalar=1.0, in1=rk[:, s, RW:2 * RW],
                                                       op0=ALU.add, op1=ALU.mult).then_inc(kd_ok, 1)
                    if name == "decay":
                        b = take(CUM)
                        wait(dve, w_ok, q)
                        dve.wait_ge(sg_ok, q + 1)
                        nc.vector.tensor_tensor(cx[:, :], b, sgm[:, :], ALU.subtract).then_inc(cx_ok, 1)
                        dve.wait_ge(w_ok, q + 1)
                        dve.wait_ge(kk_ok, q + 1)
                        nc.vector.scalar_tensor_tensor(out=We[:, :], in0=kkr[:, :], scalar=-1.0, in1=We[:, :],
                                                       op0=ALU.mult, op1=ALU.mult).then_inc(tilde, 1)
                        nc.vector.tensor_tensor(Wd[:, :], rk[:, s, 0:RW], Wd[:, :], ALU.mult).then_inc(tilde, 1)
                        dve.wait_ge(bb_ok, q + 1)
                        nc.vector.tensor_tensor(Bt[:, s, par, :], av[:, :], Wi[:, :], ALU.mult).then_inc(tilde, 1)
                        dve.wait_ge(kd_ok, q + 1)
                        nc.vector.tensor_tensor(Ct[:, s, par, :], kd[:, :], Wi[:, :], ALU.mult).then_inc(tilde, 1)
                    if name == "turn":
                        dve.wait_ge(bonus_pre, q + 1)
                        nc.vector.tensor_reduce(bonus[:, s, par, :], heads(sq[:, :]), AX.X, ALU.add).then_inc(bonus_ok, 1)
                    if name == "gram":
                        for x in range(4):
                            c, e = x // 2, x % 2
                            b = take(GRAM + x)
                            for r, (to_a, to_e) in enumerate(((AT[:, s], ET[:, s, par]), (YD[:, s], FT[:, s, par]))):
                                part = b[half(r), :].rearrange("p (j x t) -> p j x t", j=4, x=2)
                                for y, to in enumerate((to_a, to_e)):
                                    last = nc.vector.tensor_tensor(
                                        to[half(c), :, half(c)].rearrange("p (j e) t -> p j e t", e=2)[:, :, e, :], part[:, :, y, :],
                                        gram_mask[half(r), s, y:y + 1, :].broadcast_to([CHUNK, 4, CHUNK]), ALU.mult)
                            freed(GRAM + x, last)
                    if name == "y":
                        slot = Y_SLOT[level]
                        b = take(slot)
                        freed(slot, nc.vector.tensor_tensor(heads(Y[:, s, :]), heads(b),
                                                            level_mask[:, s, level:level + 1, :].broadcast_to([P, RH, CHUNK]), ALU.mult))
                        if level == 0:
                            dve.wait_ge(free[s][slot % 3], st.taken(slot))
                            nc.vector.tensor_tensor(heads(X[:, s, :]), heads(Y[:, s, :]),
                                                    eye[:, :].unsqueeze(1).broadcast_to([P, RH, CHUNK]), ALU.add).then_inc(x1_done[s], 1)
                    if name == "x":
                        if X_SLOT[level]:
                            slot = X_SLOT[level]
                            b = take(slot)
                            freed(slot, nc.vector.tensor_tensor(X[:, s, :], b, X[:, s, :], ALU.add))
                        slot = XT_SLOT[level]
                        b = take(slot)
                        if level == 0:
                            freed(slot, nc.vector.tensor_tensor(heads(XT[:, s, :]), heads(b),
                                                                eye[:, :].unsqueeze(1).broadcast_to([P, RH, CHUNK]), ALU.add))
                        else:
                            freed(slot, nc.vector.tensor_tensor(XT[:, s, :], b, XT[:, s, :], ALU.add))

                def back(st, k):
                    s, g, par = st.s, st.g, st.par
                    b = bank[:, 6 + s, :]
                    base = 7 * g
                    c = order(k // 3, s)
                    dve.wait_ge(bfull[s], base + k + 1)
                    if k in (0, 3):
                        dve.wait_ge(free[s][D_V % 3], st.taken(D_V))
                        nc.vector.tensor_tensor(U1[half(c), s, :], b[0:CHUNK, :], DV[half(c), s, par, :], ALU.add).then_inc(bvec[s], 1)
                    elif k in (1, 4):
                        nc.vector.tensor_copy(U[half(c), s, :], b[half(c), :]).then_inc(bvec[s], 1)
                    elif k in (2, 5):
                        for e in range(2):
                            h = H[half(e), s, :, half(e)]
                            last = nc.vector.tensor_tensor(h, b[half(e), :].rearrange("p (j c) -> p j c", j=4)[:, :, half(e)], h, ALU.add)
                        then(last)
                        for e in range(2):
                            h = H[half(e), s, :, half(e)]
                            w = WC[half(e), s, par, :].rearrange("p (j c) -> p j c", c=2)[:, :, c:c + 1].broadcast_to([CHUNK, 4, CHUNK])
                            last = nc.vector.tensor_tensor(h, h, w, ALU.mult)
                        if k == 2:
                            last.then_inc(bvec[s], 1)
                        else:
                            then(last)
                            if s == 0:
                                then(nc.vector.tensor_scalar(H_add[:, :, :], H_meta[:, :, :], keep[:, 2, bass.ds(g, 1)], None, ALU.mult))
                                nc.vector.scalar_tensor_tensor(out=H[:, s].rearrange("p j c -> p (j c)"), in0=H[:, s].rearrange("p j c -> p (j c)"),
                                                               scalar=keep[:, 0, bass.ds(g, 1)], in1=H_add[:, :, :].rearrange("p j c -> p (j c)"),
                                                               op0=ALU.mult, op1=ALU.add).then_inc(bvec[s], 1)
                            else:
                                nc.vector.tensor_scalar(H[:, s], H[:, s], keep[:, 1, bass.ds(g, 1)], None, ALU.mult).then_inc(bvec[s], 1)
                    else:
                        dve.wait_ge(rh_ok[s], 2 * g + 2)
                        wait(dve, out_stored[s], 16 * g)
                        nc.vector.tensor_copy(out[:, s, RW:RW + RH], bonus[:, s, par, :])
                        nc.vector.tensor_tensor(out[:, s, 0:RW], b, RHt[:, s, :], ALU.add).then_inc(bvec[s], 1)

                def meta():
                    b = bank[:, 6, :]
                    dve.wait_ge(m_full, 1)
                    nc.vector.tensor_copy(U[half(0), 0, :], b[half(0), :]).then_inc(m_vec, 1)
                    dve.wait_ge(m_full, 2)
                    nc.vector.tensor_copy(U[half(1), 0, :], bank[half(1), 7, :]).then_inc(m_vec, 1)
                    for c, to in enumerate((H[:, 0], H_meta)):
                        dve.wait_ge(m_full, 3 + c)
                        for e in range(2):
                            w = WC[half(e), 0, 0, :].rearrange("p (j c) -> p j c", c=2)[:, :, c:c + 1].broadcast_to([CHUNK, 4, CHUNK])
                            last = nc.vector.tensor_tensor(to[half(e), :, half(e)], bank[half(e), 6 + c, :].rearrange("p (j c) -> p j c", j=4)[:, :, half(e)],
                                                           w, ALU.mult)
                        last.then_inc(m_vec, 1)

                PER_FRONT = 2
                PER_WINDOW = 2 * PER_FRONT + 2 * 1 + 2 * 2 + 1

                def enter(what, g):
                    start = 3 * PER_FRONT
                    if what in ("window", "last"):
                        step.enter(start + g * PER_WINDOW)

                program(dve, front, back, meta, enter)

            @block.tensor
            def _(pe):
                pe.wait_ge(const_loaded, 16 * 11)
                pe.wait_ge(zeroed, 4)

                def front(st, name, level=None):
                    s, q, par = st.s, st.q, st.par

                    def claim(slot):
                        wait(pe, free[s][slot % 3], st.before(slot))
                        return bank[:, st.bank(slot), :]

                    def fill(slot, ins):
                        ins.then_inc(full[s][slot % 3], 1)

                    def need(slot):
                        pe.wait_ge(free[s][slot % 3], st.taken(slot))

                    if name == "lora":
                        inputs_in(pe, st)
                        for x, slot in enumerate((W_LOGIT, A_LOGIT)):
                            b = claim(slot)
                            fill(slot, nc.tensor.matmul(b, lo[0:33, s, x, :], up[0:33, s, x, :], start=True, stop=True))
                    if name == "decay":
                        pe.wait_ge(sg_ok, q + 1)
                        b = claim(CUM)
                        fill(CUM, nc.tensor.matmul(b, tri[:, s, :], sgm[:, :], start=True, stop=True))
                        b = claim(CHUNK_SUM)
                        for j in range(4):
                            last = nc.tensor.matmul(b[:, 2 * j:2 * j + 2], sgm[:, j * P:(j + 1) * P], halves[:, :], start=True, stop=True)
                        fill(CHUNK_SUM, last)
                    if name == "turn":
                        for n, (slot, x) in enumerate(((T_K, We[:, :]), (T_R, Wd[:, :]), (T_B, Bt[:, s, par, :]), (T_D, Ct[:, s, par, :]))):
                            pe.wait_ge(tilde, 4 * q + n + 1)
                            b = claim(slot)
                            for j in range(4):
                                last = nc.tensor.transpose(b[:, j * P:(j + 1) * P], x[:, j * P:(j + 1) * P], ident[:, :])
                            fill(slot, last)
                    if name == "gram":
                        need(T_D)
                        need(T_B)
                        need(T_R)
                        for x in range(4):
                            c, e = x // 2, x % 2
                            b = claim(GRAM + x)
                            for j in range(4):
                                last = nc.tensor.matmul(b[:, j * P:(j + 1) * P], BCT[half(e), s, j, c].rearrange("p x t -> p (x t)"),
                                                        KRT[half(e), s, par, j, c].rearrange("p x t -> p (x t)"), start=True, stop=True)
                            fill(GRAM + x, last)
                    if name == "dv":
                        need(GRAM + 3)
                        if not (isinstance(st.q, int) and st.q == 0):
                            pe.wait_ge(v_loaded[s][par], 16 * st.turn)
                        b = claim(D_V)
                        for h in range(RH):
                            last = nc.tensor.matmul(b[:, half(h)], YD[:, s, h, :], V[:, s, par, half(h)], start=True, stop=True)
                        fill(D_V, last)

                    def product(slot, lhsT, rhs):
                        b = claim(slot)
                        for h in range(RH):
                            last = nc.tensor.matmul(b[:, half(h)], lhsT[:, h, :], rhs(h), start=True, stop=True)
                        fill(slot, last)

                    n = 2 * LEVELS * st.n
                    if name == "y":
                        if level == 0:
                            product(Y_SLOT[0], AT[:, s], lambda h: eye[:, :])
                        else:
                            if level == 1:
                                pe.wait_ge(x1_done[s], st.n + 1)
                            else:
                                need(X_SLOT[level - 1])
                            product(Y_SLOT[level], AT[:, s], lambda h: X[:, s, half(h)])
                    if name == "x":
                        need(Y_SLOT[level])
                        if X_SLOT[level]:
                            pe.wait_ge(bd[s], n + 2 * level)
                            product(X_SLOT[level], XTd[:, s, par], lambda h: Y[:, s, half(h)])
                        pe.wait_ge(bd[s], n + 2 * level + 1)
                        if level:
                            need(XT_SLOT[level - 1])
                        product(XT_SLOT[level], YD[:, s], (lambda h: XT[:, s, half(h)]) if level else (lambda h: eye[:, :]))

                def back(st, k):
                    s, g, par = st.s, st.g, st.par
                    b = bank[:, 6 + s, :]
                    base = 7 * g
                    c = order(k // 3, s)
                    wait(pe, bvec[s], base + k)
                    if k in (0, 3):
                        for j in range(4):
                            last = nc.tensor.matmul(b[:, j * P:(j + 1) * P], KRT[:, s, par, j, c].rearrange("p x t -> p (x t)"), H[:, s, j, :],
                                                    start=True, stop=True)
                    elif k in (1, 4):
                        pe.wait_ge(rh_ok[s], 2 * g + k // 3 + 1)
                        hold(pe, bd[s], 2 * LEVELS * (st.n + 1), pe_passed)
                        for h in range(RH):
                            last = nc.tensor.matmul(b[half(c), half(h)], XTd[half(c), s, par, h, half(c)], U1[half(c), s, half(h)], start=True, stop=True)
                    elif k in (2, 5):
                        for j in range(4):
                            cols = slice(j * P, (j + 1) * P)
                            nc.tensor.matmul(b[:, cols], Bt[half(c), s, par, cols], U[half(c), s, cols], start=True, stop=False)
                            last = nc.tensor.matmul(b[:, cols], Ct[half(c), s, par, cols], V[half(c), s, par, cols], start=False, stop=True)
                    else:
                        for h in range(RH):
                            nc.tensor.matmul(b[:, half(h)], ET[:, s, par, h, :], U[:, s, half(h)], start=True, stop=False)
                            last = nc.tensor.matmul(b[:, half(h)], FT[:, s, par, h, :], V[:, s, par, half(h)], start=False, stop=True)
                    last.then_inc(bfull[s], 1)

                def meta():
                    pe.wait_ge(bd[0], 2 * LEVELS)
                    pe.wait_ge(free[0][D_V % 3], Step(0, -1, 0).taken(D_V))
                    for c in range(2):
                        for h in range(RH):
                            last = nc.tensor.matmul(bank[half(c), 6 + c, half(h)], XTd[half(c), 0, 0, h, half(c)], DV[half(c), 0, 0, half(h)],
                                                    start=True, stop=True)
                        last.then_inc(m_full, 1)
                    for c in range(2):
                        pe.wait_ge(m_vec, 2)
                        for j in range(4):
                            cols = slice(j * P, (j + 1) * P)
                            nc.tensor.matmul(bank[:, 6 + c, cols], Bt[half(c), 0, 0, cols], U[half(c), 0, cols], start=True, stop=False)
                            last = nc.tensor.matmul(bank[:, 6 + c, cols], Ct[half(c), 0, 0, cols], V[half(c), 0, 0, cols], start=False, stop=True)
                        last.then_inc(m_full, 1)
                    pe.wait_ge(m_vec, 4)

                program(pe, front, back, meta)


def mixout(nc, d):
    with ExitStack() as ctx:
        sb, ps, sem = alloc(ctx, nc)
        ident = sb("mo_ident", [P, P])
        gn_g = sb("mo_gn_g", [P, RW])
        gn_b = sb("mo_gn_b", [P, RW])
        gain = sb("mo_gain", [P, D])
        bias = sb("mo_bias", [P, D])
        gate_up = sb("mo_gate_up", [P, RW])
        neg_half = sb("mo_neg_half", [P, RH])
        w_in = sb("mo_w", [P, 2, D])
        w_hi = sb("mo_w_hi", [P, KT, D], F32R)
        w_lo = sb("mo_w_lo", [P, KT, D], F32R)
        sc = sb("mo_sc", [P, 2, 2, RW + RH])
        v = sb("mo_v", [P, 2, RW])
        gate = sb("mo_gate", [P, 2, P])
        mix = sb("mo_mix", [P, 2, D])
        h = sb("mo_h", [P, 2, D])
        o = sb("mo_o", [P, RW + RH])
        square = sb("mo_square", [P, RW])
        vb = sb("mo_vb", [P, RW])
        mean = sb("mo_mean", [P, RH])
        var = sb("mo_var", [P, RH])
        rstd = sb("mo_rstd", [P, RH])
        m_hi = sb("mo_m_hi", [P, 2, KT, P], F32R)
        m_lo = sb("mo_m_lo", [P, 2, KT, P], F32R)
        x = sb("mo_x", [P, 2, D])
        stats = sb("mo_stats", [P, 12])
        mv = sb("mo_mv", [P, 2])
        l_rstd = sb("mo_l_rstd", [P, 1])
        nmr = sb("mo_nmr", [P, 1])
        G = ps("mo_G", [P, 512])
        tp = ps("mo_tp", [P, 2, 512])
        mm = ps("mo_mm", [P, 2, 2, 512])
        const_loaded = sem("mo_const")
        half_made = sem("mo_half_made")
        w_loaded = [sem("mo_w0"), sem("mo_w1")]
        w_hi_done = sem("mo_w_hi_done")
        w_lo_done = sem("mo_w_lo_done")
        in_loaded = [sem("mo_in0"), sem("mo_in1")]
        h_loaded = [sem("mo_h0"), sem("mo_h1")]
        centred = sem("mo_centred")
        squared = sem("mo_squared")
        var_done = sem("mo_var_done")
        rstd_done = sem("mo_rstd_done")
        scaled = sem("mo_scaled")
        pool_step = sem("mo_pool_step")
        o_done = sem("mo_o_done")
        gate_done = sem("mo_gate_done")
        mix_done = sem("mo_mix_done")
        tp_done = sem("mo_tp_done")
        hi_done = sem("mo_hi_done")
        lo_done = sem("mo_lo_done")
        product_done = sem("mo_product_done")
        res_done = sem("mo_res_done")
        l_var_done = sem("mo_l_var_done")
        l_rstd_done = sem("mo_l_rstd_done")
        nmr_done = sem("mo_nmr_done")
        normed = sem("mo_normed")
        gained = sem("mo_gained")
        x_done = sem("mo_x_done")
        x_stored = [sem("mo_x0"), sem("mo_x1")]
        vec = sem("mo_vec")
        passed = sem("mo_passed")
        sp_passed = sem("mo_sp_passed")
        heads = lambda ap: ap.rearrange("p (h c) -> p h c", c=HEAD)
        spread = lambda ap: ap.unsqueeze(2).broadcast_to([P, RH, HEAD])

        def program(eng, combine, turn, finish, enter=lambda g: None):
            enter(-2)
            combine(0, 0, 0)
            enter(-1)
            turn(0, 0, 0)
            combine(1, 1, 0)

            def tile(t, q, i):
                enter(t)
                turn(t + 1, 1 - q, i + q)
                combine(t + 2, q, i + 1)
                finish(t, q, i)

            def pair(i):
                tile(2 * i, 0, i)
                tile(2 * i + 1, 1, i)

            pair(0)
            with eng.Fori(1, NT // 2 - 1) as i:
                pair(i)
            n = NT // 2 - 1
            enter(NT - 2)
            turn(NT - 1, 1, n)
            finish(NT - 2, 0, n)
            enter(NT - 1)
            finish(NT - 1, 1, n)

        with nc.Block() as block:
            @block.sync
            def _(sp):
                for to, of in ((ident[:, :], d["ident"]), (gn_g[:, :], d["gn_g"].partition_broadcast(P)), (gn_b[:, :], d["gn_b"].partition_broadcast(P)),
                               (gain[:, :], d["ln1_g"].partition_broadcast(P)), (bias[:, :], d["ln1_b"].partition_broadcast(P)),
                               (gate_up[64:128, :], d["gate_up"])):
                    sp.dma_start(to, of).then_inc(const_loaded, 16)

                def load(t, q):
                    rows = bass.ds(t * P, P)
                    hold(sp, tp_done, 2 * (t - 1), sp_passed)
                    for z in range(2):
                        sp.dma_start(sc[:, q, z, :], d["scan"][z, rows, :]).then_inc(in_loaded[q], 16)
                    sp.dma_start(v[:, q, :], d["rkv"][rows, 2 * RW:3 * RW]).then_inc(in_loaded[q], 16)
                    sp.dma_start(gate[64:128, q, :], d["lora"][64:128, bass.ds(t * P, P)]).then_inc(in_loaded[q], 16)
                    sp.dma_start(mix[:, q, RW:D], d["mix"][rows, RW:D]).then_inc(in_loaded[q], 16)
                    hold(sp, res_done, 2 * (t - 1), sp_passed)
                    sp.dma_start(h[:, q, :], d["h"][rows, :]).then_inc(h_loaded[q], 16)

                def store(t, q):
                    hold(sp, x_done, t + 1, sp_passed)
                    sp.dma_start(d["x1"][bass.ds(t * P, P), :], x[:, q, :]).then_inc(x_stored[q], 16)

                load(0, 0)
                load(1, 1)
                for k in range(KT):
                    wait(sp, w_lo_done, k - 1)
                    sp.dma_start(w_in[:, k % 2, :], d["w_out"][k * P:(k + 1) * P, :]).then_inc(w_loaded[k % 2], 16)
                with sp.Fori(1, NT // 2) as i:
                    for q in range(2):
                        load(2 * i + q, q)
                        store(2 * i + q - 2, q)
                store(NT - 2, 0)
                store(NT - 1, 1)
                for q in range(2):
                    sp.wait_ge(x_stored[q], 16 * (NT // 2))

            @block.gpsimd
            def _(pool):
                nc.gpsimd.memset(neg_half[:, :], -0.5).then_inc(half_made, 1)
                pool.wait_ge(half_made, 1)
                pool.wait_ge(const_loaded, 16 * 6)
                for k in range(KT):
                    pool.wait_ge(w_hi_done, k + 1)
                    nc.gpsimd.tensor_tensor(w_lo[:, k, :], w_in[:, k % 2, :], w_hi[:, k, :].bitcast(F32), ALU.subtract).then_inc(w_lo_done, 1)

                def combine(t, q, i):
                    pool.wait_ge(in_loaded[q], 80 * (i + 1))
                    pool.wait_ge(centred, t + 1)
                    nc.gpsimd.tensor_tensor(heads(vb[:, :]), heads(v[:, q, :]), spread(o[:, RW:RW + RH]), ALU.mult).then_inc(pool_step, 1)
                    pool.wait_ge(var_done, t + 1)
                    nc.gpsimd.tensor_tensor(rstd[:, :], var[:, :], neg_half[:, :], ALU.pow).then_inc(rstd_done, 1)
                    pool.wait_ge(pool_step, 4 * t + 1)
                    nc.gpsimd.tensor_tensor(vb[:, :], vb[:, :], gn_b[:, :], ALU.add).then_inc(pool_step, 1)
                    pool.wait_ge(scaled, t + 1)
                    nc.gpsimd.tensor_tensor(o[:, 0:RW], o[:, 0:RW], gn_g[:, :], ALU.mult).then_inc(pool_step, 1)
                    pool.wait_ge(pool_step, 4 * t + 3)
                    nc.gpsimd.tensor_tensor(o[:, 0:RW], o[:, 0:RW], vb[:, :], ALU.add).then_inc(pool_step, 1)

                def finish(t, q, i):
                    pool.wait_ge(l_var_done, t + 1)
                    nc.gpsimd.tensor_tensor(l_rstd[:, :], mv[:, 1:2], neg_half[:, 0:1], ALU.pow).then_inc(l_rstd_done, 1)
                    pool.wait_ge(gained, t + 1)
                    nc.gpsimd.tensor_tensor(x[:, q, :], x[:, q, :], bias[:, :], ALU.add).then_inc(x_done, 1)

                program(pool, combine, lambda t, q, i: None, finish)

            @block.scalar
            def _(act):
                for k in range(KT):
                    act.wait_ge(w_loaded[k % 2], 16 * (k // 2 + 1))
                    nc.scalar.activation(w_hi[:, k, :], w_in[:, k % 2, :], ACT.Copy).then_inc(w_hi_done, 1)

                def combine(t, q, i):
                    act.wait_ge(centred, t + 1)
                    nc.scalar.activation(square[:, :], o[:, 0:RW], ACT.Square).then_inc(squared, 1)

                def turn(t, q, i):
                    for b in range(2):
                        act.wait_ge(tp_done, 2 * t + b + 1)
                        wait(act, product_done, t - 1)
                        nc.scalar.activation(m_hi[:, q, 4 * b:4 * b + 4, :], tp[:, b, :].rearrange("p (k c) -> p k c", k=4), ACT.Copy).then_inc(hi_done, 1)

                def finish(t, q, i):
                    act.wait_ge(nmr_done, t + 1)
                    nc.scalar.activation(x[:, q, :], x[:, q, :], ACT.Identity, bias=nmr[:, :], scale=l_rstd[:, :]).then_inc(normed, 1)

                program(act, combine, turn, finish)

            @block.vector
            def _(dve):
                dve.wait_ge(const_loaded, 16 * 6)
                step = Tally(vec)

                def then(ins):
                    dve.wait_ge(vec, step.inc(ins))

                def combine(t, q, i):
                    dve.wait_ge(in_loaded[q], 80 * (i + 1))
                    wait(dve, mix_done, t)
                    then(nc.vector.tensor_tensor(o[:, :], sc[:, q, 0, :], sc[:, q, 1, :], ALU.add))
                    then(nc.vector.tensor_reduce(mean[:, :], heads(o[:, 0:RW]), AX.X, ALU.add))
                    nc.vector.scalar_tensor_tensor(out=heads(o[:, 0:RW]), in0=spread(mean[:, :]), scalar=-1.0 / HEAD, in1=heads(o[:, 0:RW]),
                                                   op0=ALU.mult, op1=ALU.add).then_inc(centred, 1)
                    dve.wait_ge(squared, t + 1)
                    then(nc.vector.tensor_reduce(var[:, :], heads(square[:, :]), AX.X, ALU.add))
                    nc.vector.tensor_scalar(var[:, :], var[:, :], 1.0 / HEAD, GN_EPS, ALU.mult, ALU.add).then_inc(var_done, 1)
                    dve.wait_ge(rstd_done, t + 1)
                    nc.vector.tensor_tensor(heads(o[:, 0:RW]), heads(o[:, 0:RW]), spread(rstd[:, :]), ALU.mult).then_inc(scaled, 1)
                    dve.wait_ge(pool_step, 4 * (t + 1))
                    dve.wait_ge(gate_done, t + 1)
                    wait(dve, tp_done, 2 * (t - 1))
                    nc.vector.tensor_tensor(mix[:, q, 0:RW], G[:, :], o[:, 0:RW], ALU.mult).then_inc(mix_done, 1)

                def turn(t, q, i):
                    for b in range(2):
                        dve.wait_ge(hi_done, 2 * t + b + 1)
                        nc.vector.tensor_tensor(m_lo[:, q, 4 * b:4 * b + 4, :], tp[:, b, :].rearrange("p (k c) -> p k c", k=4),
                                                m_hi[:, q, 4 * b:4 * b + 4, :].bitcast(F32), ALU.subtract).then_inc(lo_done, 1)

                def finish(t, q, i):
                    dve.wait_ge(product_done, t + 1)
                    dve.wait_ge(h_loaded[q], 16 * (i + 1))
                    wait(dve, x_stored[q], 16 * i)
                    for b in range(2):
                        cols = slice(b * 512, (b + 1) * 512)
                        nc.vector.scalar_tensor_tensor(out=x[:, q, cols], in0=h[:, q, cols], scalar=ALPHA, in1=mm[:, q, b, :],
                                                       op0=ALU.mult, op1=ALU.add).then_inc(res_done, 1)
                    for b in range(2):
                        cols = slice(b * 512, (b + 1) * 512)
                        dve.wait_ge(res_done, 2 * t + b + 1)
                        last = nc.vector.bn_stats(stats[:, 6 * b:6 * b + 6], x[:, q, cols])
                    step.inc(last)
                    wait(dve, l_rstd_done, t)
                    hold(dve, vec, step.now(), passed)
                    then(nc.vector.bn_aggr(mv[:, :], stats[:, :]))
                    nc.vector.tensor_scalar(mv[:, 1:2], mv[:, 1:2], LN_EPS, None, ALU.add).then_inc(l_var_done, 1)
                    dve.wait_ge(l_rstd_done, t + 1)
                    nc.vector.scalar_tensor_tensor(out=nmr[:, :], in0=mv[:, 0:1], scalar=-1.0, in1=l_rstd[:, :],
                                                   op0=ALU.mult, op1=ALU.mult).then_inc(nmr_done, 1)
                    dve.wait_ge(normed, t + 1)
                    nc.vector.tensor_tensor(x[:, q, :], x[:, q, :], gain[:, :], ALU.mult).then_inc(gained, 1)

                COMBINE, FINISH = 3, 2

                def enter(t):
                    if isinstance(t, int) and t < 0:
                        step.enter((t + 2) * COMBINE)
                    elif isinstance(t, int) and t >= NT - 2:
                        step.enter(NT * COMBINE + t * FINISH)
                    else:
                        step.enter(2 * COMBINE + t * (COMBINE + FINISH))

                program(dve, combine, turn, finish, enter)

            @block.tensor
            def _(pe):
                pe.wait_ge(const_loaded, 16 * 6)

                def combine(t, q, i):
                    pe.wait_ge(in_loaded[q], 80 * (i + 1))
                    wait(pe, mix_done, t)
                    nc.tensor.matmul(G[:, :], gate[64:128, q, :], gate_up[64:128, :], start=True, stop=True).then_inc(gate_done, 1)

                def turn(t, q, i):
                    pe.wait_ge(mix_done, t + 1)
                    wait(pe, lo_done, 2 * t)
                    for b in range(2):
                        for k in range(4):
                            last = nc.tensor.transpose(tp[:, b, k * P:(k + 1) * P], mix[:, q, (4 * b + k) * P:(4 * b + k + 1) * P], ident[:, :])
                        last.then_inc(tp_done, 1)

                def finish(t, q, i):
                    if isinstance(t, int) and t == 0:
                        pe.wait_ge(w_lo_done, KT)
                    pe.wait_ge(lo_done, 2 * t + 2)
                    wait(pe, res_done, 2 * (t - 1))
                    for b in range(2):
                        parts = [(m, w, k) for k in range(KT) for m, w in ((m_hi, w_hi), (m_hi, w_lo), (m_lo, w_hi))]
                        for j, (m, w, k) in enumerate(parts):
                            last = nc.tensor.matmul(mm[:, q, b, :], m[:, q, k, :], w[:, k, b * 512:(b + 1) * 512],
                                                    start=(j == 0), stop=(j == len(parts) - 1))
                    last.then_inc(product_done, 1)

                program(pe, combine, turn, finish)


def ffn(nc, d):
    for part in range(2):
        ffn_part(nc, d, part)


def ffn_part(nc, d, part):
    TILES = NT // 2
    TOK = TILES * P
    GRP = TOK // 2
    FB = D_FF // P
    NAME = f"ff{part}_"
    with ExitStack() as ctx:
        sb, ps, sem = alloc(ctx, nc)
        ident = sb(NAME + "ident", [P, P])
        gain = sb(NAME + "gain", [P, D])
        bias = sb(NAME + "bias", [P, D])
        neg_half = sb(NAME + "neg_half", [P, 1])
        x = sb(NAME + "x", [P, 2, D])
        x_hi = sb(NAME + "x_hi", [P, KT, TOK], F32R)
        x_lo = sb(NAME + "x_lo", [P, KT, TOK], F32R)
        y = sb(NAME + "y", [P, TILES, D])
        w = sb(NAME + "w", [P, 2, 3, D])
        w_hi = sb(NAME + "w_hi", [P, 2, 3, D], F32R)
        w_lo = sb(NAME + "w_lo", [P, 2, 3, D], F32R)
        th = sb(NAME + "th", [P, GRP])
        a = sb(NAME + "a", [P, GRP])
        a_hi = sb(NAME + "a_hi", [P, 2, TOK], F32R)
        a_lo = sb(NAME + "a_lo", [P, 2, TOK], F32R)
        stats = sb(NAME + "stats", [P, 12])
        mv = sb(NAME + "mv", [P, 2])
        rstd = sb(NAME + "rstd", [P, 1])
        nmr = sb(NAME + "nmr", [P, 1])
        gu = ps(NAME + "gu", [P, 2, 2, 512])
        dn = ps(NAME + "dn", [P, 4, 512])
        const_loaded = sem(NAME + "const")
        half_made = sem(NAME + "half_made")
        x_loaded = [sem(NAME + "x0"), sem(NAME + "x1")]
        tp_done = sem(NAME + "tp_done")
        x_hi_done = sem(NAME + "x_hi_done")
        x_lo_done = sem(NAME + "x_lo_done")
        y_started = sem(NAME + "y_started")
        w_loaded = [sem(NAME + "w0"), sem(NAME + "w1")]
        w_hi_done = sem(NAME + "w_hi_done")
        w_lo_done = sem(NAME + "w_lo_done")
        gu_done = sem(NAME + "gu_done")
        th_done = sem(NAME + "th_done")
        a_done = sem(NAME + "a_done")
        a_hi_done = sem(NAME + "a_hi_done")
        a_lo_done = sem(NAME + "a_lo_done")
        dn_done = sem(NAME + "dn_done")
        y_added = sem(NAME + "y_added")
        var_done = sem(NAME + "var_done")
        rstd_done = sem(NAME + "rstd_done")
        nmr_done = sem(NAME + "nmr_done")
        normed = sem(NAME + "normed")
        gained = sem(NAME + "gained")
        out_done = sem(NAME + "out_done")
        stored = sem(NAME + "stored")
        vec = sem(NAME + "vec")
        w_view = d["w_ffn_in"].rearrange("(k p) n -> p k n", p=P)
        block3 = lambda ap: ap.rearrange("p (k c) -> p k c", k=KT)
        first_row = part * TOK

        with nc.Block() as block:
            @block.sync
            def _(sp):
                for to, of in ((ident[:, :], d["ident"]), (gain[:, :], d["ln2_g"].partition_broadcast(P)), (bias[:, :], d["ln2_b"].partition_broadcast(P))):
                    sp.dma_start(to, of).then_inc(const_loaded, 16)

                def weights(f, q):
                    wait(sp, w_lo_done, 3 * (f - 1))
                    sp.dma_start(block3(w[:, q, 0, :]), w_view[:, :, bass.ds(f * P, P)]).then_inc(w_loaded[q], 16)
                    sp.dma_start(block3(w[:, q, 1, :]), w_view[:, :, bass.ds(f * P + D_FF, P)]).then_inc(w_loaded[q], 16)
                    sp.dma_start(w[:, q, 2, :], d["w_ffn_out"][bass.ds(f * P, P), :]).then_inc(w_loaded[q], 16)

                for t in range(TILES):
                    wait(sp, tp_done, 2 * (t - 1))
                    wait(sp, y_started, t - 1)
                    sp.dma_start(x[:, t % 2, :], d["x1"][first_row + t * P:first_row + (t + 1) * P, :]).then_inc(x_loaded[t % 2], 16)
                    if t < 2:
                        weights(t, t)
                with sp.Fori(1, FB // 2) as i:
                    weights(2 * i, 0)
                    weights(2 * i + 1, 1)
                for t in range(TILES):
                    sp.wait_ge(out_done, t + 1)
                    sp.dma_start(d["y"][first_row + t * P:first_row + (t + 1) * P, :], y[:, t, :]).then_inc(stored, 16)
                sp.wait_ge(stored, 16 * TILES)

            @block.gpsimd
            def _(pool):
                nc.gpsimd.memset(neg_half[:, :], -0.5).then_inc(half_made, 1)
                pool.wait_ge(half_made, 1)
                pool.wait_ge(const_loaded, 48)

                def split(f, q):
                    for x in range(3):
                        pool.wait_ge(w_hi_done, 3 * f + x + 1)
                        nc.gpsimd.tensor_tensor(w_lo[:, q, x, :], w[:, q, x, :], w_hi[:, q, x, :].bitcast(F32), ALU.subtract).then_inc(w_lo_done, 1)

                split(0, 0)
                split(1, 1)
                with pool.Fori(1, FB // 2) as i:
                    split(2 * i, 0)
                    split(2 * i + 1, 1)
                for t in range(TILES):
                    pool.wait_ge(var_done, t + 1)
                    nc.gpsimd.tensor_tensor(rstd[:, :], mv[:, 1:2], neg_half[:, :], ALU.pow).then_inc(rstd_done, 1)
                    pool.wait_ge(gained, t + 1)
                    nc.gpsimd.tensor_tensor(y[:, t, :], y[:, t, :], bias[:, :], ALU.add).then_inc(out_done, 1)

            @block.scalar
            def _(act):
                def split(f, q, i):
                    act.wait_ge(w_loaded[q], 48 * (i + 1))
                    wait(act, dn_done, 12 * i)
                    for x in range(3):
                        nc.scalar.activation(w_hi[:, q, x, :], w[:, q, x, :], ACT.Copy).then_inc(w_hi_done, 1)

                def silu(f, q):
                    for g in range(2):
                        n = 2 * f + g
                        act.wait_ge(gu_done, n + 1)
                        wait(act, a_done, n)
                        nc.scalar.activation(th[:, :], gu[:, g, 0, 0:GRP], ACT.Tanh, scale=0.5).then_inc(th_done, 1)
                        act.wait_ge(a_done, n + 1)
                        nc.scalar.activation(a_hi[:, q, g * GRP:(g + 1) * GRP], a[:, :], ACT.Copy).then_inc(a_hi_done, 1)

                split(0, 0, 0)
                for t in range(TILES):
                    for b in range(2):
                        act.wait_ge(tp_done, 2 * t + b + 1)
                        nc.scalar.activation(x_hi[:, 4 * b:4 * b + 4, t * P:(t + 1) * P],
                                             dn[:, 2 * (t % 2) + b, :].rearrange("p (k c) -> p k c", k=4), ACT.Copy).then_inc(x_hi_done, 1)
                split(1, 1, 0)
                silu(0, 0)
                silu(1, 1)
                with act.Fori(1, FB // 2) as i:
                    split(2 * i, 0, i)
                    split(2 * i + 1, 1, i)
                    silu(2 * i, 0)
                    silu(2 * i + 1, 1)
                for t in range(TILES):
                    act.wait_ge(nmr_done, t + 1)
                    nc.scalar.activation(y[:, t, :], y[:, t, :], ACT.Identity, bias=nmr[:, :], scale=rstd[:, :]).then_inc(normed, 1)

            @block.vector
            def _(dve):
                dve.wait_ge(const_loaded, 48)
                for t in range(TILES):
                    dve.wait_ge(x_loaded[t % 2], 16 * (t // 2 + 1))
                    nc.vector.tensor_scalar(y[:, t, :], x[:, t % 2, :], ALPHA, None, ALU.mult).then_inc(y_started, 1)
                    for b in range(2):
                        dve.wait_ge(x_hi_done, 2 * t + b + 1)
                        at = x_hi[:, 4 * b:4 * b + 4, t * P:(t + 1) * P]
                        nc.vector.tensor_tensor(x_lo[:, 4 * b:4 * b + 4, t * P:(t + 1) * P],
                                                dn[:, 2 * (t % 2) + b, :].rearrange("p (k c) -> p k c", k=4), at.bitcast(F32), ALU.subtract).then_inc(x_lo_done, 1)
                dve.wait_ge(y_started, TILES)
                step = Tally(vec)

                def silu(f, q):
                    for g in range(2):
                        n = 2 * f + g
                        dve.wait_ge(th_done, n + 1)
                        wait(dve, a_hi_done, n)
                        v = step.inc(nc.vector.scalar_tensor_tensor(out=th[:, :], in0=th[:, :], scalar=1.0, in1=gu[:, g, 0, 0:GRP], op0=ALU.add, op1=ALU.mult))
                        dve.wait_ge(vec, v)
                        nc.vector.scalar_tensor_tensor(out=a[:, :], in0=th[:, :], scalar=0.5, in1=gu[:, g, 1, 0:GRP],
                                                       op0=ALU.mult, op1=ALU.mult).then_inc(a_done, 1)
                        dve.wait_ge(a_hi_done, n + 1)
                        cols = slice(g * GRP, (g + 1) * GRP)
                        nc.vector.tensor_tensor(a_lo[:, q, cols], a[:, :], a_hi[:, q, cols].bitcast(F32), ALU.subtract).then_inc(a_lo_done, 1)

                def add(i):
                    for n in range(12):
                        t, c = n // 2, slice(n % 2 * 512, (n % 2 + 1) * 512)
                        dve.wait_ge(dn_done, 12 * i + n + 1)
                        wait(dve, y_added, 12 * (i - 1) + n + 1)
                        nc.vector.tensor_tensor(y[:, t, c], dn[:, n % 4, :], y[:, t, c], ALU.add).then_inc(y_added, 1)

                def pair(i):
                    step.enter(4 * i)
                    silu(2 * i, 0)
                    silu(2 * i + 1, 1)
                    add(i)
                    assert step.k == 4

                pair(0)
                with dve.Fori(1, FB // 2) as i:
                    pair(i)
                step.enter(4 * (FB // 2))
                for t in range(TILES):
                    dve.wait_ge(y_added, 12 * (FB // 2))
                    nc.vector.bn_stats(stats[:, 0:6], y[:, t, 0:512])
                    v = step.inc(nc.vector.bn_stats(stats[:, 6:12], y[:, t, 512:1024]))
                    wait(dve, rstd_done, t)
                    dve.wait_ge(vec, v)
                    v = step.inc(nc.vector.bn_aggr(mv[:, :], stats[:, :]))
                    dve.wait_ge(vec, v)
                    nc.vector.tensor_scalar(mv[:, 1:2], mv[:, 1:2], LN_EPS, None, ALU.add).then_inc(var_done, 1)
                    dve.wait_ge(rstd_done, t + 1)
                    nc.vector.scalar_tensor_tensor(out=nmr[:, :], in0=mv[:, 0:1], scalar=-1.0, in1=rstd[:, :], op0=ALU.mult, op1=ALU.mult).then_inc(nmr_done, 1)
                    dve.wait_ge(normed, t + 1)
                    nc.vector.tensor_tensor(y[:, t, :], y[:, t, :], gain[:, :], ALU.mult).then_inc(gained, 1)

            @block.tensor
            def _(pe):
                pe.wait_ge(const_loaded, 48)
                for t in range(TILES):
                    pe.wait_ge(x_loaded[t % 2], 16 * (t // 2 + 1))
                    wait(pe, x_lo_done, 2 * (t - 1))
                    for b in range(2):
                        for k in range(4):
                            last = nc.tensor.transpose(dn[:, 2 * (t % 2) + b, k * P:(k + 1) * P], x[:, t % 2, (4 * b + k) * P:(4 * b + k + 1) * P], ident[:, :])
                        last.then_inc(tp_done, 1)
                pe.wait_ge(x_lo_done, 2 * TILES)

                def gate_up(f, q):
                    pe.wait_ge(w_lo_done, 3 * (f + 1))
                    for g in range(2):
                        wait(pe, a_done, 2 * (f - 1) + g + 1)
                        for m in range(2):
                            parts = [(ww, xx, k) for k in range(KT) for ww, xx in ((w_hi, x_hi), (w_lo, x_hi), (w_hi, x_lo))]
                            for j, (ww, xx, k) in enumerate(parts):
                                last = nc.tensor.matmul(gu[:, g, m, 0:GRP], ww[:, q, m, k * P:(k + 1) * P], xx[:, k, g * GRP:(g + 1) * GRP],
                                                        start=(j == 0), stop=(j == len(parts) - 1))
                        last.then_inc(gu_done, 1)

                def down(i):
                    for n in range(12):
                        t, c = n // 2, slice(n % 2 * 512, (n % 2 + 1) * 512)
                        pe.wait_ge(a_lo_done, 4 * i + (3 if t < TILES // 2 else 4))
                        wait(pe, y_added, 12 * i + n - 3)
                        parts = [(aa, ww, q) for q in range(2) for aa, ww in ((a_hi, w_hi), (a_hi, w_lo), (a_lo, w_hi))]
                        for j, (aa, ww, q) in enumerate(parts):
                            last = nc.tensor.matmul(dn[:, n % 4, :], aa[:, q, t * P:(t + 1) * P], ww[:, q, 2, c],
                                                    start=(j == 0), stop=(j == len(parts) - 1))
                        last.then_inc(dn_done, 1)

                def pair(i):
                    gate_up(2 * i, 0)
                    gate_up(2 * i + 1, 1)
                    down(i)

                pair(0)
                with pe.Fori(1, FB // 2) as i:
                    pair(i)


def build(nc, d, upto=99):
    with ExitStack() as keep:
        h_hi = keep.enter_context(nc.sbuf_tensor("h_hi", [P, KT, (NT + 1) * P], F32R))
        h_lo = keep.enter_context(nc.sbuf_tensor("h_lo", [P, KT, (NT + 1) * P], F32R))
        project(nc, d, (h_hi, h_lo))
        if upto >= 2:
            columns(nc, d, (h_hi, h_lo))
        if upto >= 3:
            qkv(nc, d, (h_hi, h_lo))
    if upto >= 4:
        attend(nc, d)
    if upto >= 5:
        scan(nc, d)
    if upto >= 7:
        mixout(nc, d)
    if upto >= 8:
        ffn(nc, d)


SCRATCH = {"h": (T_REAL, D), "rkv": (T_REAL + 2 * N_META, 3 * RW), "lora": (P, T_REAL + 2 * N_META),
           "qkv": ((NT + 1) * P, QKV), "mix": (T_REAL, D), "scan": (2, T_REAL, RW + RH), "x1": (T_REAL, D)}


def layout(inputs, np):
    f = lambda n: np.ascontiguousarray(inputs[n])
    a = {}
    a["x"] = np.concatenate([f("x_prompt")[0], f("x_sample")[0], f("meta_tokens"),
                             np.zeros((P - N_META, D), np.float32)], axis=0)
    a["w_in"] = f("w_in")[0]
    a["mu"] = np.ascontiguousarray(f("shift_mu")[0].reshape(2, MB, P).transpose(2, 0, 1))
    for n in ("ln_in_g", "ln_in_b", "q_gain", "k_gain", "ln1_g", "ln1_b", "ln2_g", "ln2_b", "k_k", "k_a", "gn_g", "gn_b"):
        a[n] = f(n).reshape(-1)
    a["r_k"] = f("r_k").reshape(-1)
    a["lora_up"] = np.ascontiguousarray(np.stack([np.concatenate([f(w)[0], f(b)[0][:, None]], axis=1).transpose(1, 0, 2)
                                                  for w, b in (("decay_up", "decay_w0"), ("iclr_up", "iclr_a0"))], axis=2))
    a["gate_up"] = f("gate_up")[0]
    a["w_out"], a["w_ffn_in"], a["w_ffn_out"] = f("w_out")[0], f("w_ffn_in")[0], f("w_ffn_out")[0]
    a["ident"] = np.eye(P, dtype=np.float32)
    a.update(tables(np))
    return a


def tables(np):
    freqs = HEAD // 4
    grid = 64
    pos = np.arange(max(SEQS))
    inv = 10000.0 ** (-np.arange(freqs, dtype=np.float64) / freqs)
    cos, sin = np.ones((NT + 1, P, HEAD)), np.zeros((NT + 1, P, HEAD))
    for t in range(NT):
        p = pos[(t if t < 4 else t - 4) * P:][:P]
        for axis, at in enumerate((p // grid, p % grid)):
            ang = at[:, None] * inv
            for half in range(2):
                c = slice(axis * 32 + half * 16, axis * 32 + half * 16 + 16)
                cos[t, :, c] = np.cos(ang)
                sin[t, :, c] = np.sin(ang) * (-1 if half == 0 else 1)
    i = np.arange(P)
    same = i[:, None] // CHUNK == i[None, :] // CHUNK
    tri = np.stack([same & (i[:, None] <= i[None, :]), same & (i[:, None] >= i[None, :])], axis=1)
    c = np.tile(np.arange(CHUNK), 2)[:, None]
    t = np.arange(CHUNK)[None, :]
    gram = np.stack([np.stack([c < t, c <= t], axis=1), np.stack([c > t, c >= t], axis=1)], axis=1)
    level = np.stack([np.stack([(c >> l ^ 1 == t >> l) & (after if z == 0 else before)
                                for l in range(LEVELS)], axis=1) for z, (after, before) in enumerate(((c > t, c < t),) * 2)], axis=1)
    keep = np.ones((P, 3, STEPS))
    first = SEQS[0] // P
    keep[:, 0, first - 1] = 0
    keep[:, 1, STEPS - first - 1] = 0
    keep[:, 2] = 1 - keep[:, 0]
    masks = {"eye": c == t, "tri": tri, "halves": i[:, None] // CHUNK == np.arange(2)[None, :], "gram_mask": gram,
             "level_mask": level, "keep": keep}
    out = {"cos": cos, "sin": sin, **masks}
    return {n: np.ascontiguousarray(v.astype(np.float32)) for n, v in out.items()}


def declare(nc, arrays, scratch_kind=None):
    d = {n: nc.dram_tensor(f"in_{n}", a.shape, mybir.dt.from_np(a.dtype), kind="ExternalInput").ap() for n, a in arrays.items()}
    for n, shape in SCRATCH.items():
        d[n] = nc.dram_tensor(f"scratch_{n}", shape, F32, kind=scratch_kind or "Internal").ap()
    d["y"] = nc.dram_tensor("out_y", (T_REAL, D), F32, kind="ExternalOutput").ap()
    return d


def kernel(**inputs):
    import numpy as np
    import concourse.bacc as bacc
    from concourse.bass_utils import run_bass_kernel_spmd

    nc = bacc.Bacc("TRN2", target_bir_lowering=False, num_devices=1)
    arrays = layout(inputs, np)
    build(nc, declare(nc, arrays))
    r = run_bass_kernel_spmd(nc, [{f"in_{n}": a for n, a in arrays.items()}], core_ids=[0])
    y = r.results[0]["out_y"]
    return y[0:SEQS[0]][None], y[SEQS[0]:][None]
```

```python
from contextlib import ExitStack

import concourse.bass as bass
from concourse import mybir

ALU = mybir.AluOpType
ACT = mybir.ActivationFunctionType
F32 = mybir.dt.float32
F32R = mybir.dt.float32r
AX = mybir.AxisListType

P = 128
D = 1024
KT = D // P
N_META = 16
SEQS = (512, 1024)
T_REAL = sum(SEQS)
NT = T_REAL // P
META_COL = T_REAL
HEAD = 64
RW = 512
RH = RW // HEAD
RWKV_IN = 1664
MB = RWKV_IN // P
IN_WIDTH = 2432
QKV = IN_WIDTH - RWKV_IN
ATT_H = 8
KV_H = 2
CHUNK = 64
D_FF = 2816
LN_EPS = 1e-5
GN_EPS = 64e-5
QK_EPS = 1e-6
ALPHA = 2.0 ** 0.25
DECAY = 0.6065306597126334
ROW0 = 1
SEG = [(1, 17, 512), (531, 547, 1024)]
ST = 1572


class Tally:

    def __init__(self, sem):
        self.sem, self.base, self.k = sem, 0, 0

    def enter(self, base):
        self.base, self.k = base, 0

    def inc(self, ins):
        ins.then_inc(self.sem, 1)
        self.k += 1
        return self.base + self.k

    def now(self):
        return self.base + self.k


def wait(eng, sem, value):
    if isinstance(value, int) and value <= 0:
        return
    eng.wait_ge(sem, value)


def hold(eng, sem, value, passed):
    if isinstance(value, int) and value <= 0:
        return
    eng.wait_ge(sem, value)
    eng.sem_inc(passed, 1)


def alloc(ctx, nc):
    def sb(name, shape, dt=F32):
        return ctx.enter_context(nc.sbuf_tensor(name, shape, dt))

    def ps(name, shape, dt=F32):
        return ctx.enter_context(nc.psum_tensor(name, shape, dt))

    sems = []

    def sem(name):
        sems.append(nc.alloc_semaphore(name))
        return sems[-1]

    def clear():
        nc.clear_and_free_semaphores(sems)
        nc.all_engine_barrier()

    ctx.callback(clear)
    return sb, ps, sem


def project(nc, d, hT):
    h_hi, h_lo = hT
    with ExitStack() as ctx:
        sb, ps, sem = alloc(ctx, nc)
        ident = sb("pj_ident", [P, P])
        gain = sb("pj_gain", [P, D])
        bias = sb("pj_bias", [P, D])
        neg_half = sb("pj_neg_half", [P, 1])
        x_in = sb("pj_x", [P, 2, D])
        hn = sb("pj_hn", [P, 2, D])
        stats = sb("pj_stats", [P, 2, 12])
        mv = sb("pj_mv", [P, 2, 2])
        rstd = sb("pj_rstd", [P, 2, 1])
        nmr = sb("pj_nmr", [P, 2, 1])
        tp = ps("pj_tp", [P, 4, 512])
        mm = ps("pj_mm", [P, 4, 512])
        x_loaded = [sem("pj_x0"), sem("pj_x1")]
        const_loaded = sem("pj_const")
        ident_made = sem("pj_ident_made")
        stats_done = sem("pj_stats_done")
        rstd_done = sem("pj_rstd_done")
        nmr_done = sem("pj_nmr_done")
        normed = sem("pj_normed")
        gained = sem("pj_gained")
        hn_done = sem("pj_hn_done")
        tp_done = sem("pj_tp_done")
        hi_done = sem("pj_hi_done")
        lo_done = sem("pj_lo_done")
        h_stored = [sem("pj_h_stored0"), sem("pj_h_stored1")]
        vec = sem("pj_vec")
        passed = sem("pj_passed")

        def steps(eng, step):
            for t in range(-2, 2):
                step(t, t % 2, t // 2)
            with eng.Fori(1, NT // 2 - 1) as i:
                for q in range(2):
                    step(2 * i + q, q, i)
            for t in range(NT - 2, NT + 1):
                step(t, t % 2, t // 2)

        def is_tile(t):
            return not isinstance(t, int) or 0 <= t <= NT

        with nc.Block() as block:
            @block.sync
            def _(sp):
                sp.dma_start(ident[:, :], d["ident"]).then_inc(const_loaded, 16)
                sp.dma_start(gain[:, :], d["ln_in_g"].partition_broadcast(P)).then_inc(const_loaded, 16)
                sp.dma_start(bias[:, :], d["ln_in_b"].partition_broadcast(P)).then_inc(const_loaded, 16)

                def load(t, q, turn):
                    wait(sp, normed, t - 1)
                    sp.dma_start(x_in[:, q, :], d["x"][bass.ds(t * P, P), :]).then_inc(x_loaded[q], 16)

                def store(t, q):
                    wait(sp, hn_done, t + 1)
                    sp.dma_start(d["h"][bass.ds(t * P, P), :], hn[:, q, :]).then_inc(h_stored[q], 16)

                load(0, 0, 0)
                load(1, 1, 0)
                with sp.Fori(0, NT // 2 - 1) as i:
                    for q in range(2):
                        load(2 * i + q + 2, q, 0)
                        store(2 * i + q, q)
                load(NT, 0, 0)
                store(NT - 2, 0)
                store(NT - 1, 1)
                sp.wait_ge(h_stored[0], 16 * (NT // 2))
                sp.wait_ge(h_stored[1], 16 * (NT // 2))

            @block.gpsimd
            def _(pool):
                nc.gpsimd.memset(neg_half[:, :], -0.5).then_inc(ident_made, 1)
                pool.wait_ge(ident_made, 1)
                pool.wait_ge(const_loaded, 48)

                def step(t, q, i):
                    if is_tile(t):
                        pool.wait_ge(gained, t + 1)
                        nc.gpsimd.tensor_tensor(hn[:, q, :], hn[:, q, :], bias[:, :], ALU.add).then_inc(hn_done, 1)
                    if is_tile(t + 2):
                        pool.wait_ge(stats_done, t + 3)
                        nc.gpsimd.tensor_tensor(rstd[:, q, :], mv[:, q, 1:2], neg_half[:, :], ALU.pow).then_inc(rstd_done, 1)

                steps(pool, step)

            @block.scalar
            def _(act):
                def normalise(t, q, i):
                    act.wait_ge(nmr_done, t + 1)
                    act.wait_ge(rstd_done, t + 1)
                    wait(act, tp_done, 2 * (t - 1))
                    wait(act, h_stored[q], 16 * i)
                    nc.scalar.activation(hn[:, q, :], x_in[:, q, :], ACT.Identity, bias=nmr[:, q, :], scale=rstd[:, q, :]).then_inc(normed, 1)

                def step(t, q, i):
                    if is_tile(t + 1):
                        normalise(t + 1, 1 - q, i + q)
                    if is_tile(t):
                        for b in range(2):
                            act.wait_ge(tp_done, 2 * t + b + 1)
                            nc.scalar.activation(h_hi[:, 4 * b:4 * b + 4, bass.ds(t * P, P)],
                                                 tp[:, 2 * q + b, :].rearrange("p (k c) -> p k c", k=4), ACT.Copy).then_inc(hi_done, 1)

                steps(act, step)

            @block.vector
            def _(dve):
                dve.wait_ge(const_loaded, 48)
                own = Tally(vec)

                def stat(t, q, turn):
                    dve.wait_ge(x_loaded[q], 16 * (turn + 1))
                    nc.vector.bn_stats(stats[:, q, 0:6], x_in[:, q, 0:512])
                    v = own.inc(nc.vector.bn_stats(stats[:, q, 6:12], x_in[:, q, 512:1024]))
                    wait(dve, normed, t - 1)
                    hold(dve, vec, v, passed)
                    v = own.inc(nc.vector.bn_aggr(mv[:, q, :], stats[:, q, :]))
                    dve.wait_ge(vec, v)
                    nc.vector.tensor_scalar(mv[:, q, 1:2], mv[:, q, 1:2], LN_EPS, None, ALU.add).then_inc(stats_done, 1)

                def step(t, q, i):
                    own.enter(2 * (t + 2))
                    if is_tile(t + 2):
                        stat(t + 2, q, i + 1)
                    if is_tile(t + 1):
                        dve.wait_ge(rstd_done, t + 2)
                        nc.vector.scalar_tensor_tensor(out=nmr[:, 1 - q, :], in0=mv[:, 1 - q, 0:1], scalar=-1.0, in1=rstd[:, 1 - q, :],
                                                       op0=ALU.mult, op1=ALU.mult).then_inc(nmr_done, 1)
                    if is_tile(t):
                        for b in range(2):
                            dve.wait_ge(hi_done, 2 * t + b + 1)
                            hi = h_hi[:, 4 * b:4 * b + 4, bass.ds(t * P, P)]
                            nc.vector.tensor_tensor(h_lo[:, 4 * b:4 * b + 4, bass.ds(t * P, P)],
                                                    tp[:, 2 * q + b, :].rearrange("p (k c) -> p k c", k=4),
                                                    hi.bitcast(F32), ALU.subtract).then_inc(lo_done, 1)
                    if is_tile(t + 1):
                        dve.wait_ge(normed, t + 2)
                        nc.vector.tensor_tensor(hn[:, 1 - q, :], hn[:, 1 - q, :], gain[:, :], ALU.mult).then_inc(gained, 1)

                steps(dve, step)

            @block.tensor
            def _(pe):
                pe.wait_ge(const_loaded, 48)

                def tile(t, q):
                    pe.wait_ge(hn_done, t + 1)
                    wait(pe, lo_done, 2 * (t - 1))
                    for b in range(2):
                        for k in range(4):
                            last = nc.tensor.transpose(tp[:, 2 * q + b, k * P:(k + 1) * P],
                                                       hn[:, q, (4 * b + k) * P:(4 * b + k + 1) * P], ident[:, :])
                        last.then_inc(tp_done, 1)

                tile(0, 0)
                tile(1, 1)
                with pe.Fori(1, NT // 2) as i:
                    tile(2 * i, 0)
                    tile(2 * i + 1, 1)
                tile(NT, 0)


def columns(nc, d, hT):
    h_hi, h_lo = hT
    with ExitStack() as ctx:
        sb, ps, sem = alloc(ctx, nc)
        ident = sb("co_ident", [P, P])
        mu = sb("co_mu", [P, 2, MB])
        keep = sb("co_keep", [P, MB])
        w_in = sb("co_w", [P, 2, KT, P])
        w_hi = sb("co_w_hi", [P, 2, KT, P], F32R)
        w_lo = sb("co_w_lo", [P, 2, KT, P], F32R)
        raw = sb("co_raw", [P, 2, ST])
        sh = sb("co_sh", [P, ST])
        tm = sb("co_tm", [P, 2, NT, P])
        tm_meta = sb("co_tm_meta", [N_META, 2, 2, P])
        lora = sb("co_lora", [P, ST])
        mm = ps("co_mm", [P, 4, 512])
        tp = ps("co_tp", [P, 4, 512])
        const_loaded = sem("co_const")
        consts_made = sem("co_consts_made")
        w_loaded = [sem("co_w0"), sem("co_w1")]
        hi_done = sem("co_hi_done")
        lo_done = sem("co_lo_done")
        group_done = sem("co_group_done")
        raw_done = sem("co_raw_done")
        vec = sem("co_vec")
        sh_done = sem("co_sh_done")
        tp_done = sem("co_tp_done")
        tm_done = sem("co_tm_done")
        tm_stored = [sem("co_tm_stored0"), sem("co_tm_stored1")]
        lora_done = sem("co_lora_done")
        gate_half = sem("co_gate_half")
        lora_stored = sem("co_lora_stored")
        w_view = d["w_in"].rearrange("(k p) n -> p k n", p=P)

        with nc.Block() as block:
            @block.sync
            def _(sp):
                sp.dma_start(ident[:, :], d["ident"]).then_inc(const_loaded, 16)
                sp.dma_start(mu[:, :, :], d["mu"]).then_inc(const_loaded, 16)

                def load(m, q):
                    wait(sp, lo_done, m - 1)
                    sp.dma_start(w_in[:, q, :, :], w_view[:, :, bass.ds(m * P, P)]).then_inc(w_loaded[q], 16)

                def store(m, q):
                    sp.wait_ge(tm_done, m + 1)
                    sp.dma_start(d["rkv"][0:T_REAL, bass.ds(m * P, P)].rearrange("(t p) f -> p t f", p=P),
                                 tm[:, q, :, :]).then_inc(tm_stored[q], 16)
                    sp.dma_start(d["rkv"][T_REAL:T_REAL + 2 * N_META, bass.ds(m * P, P)].rearrange("(s p) f -> p s f", p=N_META),
                                 tm_meta[:, q, :, :]).then_inc(tm_stored[q], 16)

                load(0, 0)
                load(1, 1)
                load(2, 0)
                with sp.Fori(0, (MB - 3) // 2) as i:
                    load(2 * i + 3, 1)
                    store(2 * i, 0)
                    load(2 * i + 4, 0)
                    store(2 * i + 1, 1)
                store(MB - 3, 0)
                store(MB - 2, 1)
                sp.wait_ge(lora_done, 2)
                sp.wait_ge(gate_half, 1)
                out = d["lora"]
                sp.dma_start(out[:, 0:512], lora[:, 17:529]).then_inc(lora_stored, 16)
                sp.dma_start(out[:, 512:1536], lora[:, 547:1571]).then_inc(lora_stored, 16)
                sp.dma_start(out[:, 1536:1552], lora[:, 1:17]).then_inc(lora_stored, 16)
                sp.dma_start(out[:, 1552:1568], lora[:, 531:547]).then_inc(lora_stored, 16)
                sp.wait_ge(lora_stored, 64)
                for q in range(2):
                    sp.wait_ge(tm_stored[q], 32 * ((MB - 1) // 2))

            @block.gpsimd
            def _(pool):
                for q in range(2):
                    for a in (0, 529, 530, 1571):
                        nc.gpsimd.memset(raw[:, q, a:a + 1], 0.0).then_inc(consts_made, 1)

                def split(m, q, turn):
                    pool.wait_ge(hi_done, m + 1)
                    nc.gpsimd.tensor_tensor(w_lo[:, q, :, :], w_in[:, q, :, :], w_hi[:, q, :, :].bitcast(F32),
                                            ALU.subtract).then_inc(lo_done, 1)

                split(0, 0, 0)
                with pool.Fori(0, (MB - 1) // 2) as i:
                    split(2 * i + 1, 1, i)
                    split(2 * i + 2, 0, i + 1)

            @block.scalar
            def _(act):
                def split(m, q, turn):
                    act.wait_ge(w_loaded[q], 16 * (turn + 1))
                    wait(act, group_done, 3 * (m - 1))
                    nc.scalar.activation(w_hi[:, q, :, :], w_in[:, q, :, :], ACT.Copy).then_inc(hi_done, 1)

                def evict(m, q):
                    wait(act, sh_done, m - 1)
                    for g, to in ((0, 17), (1, 547), (2, 1059)):
                        act.wait_ge(group_done, 3 * m + g + 1)
                        if g == 2:
                            for at in (1, 531):
                                nc.scalar.activation(raw[:, q, at:at + N_META], mm[:, 3, 0:N_META], ACT.Copy).then_inc(raw_done, 1)
                        nc.scalar.activation(raw[:, q, to:to + 512], mm[:, g, :], ACT.Copy).then_inc(raw_done, 1)

                split(0, 0, 0)
                split(1, 1, 0)
                evict(0, 0)

                def pair(i):
                    split(2 * i + 2, 0, i + 1)
                    evict(2 * i + 1, 1)
                    split(2 * i + 3, 1, i + 1)
                    evict(2 * i + 2, 0)

                pair(0)
                with act.Fori(1, (MB - 3) // 2) as i:
                    pair(i)
                split(MB - 1, 0, MB // 2)
                evict(MB - 2, 1)
                evict(MB - 1, 0)
                act.wait_ge(sh_done, MB)
                nc.scalar.activation(lora[0:32, 1:1571], sh[0:32, 1:1571], ACT.Tanh).then_inc(lora_done, 1)
                nc.scalar.activation(lora[64:128, 1:1571], sh[64:128, 1:1571], ACT.Tanh, scale=0.5).then_inc(lora_done, 1)

            @block.vector
            def _(dve):
                dve.wait_ge(const_loaded, 32)
                dve.wait_ge(consts_made, 8)
                step = Tally(vec)
                v = step.inc(nc.vector.tensor_scalar(keep[:, :], mu[:, 0, :], -1.0, 1.0, ALU.mult, ALU.add))
                dve.wait_ge(vec, v)
                v = step.inc(nc.vector.tensor_tensor(keep[:, :], keep[:, :], mu[:, 1, :], ALU.subtract))
                dve.wait_ge(vec, v)

                def shift(m, q):
                    dve.wait_ge(raw_done, 5 * (m + 1))
                    n = ST - 2
                    v = step.inc(nc.vector.tensor_scalar(sh[:, 1:1 + n], raw[:, q, 1:1 + n], keep[:, bass.ds(m, 1)], None, ALU.mult))
                    dve.wait_ge(vec, v)
                    v = step.inc(nc.vector.scalar_tensor_tensor(out=sh[:, 1:1 + n], in0=raw[:, q, 0:n], scalar=mu[:, 0, bass.ds(m, 1)],
                                                                in1=sh[:, 1:1 + n], op0=ALU.mult, op1=ALU.add))
                    dve.wait_ge(vec, v)
                    nc.vector.scalar_tensor_tensor(out=sh[:, 1:1 + n], in0=raw[:, q, 2:2 + n], scalar=mu[:, 1, bass.ds(m, 1)],
                                                   in1=sh[:, 1:1 + n], op0=ALU.mult, op1=ALU.add).then_inc(sh_done, 1)

                def turned(m, q, turn):
                    wait(dve, tm_stored[q], 32 * turn)
                    for b in range(3):
                        dve.wait_ge(tp_done, 4 * m + b + 1)
                        nc.vector.tensor_copy(tm[:, q, 4 * b:4 * b + 4, :], tp[:, b, :].rearrange("p (t f) -> p t f", t=4))
                    dve.wait_ge(tp_done, 4 * m + 4)
                    nc.vector.tensor_copy(tm_meta[:, q, :, :], tp[0:N_META, 3, 0:2 * P].rearrange("p (s f) -> p s f", s=2)).then_inc(tm_done, 1)

                shift(0, 0)
                first = step.now()

                def pair(i):
                    step.enter(first + i * 4)
                    turned(2 * i, 0, i)
                    shift(2 * i + 1, 1)
                    turned(2 * i + 1, 1, i)
                    shift(2 * i + 2, 0)
                    assert step.k == 4

                pair(0)
                with dve.Fori(1, (MB - 1) // 2) as i:
                    pair(i)
                step.enter(first + 4 * ((MB - 1) // 2))
                dve.wait_ge(lora_done, 2)
                nc.vector.tensor_copy(lora[32:64, 1:1571], sh[32:64, 1:1571])
                nc.vector.tensor_scalar(lora[64:128, 1:1571], lora[64:128, 1:1571], 0.5, 0.5, ALU.mult, ALU.add).then_inc(gate_half, 1)

            @block.tensor
            def _(pe):
                pe.wait_ge(const_loaded, 32)

                def product(m, q):
                    pe.wait_ge(lo_done, m + 1)
                    pe.wait_ge(hi_done, m + 1)
                    for g in range(3):
                        wait(pe, raw_done, 5 * (m - 1) + (1, 2, 5)[g])
                        parts = [(w, x, k) for k in range(KT) for w, x in ((w_hi, h_hi), (w_lo, h_hi), (w_hi, h_lo))]
                        for j, (w, x, k) in enumerate(parts):
                            last = nc.tensor.matmul(mm[:, g, :], w[:, q, k, :], x[:, k, g * 512:(g + 1) * 512],
                                                    start=(j == 0), stop=(j == len(parts) - 1))
                            if g == 2:
                                last = nc.tensor.matmul(mm[:, 3, 0:N_META], w[:, q, k, :], x[:, k, META_COL:META_COL + N_META],
                                                        start=(j == 0), stop=(j == len(parts) - 1))
                        last.then_inc(group_done, 1)

                def turn(m):
                    pe.wait_ge(sh_done, m + 1)
                    wait(pe, tm_done, m)
                    for b in range(3):
                        for t in range(4 * b, 4 * b + 4):
                            at = 17 + t * P if t < 4 else 547 + (t - 4) * P
                            last = nc.tensor.transpose(tp[:, b, (t % 4) * P:(t % 4 + 1) * P], sh[:, at:at + P], ident[:, :])
                        last.then_inc(tp_done, 1)
                    for s, at in enumerate((1, 531)):
                        last = nc.tensor.transpose(tp[0:N_META, 3, s * P:(s + 1) * P], sh[:, at:at + N_META], ident[:, :])
                    last.then_inc(tp_done, 1)

                def pair(i):
                    product(2 * i + 1, 1)
                    turn(2 * i)
                    product(2 * i + 2, 0)
                    turn(2 * i + 1)

                product(0, 0)
                pair(0)
                with pe.Fori(1, (MB - 1) // 2) as i:
                    pair(i)


def qkv(nc, d, hT):
    h_hi, h_lo = hT
    NQK = 640
    W_SLOTS = 4
    with ExitStack() as ctx:
        sb, ps, sem = alloc(ctx, nc)
        w_in = sb("qk_w", [P, W_SLOTS, QKV])
        w_hi = sb("qk_w_hi", [P, KT, QKV], F32R)
        w_lo = sb("qk_w_lo", [P, KT, QKV], F32R)
        cos = sb("qk_cos", [P, NT + 1, HEAD])
        sin = sb("qk_sin", [P, NT + 1, HEAD])
        gain = sb("qk_gain", [P, 2, HEAD])
        neg_half = sb("qk_neg_half", [P, 10])
        square = sb("qk_square", [P, NQK])
        ssq = sb("qk_ssq", [P, 2, 10])
        rstd = sb("qk_rstd", [P, 2, 10])
        normed = sb("qk_normed", [P, 2, NQK])
        turned = sb("qk_turned", [P, 2, NQK])
        out = sb("qk_out", [P, 2, QKV])
        mm = ps("qk_mm", [P, 2, 2, 512])
        const_loaded = sem("qk_const")
        half_made = sem("qk_half_made")
        w_loaded = [sem(f"qk_w{k}") for k in range(W_SLOTS)]
        hi_done = sem("qk_hi_done")
        lo_done = sem("qk_lo_done")
        product_done = sem("qk_product_done")
        squared = sem("qk_squared")
        ssq_done = sem("qk_ssq_done")
        rstd_done = sem("qk_rstd_done")
        norm_done = sem("qk_norm_done")
        swap_done = sem("qk_swap_done")
        v_done = sem("qk_v_done")
        out_done = sem("qk_out_done")
        stored = [sem("qk_stored0"), sem("qk_stored1")]
        vec = sem("qk_vec")
        last_tile = NT
        with nc.Block() as block:
            @block.sync
            def _(sp):
                for k in range(KT):
                    wait(sp, lo_done, k + 1 - W_SLOTS)
                    sp.dma_start(w_in[:, k % W_SLOTS, :], d["w_in"][k * P:(k + 1) * P, RWKV_IN:IN_WIDTH]).then_inc(w_loaded[k % W_SLOTS], 16)
                    if k == W_SLOTS - 1:
                        sp.dma_start(cos[:, :, :], d["cos"].rearrange("t p c -> p t c")).then_inc(const_loaded, 16)
                        sp.dma_start(sin[:, :, :], d["sin"].rearrange("t p c -> p t c")).then_inc(const_loaded, 16)
                        sp.dma_start(gain[:, 0, :], d["q_gain"].partition_broadcast(P)).then_inc(const_loaded, 16)
                        sp.dma_start(gain[:, 1, :], d["k_gain"].partition_broadcast(P)).then_inc(const_loaded, 16)

                def store(t, q):
                    sp.wait_ge(out_done, t + 1)
                    sp.dma_start(d["qkv"][bass.ds(t * P, P), :], out[:, q, :]).then_inc(stored[q], 16)

                with sp.Fori(0, NT // 2) as i:
                    store(2 * i, 0)
                    store(2 * i + 1, 1)
                store(last_tile, 0)
                sp.wait_ge(stored[0], 16 * (NT // 2 + 1))
                sp.wait_ge(stored[1], 16 * (NT // 2))

            @block.gpsimd
            def _(pool):
                nc.gpsimd.memset(neg_half[:, :], -0.5).then_inc(half_made, 1)
                pool.wait_ge(half_made, 1)
                pool.wait_ge(const_loaded, 64)

                def tile(t, q):
                    pool.wait_ge(ssq_done, t + 1)
                    nc.gpsimd.tensor_tensor(rstd[:, q, :], ssq[:, q, :], neg_half[:, :], ALU.pow).then_inc(rstd_done, 1)
                    pool.wait_ge(norm_done, t + 1)
                    wait(pool, out_done, t - 1)
                    x = normed[:, q, :].rearrange("p (h a s f) -> p h a s f", a=2, s=2, f=16)
                    o = turned[:, q, :].rearrange("p (h a s f) -> p h a s f", a=2, s=2, f=16)
                    tab = sin[:, bass.ds(t, 1), :].rearrange("p o (a s f) -> p o a s f", a=2, s=2)
                    for s in range(2):
                        nc.gpsimd.tensor_tensor(o[:, :, :, s, :], x[:, :, :, 1 - s, :],
                                                tab[:, :, :, s, :].broadcast_to([P, 10, 2, 16]), ALU.mult).then_inc(swap_done, 1)

                tile(0, 0)
                tile(1, 1)
                with pool.Fori(1, NT // 2) as i:
                    tile(2 * i, 0)
                    tile(2 * i + 1, 1)
                tile(last_tile, 0)

            @block.scalar
            def _(act):
                for k in range(KT):
                    act.wait_ge(w_loaded[k % W_SLOTS], 16 * (k // W_SLOTS + 1))
                    nc.scalar.activation(w_hi[:, k, :], w_in[:, k % W_SLOTS, :], ACT.Copy).then_inc(hi_done, 1)

                def tile(t, q, turn):
                    act.wait_ge(product_done, t + 1)
                    wait(act, ssq_done, t)
                    nc.scalar.activation(square[:, 0:512], mm[:, q, 0, :], ACT.Square)
                    nc.scalar.activation(square[:, 512:NQK], mm[:, q, 1, 0:P], ACT.Square).then_inc(squared, 1)
                    wait(act, stored[q], 16 * turn)
                    nc.scalar.activation(out[:, q, NQK:QKV], mm[:, q, 1, P:2 * P], ACT.Copy).then_inc(v_done, 1)

                tile(0, 0, 0)
                tile(1, 1, 0)
                with act.Fori(1, NT // 2) as i:
                    tile(2 * i, 0, i)
                    tile(2 * i + 1, 1, i)
                tile(last_tile, 0, NT // 2)

            @block.vector
            def _(dve):
                for k in range(KT):
                    dve.wait_ge(hi_done, k + 1)
                    nc.vector.tensor_tensor(w_lo[:, k, :], w_in[:, k % W_SLOTS, :], w_hi[:, k, :].bitcast(F32), ALU.subtract).then_inc(lo_done, 1)
                dve.wait_ge(const_loaded, 64)
                step = Tally(vec)

                def tile(t, q):
                    heads = lambda ap: ap.rearrange("p (h c) -> p h c", c=HEAD)
                    dve.wait_ge(squared, t + 1)
                    wait(dve, rstd_done, t - 1)
                    v = step.inc(nc.vector.tensor_reduce(ssq[:, q, :], heads(square[:, :]), AX.X, ALU.add))
                    dve.wait_ge(vec, v)
                    nc.vector.tensor_scalar(ssq[:, q, :], ssq[:, q, :], 1.0 / HEAD, QK_EPS, ALU.mult, ALU.add).then_inc(ssq_done, 1)
                    dve.wait_ge(rstd_done, t + 1)
                    wait(dve, swap_done, 2 * (t - 1))
                    dve.wait_ge(v_done, t + 1)
                    r = rstd[:, q, :].unsqueeze(2)
                    nc.vector.tensor_tensor(heads(normed[:, q, 0:512]), heads(mm[:, q, 0, :]), r[:, 0:8, :].broadcast_to([P, 8, HEAD]), ALU.mult)
                    v = step.inc(nc.vector.tensor_tensor(heads(normed[:, q, 512:NQK]), heads(mm[:, q, 1, 0:P]),
                                                         r[:, 8:10, :].broadcast_to([P, 2, HEAD]), ALU.mult))
                    dve.wait_ge(vec, v)
                    nc.vector.tensor_tensor(heads(normed[:, q, 0:512]), heads(normed[:, q, 0:512]),
                                            gain[:, 0:1, :].broadcast_to([P, 8, HEAD]), ALU.mult)
                    nc.vector.tensor_tensor(heads(normed[:, q, 512:NQK]), heads(normed[:, q, 512:NQK]),
                                            gain[:, 1:2, :].broadcast_to([P, 2, HEAD]), ALU.mult).then_inc(norm_done, 1)
                    dve.wait_ge(norm_done, t + 1)
                    c = cos[:, bass.ds(t, 1), :]
                    x = normed[:, q, 0:512].rearrange("p (g j c) -> p g j c", g=2, j=4)
                    y = out[:, q, 0:512].rearrange("p (j g c) -> p g j c", g=2, j=4)
                    s = turned[:, q, 0:512].rearrange("p (g j c) -> p g j c", g=2, j=4)
                    nc.vector.tensor_tensor(y[:, 0], x[:, 0], c.broadcast_to([P, 4, HEAD]), ALU.mult)
                    nc.vector.tensor_tensor(y[:, 1], x[:, 1], c.broadcast_to([P, 4, HEAD]), ALU.mult)
                    v = step.inc(nc.vector.tensor_tensor(heads(out[:, q, 512:NQK]), heads(normed[:, q, 512:NQK]), c.broadcast_to([P, 2, HEAD]), ALU.mult))
                    dve.wait_ge(vec, v)
                    dve.wait_ge(swap_done, 2 * t + 2)
                    nc.vector.tensor_tensor(y, y, s, ALU.add)
                    nc.vector.tensor_tensor(out[:, q, 512:NQK], out[:, q, 512:NQK], turned[:, q, 512:NQK], ALU.add).then_inc(out_done, 1)

                tile(0, 0)
                tile(1, 1)
                with dve.Fori(1, NT // 2) as i:
                    step.enter(i * 6)
                    tile(2 * i, 0)
                    tile(2 * i + 1, 1)
                    assert step.k == 6
                step.enter(6 * (NT // 2))
                tile(last_tile, 0)

            @block.tensor
            def _(pe):
                def tile(t, q, cols):
                    wait(pe, norm_done, t - 1)
                    wait(pe, v_done, t - 1)
                    for k in range(KT):
                        if t == 0:
                            pe.wait_ge(lo_done, k + 1)
                        for j, (x, w) in enumerate(((h_hi, w_hi), (h_hi, w_lo), (h_lo, w_hi))):
                            for c, width in ((0, 512), (1, 256)):
                                last = nc.tensor.matmul(mm[:, q, c, 0:width], x[:, k, cols], w[:, k, c * 512:c * 512 + width],
                                                        start=(k == 0 and j == 0), stop=(k == KT - 1 and j == 2))
                    last.then_inc(product_done, 1)

                for t in range(NT + 1):
                    tile(t, t % 2, slice(t * P, (t + 1) * P))


def attend(nc, d):
    SCALE = HEAD ** -0.5
    with ExitStack() as ctx:
        sb, ps, sem = alloc(ctx, nc)
        ident = sb("at_ident", [P, P])
        kv = sb("at_kv", [P, NT + 1, 256])
        v_meta = sb("at_v_meta", [P, ATT_H * HEAD])
        kT = sb("at_kT", [P, (NT + 1) * P])
        k_meta = sb("at_k_meta", [P, KV_H * N_META])
        q_in = sb("at_q", [P, 2, 512])
        qT = sb("at_qT", [P, 2, 4, P])
        probs = sb("at_probs", [P, 2, 1024])
        probsT = sb("at_probsT", [P, 2, 1024])
        top = sb("at_top", [P, 2])
        neg_top = sb("at_neg_top", [P, 2, ATT_H])
        total = sb("at_total", [P, 2, ATT_H])
        m_score = sb("at_m_score", [P, ATT_H * N_META])
        m_top = sb("at_m_top", [P, ATT_H])
        m_arg = sb("at_m_arg", [P, ATT_H * N_META])
        m_prob = sb("at_m_prob", [P, ATT_H * N_META])
        m_probT = sb("at_m_probT", [P, P])
        m_sum = sb("at_m_sum", [P, ATT_H])
        inv = sb("at_inv", [P, ATT_H])
        out = sb("at_out", [P, 2, 512])
        S = ps("at_S", [P, 2, 2, 512])
        PT = ps("at_PT", [P, 2, 512])
        M = ps("at_M", [P, 512])
        O = ps("at_O", [P, 512])
        loaded = sem("at_loaded")
        zeroed = sem("at_zeroed")
        k_zeroed = sem("at_k_zeroed")
        vm_loaded = sem("at_vm_loaded")
        kT_done = sem("at_kT_done")
        kT_copied = sem("at_kT_copied")
        q_loaded = [sem("at_q0"), sem("at_q1")]
        qT_done = sem("at_qT_done")
        qT_copied = sem("at_qT_copied")
        ms_done = sem("at_ms_done")
        ms_copied = sem("at_ms_copied")
        s_done = sem("at_s_done")
        top_done = sem("at_top_done")
        exp_done = sem("at_exp_done")
        t_done = sem("at_t_done")
        t_by_vec = sem("at_t_by_vec")
        t_by_act = sem("at_t_by_act")
        pv_done = sem("at_pv_done")
        m_arg_done = sem("at_m_arg_done")
        m_exp_done = sem("at_m_exp_done")
        mT_done = sem("at_mT_done")
        mT_copied = sem("at_mT_copied")
        o_done = sem("at_o_done")
        out_done = sem("at_out_done")
        out_stored = [sem("at_out0"), sem("at_out1")]
        vec = sem("at_vec")
        sp_passed = sem("at_sp_passed")

        QUERY_AT = 5

        def over(eng, pair):
            pair(0, 0, 4, (0, 4))
            pair(1, 0, 4, (4, 8))
            with eng.Fori(2, NT // 2 - 1) as i:
                pair(i, 4, 8, (4, 8))
            pair(NT // 2 - 1, 4, 8, None)

        with nc.Block() as block:
            @block.sync
            def _(sp):
                sp.dma_start(ident[:, :], d["ident"]).then_inc(loaded, 16)
                sp.dma_start(kv[:, :, :], d["qkv"][:, 512:QKV].rearrange("(t p) c -> p t c", p=P)).then_inc(loaded, 16)
                sp.wait_ge(zeroed, 1)
                for h in range(ATT_H):
                    g = h // 4
                    sp.dma_start(v_meta[h * N_META:(h + 1) * N_META, h * HEAD:(h + 1) * HEAD],
                                 d["qkv"][NT * P:NT * P + N_META, 640 + g * HEAD:640 + (g + 1) * HEAD]).then_inc(vm_loaded, 16)

                def load(t, q):
                    hold(sp, qT_done, t - 1, sp_passed)
                    sp.dma_start(q_in[:, q, :], d["qkv"][bass.ds(t * P, P), 0:512]).then_inc(q_loaded[q], 16)

                def store(t, q):
                    hold(sp, out_done, t + 1, sp_passed)
                    sp.dma_start(d["mix"][bass.ds(t * P, P), RW:D], out[:, q, :]).then_inc(out_stored[q], 16)

                load(0, 0)
                load(1, 1)
                with sp.Fori(0, NT // 2 - 1) as i:
                    for q in range(2):
                        load(2 * i + q + 2, q)
                        store(2 * i + q, q)
                store(NT - 2, 0)
                store(NT - 1, 1)
                for q in range(2):
                    sp.wait_ge(out_stored[q], 16 * (NT // 2))

            @block.gpsimd
            def _(pool):
                nc.gpsimd.memset(v_meta[:, :], 0.0).then_inc(zeroed, 1)
                nc.gpsimd.memset(k_meta[:, :], 0.0).then_inc(k_zeroed, 1)

            @block.scalar
            def _(act):
                def pair(i, first, n, after):
                    half = n // 2 * P
                    for q in range(2):
                        t = 2 * i + q
                        for h in range(ATT_H):
                            u = t * ATT_H + h
                            act.wait_ge(top_done, u + 1)
                            wait(act, t_done, 2 * (u - 1))
                            nc.scalar.activation(probs[:, h % 2, 0:n * P], S[:, h % 2].rearrange("p b c -> p (b c)")[:, 0:n * P], ACT.Exp,
                                                 bias=neg_top[:, q, h:h + 1], scale=SCALE, accum_out=total[:, q, h:h + 1]).then_inc(exp_done, 1)
                            act.wait_ge(t_done, 2 * u + 2)
                            wait(act, pv_done, u - 1)
                            nc.scalar.activation(probsT[:, h % 2, half:2 * half], PT[:, 1, 0:half], ACT.Copy).then_inc(t_by_act, 1)
                        act.wait_ge(m_arg_done, t + 1)
                        wait(act, mT_done, t)
                        nc.scalar.activation(m_prob[:, :], m_arg[:, :], ACT.Exp).then_inc(m_exp_done, 1)

                over(act, pair)

            @block.vector
            def _(dve):
                for b in range(4):
                    n = 4 if b < 3 else 1
                    dve.wait_ge(kT_done, b + 1)
                    nc.vector.tensor_copy(kT[:, b * 512:b * 512 + n * P], S[:, b // 2, b % 2, 0:n * P]).then_inc(kT_copied, 1)
                dve.wait_ge(k_zeroed, 1)
                dve.wait_ge(kT_copied, 4)
                for g in range(KV_H):
                    nc.vector.tensor_copy(k_meta[g * HEAD:(g + 1) * HEAD, g * N_META:(g + 1) * N_META],
                                          kT[g * HEAD:(g + 1) * HEAD, META_COL:META_COL + N_META]).then_inc(kT_copied, 1)
                step = Tally(vec)
                per = 4
                heads = lambda ap, c: ap.rearrange("p (h c) -> p h c", c=c)

                def query(t, q):
                    dve.wait_ge(qT_done, t + 1)
                    nc.vector.tensor_copy(qT[:, q, :, :], M[:, :].rearrange("p (j c) -> p j c", j=4)).then_inc(qT_copied, 1)

                def meta_scores(t):
                    dve.wait_ge(ms_done, t + 1)
                    v = step.inc(nc.vector.tensor_copy(m_score[:, :].rearrange("p (g j c) -> p g j c", g=2, j=4),
                                                       M[:, 0:P].rearrange("p (j g c) -> p g j c", g=2, j=4)))
                    dve.wait_ge(vec, v)
                    nc.vector.tensor_reduce(m_top[:, :], heads(m_score[:, :], N_META), AX.X, ALU.max).then_inc(ms_copied, 1)
                    dve.wait_ge(ms_copied, t + 1)

                def pair(i, first, n, after):
                    half = n // 2 * P
                    for q in range(2):
                        t = 2 * i + q
                        step.enter(t * (ATT_H + per))
                        meta_scores(t)
                        for h in range(ATT_H):
                            u = t * ATT_H + h
                            dve.wait_ge(s_done, u + 1)
                            v = step.inc(nc.vector.tensor_reduce(top[:, h % 2:h % 2 + 1], S[:, h % 2].rearrange("p b c -> p (b c)")[:, 0:n * P], AX.X, ALU.max))
                            dve.wait_ge(vec, v)
                            nc.vector.tensor_scalar(neg_top[:, q, h:h + 1], top[:, h % 2:h % 2 + 1], m_top[:, h:h + 1], -SCALE,
                                                    ALU.max, ALU.mult).then_inc(top_done, 1)
                            if h > 0:
                                turned(u - 1, h - 1, half)
                            if h == QUERY_AT and (q == 0 or after):
                                query(t + 1, 1 - q)
                        turned(t * ATT_H + ATT_H - 1, ATT_H - 1, half)
                        dve.wait_ge(top_done, (t + 1) * ATT_H)
                        nc.vector.scalar_tensor_tensor(out=heads(m_arg[:, :], N_META), in0=heads(m_score[:, :], N_META), scalar=SCALE,
                                                       in1=neg_top[:, q, :].unsqueeze(2).broadcast_to([P, ATT_H, N_META]),
                                                       op0=ALU.mult, op1=ALU.add).then_inc(m_arg_done, 1)
                        dve.wait_ge(m_exp_done, t + 1)
                        v = step.inc(nc.vector.tensor_reduce(m_sum[:, :], heads(m_prob[:, :], N_META), AX.X, ALU.add))
                        dve.wait_ge(vec, v)
                        v = step.inc(nc.vector.tensor_tensor(m_sum[:, :], m_sum[:, :], total[:, q, :], ALU.add))
                        dve.wait_ge(vec, v)
                        v = step.inc(nc.vector.reciprocal(inv[:, :], m_sum[:, :]))
                        dve.wait_ge(mT_done, t + 1)
                        nc.vector.tensor_copy(m_probT[:, :], M[:, 0:P]).then_inc(mT_copied, 1)
                        dve.wait_ge(vec, v)
                        dve.wait_ge(o_done, t + 1)
                        wait(dve, out_stored[q], i * 16)
                        nc.vector.tensor_tensor(heads(out[:, q, :], HEAD), heads(O[:, :], HEAD),
                                                inv[:, :].unsqueeze(2).broadcast_to([P, ATT_H, HEAD]), ALU.mult).then_inc(out_done, 1)
                        assert step.k == ATT_H + per

                def turned(u, h, half):
                    dve.wait_ge(t_done, 2 * u + 1)
                    wait(dve, pv_done, u - 1)
                    nc.vector.tensor_copy(probsT[:, h % 2, 0:half], PT[:, 0, 0:half]).then_inc(t_by_vec, 1)

                query(0, 0)
                over(dve, pair)

            @block.tensor
            def _(pe):
                pe.wait_ge(loaded, 32)
                for t in range(NT + 1):
                    last = nc.tensor.transpose(S[:, t // 8, t // 4 % 2, t % 4 * P:(t % 4 + 1) * P], kv[:, t, 0:P], ident[:, :])
                    if t % 4 == 3 or t == NT:
                        last.then_inc(kT_done, 1)
                pe.wait_ge(vm_loaded, 16 * ATT_H)
                pe.wait_ge(kT_copied, 6)

                def rows(h):
                    g = h // 4
                    return slice(g * HEAD, (g + 1) * HEAD)

                def query(t, q, i):
                    wait(pe, ms_copied, t)
                    pe.wait_ge(q_loaded[q], 16 * (i + 1))
                    for j in range(4):
                        last = nc.tensor.transpose(M[:, j * P:(j + 1) * P], q_in[:, q, j * P:(j + 1) * P], ident[:, :])
                    last.then_inc(qT_done, 1)

                def meta_scores(t, q):
                    wait(pe, mT_copied, t)
                    for j in range(4):
                        last = nc.tensor.matmul(M[:, j * 32:(j + 1) * 32], qT[:, q, j, :], k_meta[:, :], start=True, stop=True)
                    last.then_inc(ms_done, 1)

                def score(t, q, h, first, n):
                    u = t * ATT_H + h
                    wait(pe, exp_done, u - 1)
                    for b in range(n // 4):
                        c = (first + 4 * b) * P
                        last = nc.tensor.matmul(S[:, h % 2, b, :], qT[rows(h), q, h % 4, :], kT[rows(h), c:c + 512], start=True, stop=True)
                    last.then_inc(s_done, 1)

                def turn(t, h, n):
                    u = t * ATT_H + h
                    pe.wait_ge(exp_done, u + 1)
                    for b in range(2):
                        wait(pe, (t_by_vec, t_by_act)[b], u)
                        for k in range(n // 2):
                            at = (b * (n // 2) + k) * P
                            last = nc.tensor.transpose(PT[:, b, k * P:(k + 1) * P], probs[:, h % 2, at:at + P], ident[:, :])
                        last.then_inc(t_done, 1)

                def value(t, h, first, n):
                    u = t * ATT_H + h
                    pe.wait_ge(t_by_vec, u + 1)
                    pe.wait_ge(t_by_act, u + 1)
                    if h == 0:
                        wait(pe, out_done, t)
                    for k in range(n):
                        g = h // 4
                        for c in range(2):
                            at = k * P + c * (P // 2)
                            last = nc.tensor.matmul(O[c * 64:c * 64 + 64, h * HEAD:(h + 1) * HEAD], probsT[:, h % 2, at:at + P // 2],
                                                    kv[:, first + k, P + g * HEAD:P + (g + 1) * HEAD], start=(h == 0 and k == 0), stop=False,
                                                    skip_group_check=True)
                    last.then_inc(pv_done, 1)

                def pair(i, first, n, after):
                    for q in range(2):
                        t = 2 * i + q
                        meta_scores(t, q)
                        for h in range(ATT_H):
                            if h + 1 < ATT_H:
                                score(t, q, h + 1, first, n)
                            if h > 0:
                                value(t, h - 1, first, n)
                            if h == QUERY_AT and (q == 0 or after):
                                query(t + 1, 1 - q, i + q)
                            turn(t, h, n)
                        value(t, ATT_H - 1, first, n)
                        if q == 0 or after:
                            pe.wait_ge(qT_copied, t + 2)
                            score(t + 1, 1 - q, 0, *((first, n) if q == 0 else after))
                        pe.wait_ge(m_exp_done, t + 1)
                        nc.tensor.transpose(M[:, 0:P], m_prob[:, :], ident[:, :]).then_inc(mT_done, 1)
                        pe.wait_ge(mT_copied, t + 1)
                        nc.tensor.matmul(O[:, :], m_probT[:, :], v_meta[:, :], start=False, stop=True, skip_group_check=True).then_inc(o_done, 1)

                query(0, 0, 0)
                pe.wait_ge(qT_copied, 1)
                score(0, 0, 0, 0, 4)
                over(pe, pair)


W_LOGIT, A_LOGIT, CUM, CHUNK_SUM, T_K, T_R, T_B, T_D = range(8)
GRAM = 8
D_V = 12
Y_SLOT = (13, 14, 17, 20, 23, 26)
X_SLOT = (None, 15, 18, 21, 24, None)
XT_SLOT = (None, 16, 19, 22, 25, 27)
SLOTS = 28
PER_BANK = [len(range(b, SLOTS, 3)) for b in range(3)]
LEVELS = 6
STEPS = NT
LEVEL_STAGES = [(x, l) for l in range(LEVELS) for x in ("y", "x", "t") if x != "x" or X_SLOT[l]]
BACK = ("carry0", "solve0", "state0", "carry1", "solve1", "state1", "emit")

PREP = {"logits": 0.035, "gates": 0.08, "sums": 0.2, "decay": 0.27, "keys": 0.33, "tilde": 0.44, "turn0": 0.52, "turn1": 0.6,
        "gram0": 0.68, "gram1": 0.75, "gram2": 0.82, "gram3": 0.89, "dv": 0.95}


def among(prep, levels, back=()):
    at = [(PREP[stage[-2] if stage[-1] is None else stage[-1]], 0, stage) for stage in prep]
    at += [((k + 0.5) / len(part), n, stage) for n, part in ((1, levels), (2, back)) for k, stage in enumerate(part)]
    return [stage for _, _, stage in sorted(at, key=lambda x: x[:2])]


def scan_order():
    order = []
    for prep, other in (("B", "F"), ("F", "B")):
        levels = "levels now" if prep == "B" else "levels"
        order += among([("prep", prep, name, None) for name in PREP], [(levels, other, x, l) for x, l in LEVEL_STAGES],
                       [("back", prep, k, None) for k in range(len(BACK))])
    return order


def scan(nc, d):
    S2 = {"F": 0, "B": 1}
    with ExitStack() as ctx:
        sb, ps, sem = alloc(ctx, nc)
        ident = sb("sc_ident", [P, P])
        eye = sb("sc_eye", [P, CHUNK])
        tri = sb("sc_tri", [P, 2, P])
        halves = sb("sc_halves", [P, 2])
        gram_mask = sb("sc_gram_mask", [P, 2, 2, CHUNK])
        level_mask = sb("sc_level_mask", [P, 2, LEVELS, CHUNK])
        keep = sb("sc_keep", [P, 3, STEPS])
        k_k = sb("sc_k_k", [P, RW])
        k_a = sb("sc_k_a", [P, RW])
        r_k = sb("sc_r_k", [P, RW])
        up = sb("sc_up", [33, 2, 2, RW])
        neg_half = sb("sc_neg_half", [P, RH])

        rk = sb("sc_rk", [P, 2, 2 * RW])
        lo = sb("sc_lo", [33, 2, 2, P])
        V = sb("sc_V", [P, 2, 2, RW])
        sgm = sb("sc_sgm", [P, RW])
        av = sb("sc_av", [P, RW])
        kkr = sb("sc_kkr", [P, RW])
        sq = sb("sc_sq", [P, RW])
        ssq = sb("sc_ssq", [P, RH])
        inv = sb("sc_inv", [P, RH])
        cx = sb("sc_cx", [P, RW])
        Wd = sb("sc_W", [P, RW])
        Wi = sb("sc_Wi", [P, RW])
        We = sb("sc_We", [P, RW])
        kd = sb("sc_kd", [P, RW])
        Bt = sb("sc_Bt", [P, 2, 2, RW])
        Ct = sb("sc_Ct", [P, 2, 2, RW])
        bonus = sb("sc_bonus", [P, 2, 2, RH])
        WC = sb("sc_WC", [P, 2, 2, 8])
        KRT = sb("sc_KRT", [P, 2, 2, 4, 2, 2, CHUNK])
        BCT = sb("sc_BCT", [P, 2, 4, 2, 2, CHUNK])
        AT = sb("sc_AT", [P, 2, RH, P])
        ET = sb("sc_ET", [P, 2, 2, RH, P])
        FT = sb("sc_FT", [P, 2, 2, RH, P])
        YD = sb("sc_YD", [P, 2, RH, P])
        XTd = sb("sc_XTd", [P, 2, 2, RH, P])
        Y = sb("sc_Y", [P, 2, RW])
        X = sb("sc_X", [P, 2, RW])
        XT = sb("sc_XT", [P, 2, RW])
        DV = sb("sc_DV", [P, 2, 2, RW])
        H = sb("sc_H", [P, 2, 4, P])
        H_meta = sb("sc_H_meta", [P, 4, P])
        H_add = sb("sc_H_add", [P, 4, P])
        U1 = sb("sc_U1", [P, 2, RW])
        U = sb("sc_U", [P, 2, RW])
        RHt = sb("sc_RH", [P, 2, RW])
        out = sb("sc_out", [P, 2, RW + RH])
        bank = ps("sc_bank", [P, 8, 512])

        const_loaded = sem("sc_const")
        zeroed = sem("sc_zeroed")
        ones_made = sem("sc_ones_made")
        in_loaded = [sem("sc_in0"), sem("sc_in1")]
        v_loaded = [[sem(f"sc_v{s}{p}") for p in range(2)] for s in range(2)]
        meta_loaded = sem("sc_meta_loaded")
        full = [[sem(f"sc_full{s}{b}") for b in range(3)] for s in range(2)]
        free = [[sem(f"sc_free{s}{b}") for b in range(3)] for s in range(2)]
        bd = [sem("sc_bd0"), sem("sc_bd1")]
        first_x = [sem("sc_first_x0"), sem("sc_first_x1")]
        first_xt = [sem("sc_first_xt0"), sem("sc_first_xt1")]
        sg_raw = sem("sc_sg_raw")
        a_raw = sem("sc_a_raw")
        sg_ok = sem("sc_sg_ok")
        a_ok = sem("sc_a_ok")
        kk_raw = sem("sc_kk_raw")
        sq_ok = sem("sc_sq_ok")
        ssq_ok = sem("sc_ssq_ok")
        inv_ok = sem("sc_inv_ok")
        kk_ok = sem("sc_kk_ok")
        cx_ok = sem("sc_cx_ok")
        w_ok = sem("sc_w_ok")
        kd_ok = sem("sc_kd_ok")
        bb_ok = sem("sc_bb_ok")
        tilde = sem("sc_tilde")
        bonus_pre = sem("sc_bonus_pre")
        bonus_ok = sem("sc_bonus_ok")
        bonus_half = sem("sc_bonus_half")
        bfull = [sem("sc_bfull0"), sem("sc_bfull1")]
        bvec = [sem("sc_bvec0"), sem("sc_bvec1")]
        rh_ok = [sem("sc_rh0"), sem("sc_rh1")]
        m_full = sem("sc_m_full")
        m_vec = sem("sc_m_vec")
        out_stored = [sem("sc_out0"), sem("sc_out1")]
        vec = sem("sc_vec")
        sp_passed = sem("sc_sp_passed")
        pe_passed = sem("sc_pe_passed")

        heads = lambda ap, c=HEAD: ap.rearrange("p (h c) -> p h c", c=c)
        half = lambda c: slice(c * CHUNK, (c + 1) * CHUNK)

        class Step:

            def __init__(self, s, g, par, turn=0):
                self.s, self.g, self.par, self.turn = s, g, par, turn
                self.n = g + 1 if s == 0 else g
                self.q = 2 * g + 2 - s

            def full(self, slot):
                return self.n * PER_BANK[slot % 3] + slot // 3 + 1

            def taken(self, slot):
                return self.n * PER_BANK[slot % 3] + slot // 3 + 1

            def before(self, slot):
                return self.n * PER_BANK[slot % 3] + slot // 3

            def bank(self, slot):
                return 3 * self.s + slot % 3

        def inputs_in(eng, st):
            if isinstance(st.q, int) and st.q == 0:
                eng.wait_ge(meta_loaded, 16 * 8)
            else:
                eng.wait_ge(in_loaded[st.s], 16 * 3 * (st.g + 1))

        PER_FRONT_BD = 2 * LEVELS - 1

        def order(c, s):
            return c if s == 0 else 1 - c

        def window(front, back, g, q, i, last=False):
            for kind, stream, name, level in scan_order():
                s = S2[stream]
                if kind == "back":
                    back(Step(s, g, (q + 1) % 2), name)
                elif kind == "levels now":
                    front(Step(s, g, (q + 1) % 2), name, level)
                elif not last:
                    front(Step(s, g + 1, q, i + q + 1), name, level)

        def program(eng, front, back, meta, enter=lambda *a: None):
            def both(preps, levels):
                for st, *stage in among([(preps, name) for name in PREP], [(levels, x, l) for x, l in LEVEL_STAGES]):
                    front(st, *stage)

            enter(None)
            tokens, first_f, first_b = Step(0, -1, 0), Step(0, 0, 1, 1), Step(1, 0, 1, 1)
            for name in PREP:
                front(tokens, name)
            both(first_b, tokens)
            meta()
            both(first_f, first_b)

            def pair(i):
                for q in range(2):
                    enter(2 * i + q)
                    window(front, back, 2 * i + q, q, i)

            pair(0)
            with eng.Fori(1, STEPS // 2 - 1) as i:
                pair(i)
            enter(STEPS - 2)
            window(front, back, STEPS - 2, 0, STEPS // 2 - 1)
            enter(STEPS - 1)
            window(front, back, STEPS - 1, 1, STEPS // 2 - 1, last=True)

        with nc.Block() as block:
            @block.sync
            def _(sp):
                consts = [(ident[:, :], d["ident"]), (eye[:, :], d["eye"]), (tri[:, :, :], d["tri"]), (halves[:, :], d["halves"]),
                          (gram_mask[:, :, :, :], d["gram_mask"]), (level_mask[:, :, :, :], d["level_mask"]), (keep[:, :, :], d["keep"]),
                          (k_k[:, :], d["k_k"].partition_broadcast(P)), (k_a[:, :], d["k_a"].partition_broadcast(P)),
                          (r_k[:, :], d["r_k"].partition_broadcast(P)), (up[:, :, :, :], d["lora_up"])]
                for to, of in consts:
                    sp.dma_start(to, of).then_inc(const_loaded, 16)
                sp.wait_ge(zeroed, 3)
                for c in range(2):
                    rows = slice(c * CHUNK + CHUNK - N_META, (c + 1) * CHUNK)
                    at = T_REAL + c * N_META
                    sp.dma_start(rk[rows, 0, :], d["rkv"][at:at + N_META, 0:2 * RW]).then_inc(meta_loaded, 16)
                    for x in range(2):
                        sp.dma_start(lo[0:32, 0, x, rows], d["lora"][32 * x:32 * x + 32, at:at + N_META]).then_inc(meta_loaded, 16)
                    sp.dma_start(V[rows, 0, 0, :], d["rkv"][at:at + N_META, 2 * RW:3 * RW]).then_inc(meta_loaded, 16)

                def load(g, par, s):
                    st = Step(s, g, par)
                    t = g if s == 0 else STEPS - 1 - g
                    if not (isinstance(g, int) and g == 0 and s == 1):
                        q = st.q - 2
                        hold(sp, bonus_pre, q + 1, sp_passed)
                        hold(sp, tilde, 4 * (q + 1), sp_passed)
                    sp.dma_start(rk[:, s, :], d["rkv"][bass.ds(t * P, P), 0:2 * RW]).then_inc(in_loaded[s], 16)
                    for x in range(2):
                        sp.dma_start(lo[0:32, s, x, :], d["lora"][32 * x:32 * x + 32, bass.ds(t * P, P)]).then_inc(in_loaded[s], 16)
                    hold(sp, bfull[s], 7 * (g - 1), sp_passed)
                    sp.dma_start(V[:, s, par, :], d["rkv"][bass.ds(t * P, P), 2 * RW:3 * RW]).then_inc(v_loaded[s][par], 16)

                def store(g, s):
                    t = g if s == 0 else STEPS - 1 - g
                    hold(sp, bvec[s], 7 * (g + 1), sp_passed)
                    sp.dma_start(d["scan"][s, bass.ds(t * P, P), :], out[:, s, :]).then_inc(out_stored[s], 16)

                load(0, 1, 1)
                load(0, 1, 0)
                for s in range(2):
                    load(1, 0, s)
                with sp.Fori(1, STEPS // 2) as i:
                    for q in range(2):
                        for s in (1, 0):
                            load(2 * i + q, (q + 1) % 2, s)
                            store(2 * i + q - 2, s)
                for g in (STEPS - 2, STEPS - 1):
                    for s in range(2):
                        store(g, s)
                for s in range(2):
                    sp.wait_ge(out_stored[s], 16 * STEPS)

            @block.gpsimd
            def _(pool):
                for part in (rk[:, 0, :], V[:, 0, 0, :], lo[0:32, 0, :, :]):
                    nc.gpsimd.memset(part, 0.0).then_inc(zeroed, 1)
                pool.wait_ge(zeroed, 3)
                nc.gpsimd.memset(lo[32:33, :, :, :], 1.0).then_inc(ones_made, 1)
                pool.wait_ge(ones_made, 1)
                nc.gpsimd.memset(neg_half[:, :], -0.5)
                for part in (AT[:, :, :, :], YD[:, :, :, :], H[:, :, :, :], H_meta[:, :, :]):
                    nc.gpsimd.memset(part, 0.0)
                for p in range(2):
                    for t in (ET, FT, XTd):
                        nc.gpsimd.memset(t[:, :, p], 0.0)
                nc.gpsimd.memset(out[:, :, RW:RW + RH], 0.0).then_inc(zeroed, 1)
                pool.wait_ge(zeroed, 4)
                pool.wait_ge(const_loaded, 16 * 11)

                def front(st, name, level=None):
                    s, q = st.s, st.q
                    if name == "logits":
                        inputs_in(pool, st)
                        wait(pool, tilde, 4 * q - 3)
                        wait(pool, bb_ok, q)
                        nc.gpsimd.tensor_tensor(kkr[:, :], rk[:, s, RW:2 * RW], k_k[:, :], ALU.mult).then_inc(kk_raw, 1)
                    if name == "decay":
                        pool.wait_ge(ssq_ok, q + 1)
                        nc.gpsimd.tensor_tensor(inv[:, :], ssq[:, :], neg_half[:, :], ALU.pow).then_inc(inv_ok, 1)
                    if name == "keys":
                        pool.wait_ge(inv_ok, q + 1)
                        pool.wait_ge(sq_ok, q + 1)
                        nc.gpsimd.tensor_tensor(heads(kkr[:, :]), heads(kkr[:, :]), inv[:, :].unsqueeze(2).broadcast_to([P, RH, HEAD]),
                                                ALU.mult).then_inc(kk_ok, 1)
                        pool.wait_ge(kd_ok, q + 1)
                        pool.wait_ge(kk_ok, q + 1)
                        nc.gpsimd.tensor_tensor(av[:, :], kkr[:, :], av[:, :], ALU.mult).then_inc(bb_ok, 1)
                    if name == "tilde":
                        nc.gpsimd.tensor_tensor(sq[:, :], rk[:, s, 0:RW], kd[:, :], ALU.mult).then_inc(bonus_half, 1)
                        pool.wait_ge(bonus_half, q + 1)
                        nc.gpsimd.tensor_tensor(sq[:, :], sq[:, :], r_k[:, :], ALU.mult).then_inc(bonus_pre, 1)

                    if name == "dv":
                        wait(pool, bd[s], PER_FRONT_BD * st.n)
                        pool.wait_ge(free[s][(GRAM + 3) % 3], st.taken(GRAM + 3))
                        for c in range(2):
                            nc.gpsimd.tensor_tensor(heads(XT[half(c), s, :]), AT[half(c), s, :, half(c)],
                                                    level_mask[half(c), 1 - s, 0:1, :].broadcast_to([CHUNK, RH, CHUNK]), ALU.mult).then_inc(first_xt[s], 1)
                            pool.wait_ge(first_xt[s], 3 * st.n + 1 + c)
                        nc.gpsimd.tensor_tensor(heads(XT[:, s, :]), heads(XT[:, s, :]),
                                                eye[:, :].unsqueeze(1).broadcast_to([P, RH, CHUNK]), ALU.add).then_inc(first_xt[s], 1)

                program(pool, front, lambda st, k: None, lambda: None)

            @block.scalar
            def _(act):
                act.wait_ge(const_loaded, 16 * 11)
                act.wait_ge(zeroed, 4)

                def front(st, name, level=None):
                    s, q, par = st.s, st.q, st.par

                    def take(slot, ins=None):
                        act.wait_ge(full[s][slot % 3], st.full(slot))

                    def copy(slot, to, func=ACT.Copy, scale=1.0, cols=slice(0, 512)):
                        take(slot)
                        nc.scalar.activation(to, bank[:, st.bank(slot), cols], func, scale=scale).then_inc(free[s][slot % 3], 1)

                    if name == "logits":
                        wait(act, cx_ok, q)
                        take(W_LOGIT)
                        nc.scalar.activation(sgm[:, :], bank[:, st.bank(W_LOGIT), :], ACT.Tanh, scale=0.5).then_inc(free[s][0], 1)
                        wait(act, tilde, 4 * q)
                        take(A_LOGIT)
                        nc.scalar.activation(av[:, :], bank[:, st.bank(A_LOGIT), :], ACT.Tanh, scale=0.5).then_inc(free[s][1], 1)
                    if name == "gates":
                        act.wait_ge(kk_raw, q + 1)
                        wait(act, bonus_ok, q)
                        nc.scalar.activation(sq[:, :], kkr[:, :], ACT.Square).then_inc(sq_ok, 1)
                    if name == "decay":
                        act.wait_ge(cx_ok, q + 1)
                        wait(act, tilde, 4 * q)
                        b = bank[:, st.bank(CUM), :]
                        take(CUM)
                        nc.scalar.activation(Wi[:, :], b, ACT.Exp, scale=DECAY)
                        nc.scalar.activation(Wd[:, :], b, ACT.Exp, scale=-DECAY).then_inc(free[s][2], 1)
                        nc.scalar.activation(We[:, :], cx[:, :], ACT.Exp, scale=-DECAY).then_inc(w_ok, 1)
                        take(CHUNK_SUM)
                        nc.scalar.activation(WC[:, s, par, :], bank[:, st.bank(CHUNK_SUM), 0:8], ACT.Exp, scale=-DECAY).then_inc(free[s][0], 1)
                    if name in ("turn0", "turn1"):
                        for slot in (T_K, T_R) if name == "turn0" else (T_B, T_D):
                            x = (slot - T_K) % 2
                            to = KRT[:, s, par, :, :, x, :] if slot < T_B else BCT[:, s, :, :, x, :]
                            take(slot)
                            nc.scalar.activation(to.rearrange("p j c t -> p (j c) t"), heads(bank[:, st.bank(slot), :]), ACT.Copy).then_inc(free[s][slot % 3], 1)
                    if name == "dv":
                        copy(D_V, DV[:, s, par, :])
                    if name == "y" and level:
                        slot = Y_SLOT[level]
                        act.wait_ge(free[s][slot % 3], st.taken(slot))
                        for c in range(2):
                            last = nc.scalar.activation(YD[half(c), s, :, half(c)], heads(Y[half(c), s, :]), ACT.Copy)
                        last.then_inc(bd[s], 1)
                    if name == "t":
                        slot = XT_SLOT[level]
                        if level:
                            act.wait_ge(free[s][slot % 3], st.taken(slot))
                        else:
                            act.wait_ge(first_xt[s], 3 * st.n + 3)
                        for c in range(2):
                            last = nc.scalar.activation(XTd[half(c), s, par, :, half(c)], heads(XT[half(c), s, :]), ACT.Copy)
                        last.then_inc(bd[s], 1)

                def back(st, k):
                    if k not in (0, 3):
                        return
                    s = st.s
                    act.wait_ge(bfull[s], 7 * st.g + k + 1)
                    wait(act, bvec[s], 7 * st.g)
                    c = order(k // 3, s)
                    nc.scalar.activation(RHt[half(c), s, :], bank[64:128, 6 + s, :], ACT.Copy).then_inc(rh_ok[s], 1)

                program(act, front, back, lambda: None)

            @block.vector
            def _(dve):
                dve.wait_ge(const_loaded, 16 * 11)
                dve.wait_ge(zeroed, 4)
                step = Tally(vec)

                def then(ins):
                    dve.wait_ge(vec, step.inc(ins))

                def front(st, name, level=None):
                    s, q, par = st.s, st.q, st.par

                    def take(slot):
                        dve.wait_ge(full[s][slot % 3], st.full(slot))
                        return bank[:, st.bank(slot), :]

                    def freed(slot, ins):
                        ins.then_inc(free[s][slot % 3], 1)

                    if name == "sums":
                        dve.wait_ge(sq_ok, q + 1)
                        wait(dve, inv_ok, q)
                        then(nc.vector.tensor_reduce(ssq[:, :], heads(sq[:, :]), AX.X, ALU.add))
                        nc.vector.tensor_scalar(ssq[:, :], ssq[:, :], 1e-24, None, ALU.max).then_inc(ssq_ok, 1)
                    if name == "gates":
                        dve.wait_ge(free[s][0], st.taken(W_LOGIT))
                        nc.vector.tensor_scalar(sgm[:, :], sgm[:, :], 0.5, 0.5, ALU.mult, ALU.add).then_inc(sg_ok, 1)
                        dve.wait_ge(free[s][1], st.taken(A_LOGIT))
                        nc.vector.tensor_scalar(av[:, :], av[:, :], 0.5, 0.5, ALU.mult, ALU.add).then_inc(a_ok, 1)
                    if name == "decay":
                        b = take(CUM)
                        wait(dve, w_ok, q)
                        dve.wait_ge(sg_ok, q + 1)
                        nc.vector.tensor_tensor(cx[:, :], b, sgm[:, :], ALU.subtract).then_inc(cx_ok, 1)
                        dve.wait_ge(a_ok, q + 1)
                        wait(dve, bonus_pre, q)
                        inputs_in(dve, st)
                        then(nc.vector.scalar_tensor_tensor(out=kd[:, :], in0=av[:, :], scalar=1.0, in1=k_a[:, :], op0=ALU.subtract, op1=ALU.mult))
                        nc.vector.scalar_tensor_tensor(out=kd[:, :], in0=kd[:, :], scalar=1.0, in1=rk[:, s, RW:2 * RW],
                                                       op0=ALU.add, op1=ALU.mult).then_inc(kd_ok, 1)
                    if name == "tilde":
                        dve.wait_ge(w_ok, q + 1)
                        dve.wait_ge(kk_ok, q + 1)
                        nc.vector.scalar_tensor_tensor(out=We[:, :], in0=kkr[:, :], scalar=-1.0, in1=We[:, :],
                                                       op0=ALU.mult, op1=ALU.mult).then_inc(tilde, 1)
                        nc.vector.tensor_tensor(Wd[:, :], rk[:, s, 0:RW], Wd[:, :], ALU.mult).then_inc(tilde, 1)
                        dve.wait_ge(bb_ok, q + 1)
                        nc.vector.tensor_tensor(Bt[:, s, par, :], av[:, :], Wi[:, :], ALU.mult).then_inc(tilde, 1)
                        dve.wait_ge(kd_ok, q + 1)
                        nc.vector.tensor_tensor(Ct[:, s, par, :], kd[:, :], Wi[:, :], ALU.mult).then_inc(tilde, 1)
                    if name == "turn1":
                        dve.wait_ge(bonus_pre, q + 1)
                        nc.vector.tensor_reduce(bonus[:, s, par, :], heads(sq[:, :]), AX.X, ALU.add).then_inc(bonus_ok, 1)
                    if name[:4] == "gram":
                        x = int(name[4])
                        c, e = x // 2, x % 2
                        b = take(GRAM + x)
                        for r, (to_a, to_e) in enumerate(((AT[:, s], ET[:, s, par]), (YD[:, s], FT[:, s, par]))):
                            part = b[half(r), :].rearrange("p (j x t) -> p j x t", j=4, x=2)
                            for y, to in enumerate((to_a, to_e)):
                                last = nc.vector.tensor_tensor(
                                    to[half(c), :, half(c)].rearrange("p (j e) t -> p j e t", e=2)[:, :, e, :], part[:, :, y, :],
                                    gram_mask[half(r), s, y:y + 1, :].broadcast_to([CHUNK, 4, CHUNK]), ALU.mult)
                        freed(GRAM + x, last)
                    if name == "y":
                        slot = Y_SLOT[level]
                        b = take(slot)
                        freed(slot, nc.vector.tensor_tensor(heads(Y[:, s, :]), heads(b),
                                                            level_mask[:, s, level:level + 1, :].broadcast_to([P, RH, CHUNK]), ALU.mult))
                        if level == 0:
                            dve.wait_ge(free[s][slot % 3], st.taken(slot))
                            nc.vector.tensor_tensor(heads(X[:, s, :]), heads(Y[:, s, :]),
                                                    eye[:, :].unsqueeze(1).broadcast_to([P, RH, CHUNK]), ALU.add).then_inc(first_x[s], 1)
                    if name == "x":
                        slot = X_SLOT[level]
                        b = take(slot)
                        freed(slot, nc.vector.tensor_tensor(X[:, s, :], b, X[:, s, :], ALU.add))
                    if name == "t" and level:
                        slot = XT_SLOT[level]
                        b = take(slot)
                        freed(slot, nc.vector.tensor_tensor(XT[:, s, :], b, XT[:, s, :], ALU.add))

                def back(st, k):
                    s, g, par = st.s, st.g, st.par
                    b = bank[:, 6 + s, :]
                    base = 7 * g
                    c = order(k // 3, s)
                    dve.wait_ge(bfull[s], base + k + 1)
                    if k in (0, 3):
                        dve.wait_ge(free[s][D_V % 3], st.taken(D_V))
                        nc.vector.tensor_tensor(U1[half(c), s, :], b[0:CHUNK, :], DV[half(c), s, par, :], ALU.add).then_inc(bvec[s], 1)
                    elif k in (1, 4):
                        nc.vector.tensor_copy(U[half(c), s, :], b[half(c), :]).then_inc(bvec[s], 1)
                    elif k in (2, 5):
                        for e in range(2):
                            h = H[half(e), s, :, half(e)]
                            last = nc.vector.tensor_tensor(h, b[half(e), :].rearrange("p (j c) -> p j c", j=4)[:, :, half(e)], h, ALU.add)
                        then(last)
                        for e in range(2):
                            h = H[half(e), s, :, half(e)]
                            w = WC[half(e), s, par, :].rearrange("p (j c) -> p j c", c=2)[:, :, c:c + 1].broadcast_to([CHUNK, 4, CHUNK])
                            last = nc.vector.tensor_tensor(h, h, w, ALU.mult)
                        if k == 2:
                            last.then_inc(bvec[s], 1)
                        else:
                            then(last)
                            if s == 0:
                                then(nc.vector.tensor_scalar(H_add[:, :, :], H_meta[:, :, :], keep[:, 2, bass.ds(g, 1)], None, ALU.mult))
                                nc.vector.scalar_tensor_tensor(out=H[:, s].rearrange("p j c -> p (j c)"), in0=H[:, s].rearrange("p j c -> p (j c)"),
                                                               scalar=keep[:, 0, bass.ds(g, 1)], in1=H_add[:, :, :].rearrange("p j c -> p (j c)"),
                                                               op0=ALU.mult, op1=ALU.add).then_inc(bvec[s], 1)
                            else:
                                nc.vector.tensor_scalar(H[:, s], H[:, s], keep[:, 1, bass.ds(g, 1)], None, ALU.mult).then_inc(bvec[s], 1)
                    else:
                        dve.wait_ge(rh_ok[s], 2 * g + 2)
                        wait(dve, out_stored[s], 16 * g)
                        nc.vector.tensor_copy(out[:, s, RW:RW + RH], bonus[:, s, par, :])
                        nc.vector.tensor_tensor(out[:, s, 0:RW], b, RHt[:, s, :], ALU.add).then_inc(bvec[s], 1)

                def meta():
                    b = bank[:, 6, :]
                    dve.wait_ge(m_full, 1)
                    nc.vector.tensor_copy(U[half(0), 0, :], b[half(0), :]).then_inc(m_vec, 1)
                    dve.wait_ge(m_full, 2)
                    nc.vector.tensor_copy(U[half(1), 0, :], bank[half(1), 7, :]).then_inc(m_vec, 1)
                    for c, to in enumerate((H[:, 0], H_meta)):
                        dve.wait_ge(m_full, 3 + c)
                        for e in range(2):
                            w = WC[half(e), 0, 0, :].rearrange("p (j c) -> p j c", c=2)[:, :, c:c + 1].broadcast_to([CHUNK, 4, CHUNK])
                            last = nc.vector.tensor_tensor(to[half(e), :, half(e)], bank[half(e), 6 + c, :].rearrange("p (j c) -> p j c", j=4)[:, :, half(e)],
                                                           w, ALU.mult)
                        last.then_inc(m_vec, 1)

                PER_PREP = 2
                PER_WINDOW = 2 * PER_PREP + 2 * 1 + 2 * 2 + 1

                def enter(g):
                    if g is not None:
                        step.enter(3 * PER_PREP + g * PER_WINDOW)

                program(dve, front, back, meta, enter)

            @block.tensor
            def _(pe):
                pe.wait_ge(const_loaded, 16 * 11)
                pe.wait_ge(zeroed, 4)

                def front(st, name, level=None):
                    s, q, par = st.s, st.q, st.par

                    def claim(slot):
                        wait(pe, free[s][slot % 3], st.before(slot))
                        return bank[:, st.bank(slot), :]

                    def fill(slot, ins):
                        ins.then_inc(full[s][slot % 3], 1)

                    def need(slot):
                        pe.wait_ge(free[s][slot % 3], st.taken(slot))

                    if name == "logits":
                        inputs_in(pe, st)
                        for x, slot in enumerate((W_LOGIT, A_LOGIT)):
                            b = claim(slot)
                            fill(slot, nc.tensor.matmul(b, lo[0:33, s, x, :], up[0:33, s, x, :], start=True, stop=True))
                    if name == "sums":
                        pe.wait_ge(sg_ok, q + 1)
                        b = claim(CUM)
                        fill(CUM, nc.tensor.matmul(b, tri[:, s, :], sgm[:, :], start=True, stop=True))
                        b = claim(CHUNK_SUM)
                        for j in range(4):
                            last = nc.tensor.matmul(b[:, 2 * j:2 * j + 2], sgm[:, j * P:(j + 1) * P], halves[:, :], start=True, stop=True)
                        fill(CHUNK_SUM, last)
                    if name in ("turn0", "turn1"):
                        tildes = ((0, T_K, We[:, :]), (1, T_R, Wd[:, :]), (2, T_B, Bt[:, s, par, :]), (3, T_D, Ct[:, s, par, :]))
                        for n, slot, x in tildes[:2] if name == "turn0" else tildes[2:]:
                            pe.wait_ge(tilde, 4 * q + n + 1)
                            b = claim(slot)
                            for j in range(4):
                                last = nc.tensor.transpose(b[:, j * P:(j + 1) * P], x[:, j * P:(j + 1) * P], ident[:, :])
                            fill(slot, last)
                    if name[:4] == "gram":
                        if name == "gram0":
                            need(T_D)
                            need(T_B)
                            need(T_R)
                        x = int(name[4])
                        c, e = x // 2, x % 2
                        b = claim(GRAM + x)
                        for j in range(4):
                            last = nc.tensor.matmul(b[:, j * P:(j + 1) * P], BCT[half(e), s, j, c].rearrange("p x t -> p (x t)"),
                                                    KRT[half(e), s, par, j, c].rearrange("p x t -> p (x t)"), start=True, stop=True)
                        fill(GRAM + x, last)
                    if name == "dv":
                        need(GRAM + 3)
                        if not (isinstance(st.q, int) and st.q == 0):
                            pe.wait_ge(v_loaded[s][par], 16 * st.turn)
                        b = claim(D_V)
                        for h in range(RH):
                            for c in range(2):
                                last = nc.tensor.matmul(b[half(c), half(h)], YD[:, s, h, half(c)], V[:, s, par, half(h)], start=True, stop=True)
                        fill(D_V, last)

                    def product(slot, lhsT, rhs):
                        b = claim(slot)
                        for h in range(RH):
                            for c in range(2):
                                last = nc.tensor.matmul(b[half(c), half(h)], lhsT[:, h, half(c)], rhs(h), start=True, stop=True)
                        fill(slot, last)

                    n = PER_FRONT_BD * st.n
                    if name == "y":
                        if level == 0:
                            product(Y_SLOT[0], AT[:, s], lambda h: eye[:, :])
                        else:
                            if level == 1:
                                pe.wait_ge(first_x[s], st.n + 1)
                            else:
                                need(X_SLOT[level - 1])
                            product(Y_SLOT[level], AT[:, s], lambda h: X[:, s, half(h)])
                    if name == "x":
                        need(Y_SLOT[level])
                        pe.wait_ge(bd[s], n + 2 * level - 1)
                        product(X_SLOT[level], XTd[:, s, par], lambda h: Y[:, s, half(h)])
                    if name == "t" and level:
                        need(Y_SLOT[level])
                        pe.wait_ge(bd[s], n + 2 * level)
                        if level == 1:
                            pe.wait_ge(first_xt[s], 3 * st.n + 3)
                        else:
                            need(XT_SLOT[level - 1])
                        product(XT_SLOT[level], YD[:, s], lambda h: XT[:, s, half(h)])

                def back(st, k):
                    s, g, par = st.s, st.g, st.par
                    b = bank[:, 6 + s, :]
                    base = 7 * g
                    c = order(k // 3, s)
                    wait(pe, bvec[s], base + k)
                    if k in (0, 3):
                        for j in range(4):
                            last = nc.tensor.matmul(b[:, j * P:(j + 1) * P], KRT[:, s, par, j, c].rearrange("p x t -> p (x t)"), H[:, s, j, :],
                                                    start=True, stop=True)
                    elif k in (1, 4):
                        pe.wait_ge(rh_ok[s], 2 * g + k // 3 + 1)
                        hold(pe, bd[s], PER_FRONT_BD * (st.n + 1), pe_passed)
                        for h in range(RH):
                            last = nc.tensor.matmul(b[half(c), half(h)], XTd[half(c), s, par, h, half(c)], U1[half(c), s, half(h)], start=True, stop=True)
                    elif k in (2, 5):
                        for j in range(4):
                            cols = slice(j * P, (j + 1) * P)
                            nc.tensor.matmul(b[:, cols], Bt[half(c), s, par, cols], U[half(c), s, cols], start=True, stop=False)
                            last = nc.tensor.matmul(b[:, cols], Ct[half(c), s, par, cols], V[half(c), s, par, cols], start=False, stop=True)
                    else:
                        for h in range(RH):
                            for x in range(2):
                                nc.tensor.matmul(b[half(x), half(h)], ET[:, s, par, h, half(x)], U[:, s, half(h)], start=True, stop=False)
                                last = nc.tensor.matmul(b[half(x), half(h)], FT[:, s, par, h, half(x)], V[:, s, par, half(h)], start=False, stop=True)
                    last.then_inc(bfull[s], 1)

                def meta():
                    pe.wait_ge(bd[0], PER_FRONT_BD)
                    pe.wait_ge(free[0][D_V % 3], Step(0, -1, 0).taken(D_V))
                    for c in range(2):
                        for h in range(RH):
                            last = nc.tensor.matmul(bank[half(c), 6 + c, half(h)], XTd[half(c), 0, 0, h, half(c)], DV[half(c), 0, 0, half(h)],
                                                    start=True, stop=True)
                        last.then_inc(m_full, 1)
                    for c in range(2):
                        pe.wait_ge(m_vec, 2)
                        for j in range(4):
                            cols = slice(j * P, (j + 1) * P)
                            nc.tensor.matmul(bank[:, 6 + c, cols], Bt[half(c), 0, 0, cols], U[half(c), 0, cols], start=True, stop=False)
                            last = nc.tensor.matmul(bank[:, 6 + c, cols], Ct[half(c), 0, 0, cols], V[half(c), 0, 0, cols], start=False, stop=True)
                        last.then_inc(m_full, 1)
                    pe.wait_ge(m_vec, 4)

                program(pe, front, back, meta)


def mixout(nc, d):
    W_SLOTS = 4
    with ExitStack() as ctx:
        sb, ps, sem = alloc(ctx, nc)
        ident = sb("mo_ident", [P, P])
        gn_g = sb("mo_gn_g", [P, RW])
        gn_b = sb("mo_gn_b", [P, RW])
        gain = sb("mo_gain", [P, D])
        bias = sb("mo_bias", [P, D])
        gate_up = sb("mo_gate_up", [P, RW])
        neg_half = sb("mo_neg_half", [P, RH])
        w_in = sb("mo_w", [P, W_SLOTS, D])
        w_hi = sb("mo_w_hi", [P, KT, D], F32R)
        w_lo = sb("mo_w_lo", [P, KT, D], F32R)
        sc = sb("mo_sc", [P, 2, 2, RW + RH])
        v = sb("mo_v", [P, 2, RW])
        gate = sb("mo_gate", [P, 2, P])
        mix = sb("mo_mix", [P, 2, D])
        h = sb("mo_h", [P, 2, D])
        o = sb("mo_o", [P, RW + RH])
        square = sb("mo_square", [P, RW])
        vb = sb("mo_vb", [P, RW])
        mean = sb("mo_mean", [P, RH])
        var = sb("mo_var", [P, RH])
        rstd = sb("mo_rstd", [P, RH])
        m_hi = sb("mo_m_hi", [P, 2, KT, P], F32R)
        m_lo = sb("mo_m_lo", [P, 2, KT, P], F32R)
        x = sb("mo_x", [P, 2, D])
        stats = sb("mo_stats", [P, 12])
        mv = sb("mo_mv", [P, 2])
        l_rstd = sb("mo_l_rstd", [P, 1])
        nmr = sb("mo_nmr", [P, 1])
        G = ps("mo_G", [P, 512])
        tp = ps("mo_tp", [P, 2, 512])
        mm = ps("mo_mm", [P, 2, 2, 512])
        const_loaded = sem("mo_const")
        half_made = sem("mo_half_made")
        w_loaded = [sem(f"mo_w{k}") for k in range(W_SLOTS)]
        w_hi_done = sem("mo_w_hi_done")
        w_lo_done = sem("mo_w_lo_done")
        in_loaded = [sem("mo_in0"), sem("mo_in1")]
        h_loaded = [sem("mo_h0"), sem("mo_h1")]
        centred = sem("mo_centred")
        squared = sem("mo_squared")
        var_done = sem("mo_var_done")
        rstd_done = sem("mo_rstd_done")
        scaled = sem("mo_scaled")
        pool_step = sem("mo_pool_step")
        o_done = sem("mo_o_done")
        gate_done = sem("mo_gate_done")
        mix_done = sem("mo_mix_done")
        tp_done = sem("mo_tp_done")
        hi_done = sem("mo_hi_done")
        lo_done = sem("mo_lo_done")
        product_done = sem("mo_product_done")
        res_done = sem("mo_res_done")
        l_var_done = sem("mo_l_var_done")
        l_rstd_done = sem("mo_l_rstd_done")
        nmr_done = sem("mo_nmr_done")
        normed = sem("mo_normed")
        gained = sem("mo_gained")
        x_done = sem("mo_x_done")
        x_stored = [sem("mo_x0"), sem("mo_x1")]
        vec = sem("mo_vec")
        passed = sem("mo_passed")
        sp_passed = sem("mo_sp_passed")
        heads = lambda ap: ap.rearrange("p (h c) -> p h c", c=HEAD)
        spread = lambda ap: ap.unsqueeze(2).broadcast_to([P, RH, HEAD])

        def program(combine=None, turn=None, product=None, finish=None, enter=lambda t: None):
            def stages(t, at):
                enter(t)
                known = isinstance(t, int)
                for stage, ahead, k in ((product, 0, None), (combine, 3, 0), (finish, -1, 0), (combine, 3, 1), (finish, -1, 1),
                                        (combine, 3, 2), (finish, -1, 2), (combine, 3, 3), (turn, 2, None)):
                    if stage and not (known and not 0 <= t + ahead < NT):
                        tile, q, i = at(ahead)
                        stage(tile, q, i, *(() if k is None else (k,)))

            def fixed(t):
                stages(t, lambda ahead: (t + ahead, (t + ahead) % 2, (t + ahead) // 2))

            def body(i):
                for p in range(2):
                    stages(2 * i + p, lambda ahead: (2 * i + p + ahead, (p + ahead) % 2, i + (p + ahead) // 2))

            return fixed, body

        FIRST, LAST = 4, NT - 4

        def split_before(t):
            return range((t + 2) * 3, min((t + 3) * 3, KT)) if isinstance(t, int) and -2 <= t <= 0 else ()

        def run(eng, **kinds):
            fixed, body = program(**kinds)
            for t in range(-3, FIRST):
                fixed(t)
            with eng.Fori(FIRST // 2, LAST // 2) as i:
                body(i)
            for t in range(LAST, NT + 1):
                fixed(t)

        with nc.Block() as block:
            @block.sync
            def _(sp):
                for to, of in ((ident[:, :], d["ident"]), (gn_g[:, :], d["gn_g"].partition_broadcast(P)), (gn_b[:, :], d["gn_b"].partition_broadcast(P)),
                               (gain[:, :], d["ln1_g"].partition_broadcast(P)), (bias[:, :], d["ln1_b"].partition_broadcast(P)),
                               (gate_up[64:128, :], d["gate_up"])):
                    sp.dma_start(to, of).then_inc(const_loaded, 16)

                def load(t, q):
                    rows = bass.ds(t * P, P)
                    hold(sp, tp_done, 2 * (t - 1), sp_passed)
                    for z in range(2):
                        sp.dma_start(sc[:, q, z, :], d["scan"][z, rows, :]).then_inc(in_loaded[q], 16)
                    sp.dma_start(v[:, q, :], d["rkv"][rows, 2 * RW:3 * RW]).then_inc(in_loaded[q], 16)
                    sp.dma_start(gate[64:128, q, :], d["lora"][64:128, bass.ds(t * P, P)]).then_inc(in_loaded[q], 16)
                    sp.dma_start(mix[:, q, RW:D], d["mix"][rows, RW:D]).then_inc(in_loaded[q], 16)

                def load_h(t, q):
                    rows = bass.ds(t * P, P)
                    hold(sp, res_done, 2 * (t - 1), sp_passed)
                    sp.dma_start(h[:, q, :], d["h"][rows, :]).then_inc(h_loaded[q], 16)

                def store(t, q):
                    hold(sp, x_done, t + 1, sp_passed)
                    sp.dma_start(d["x1"][bass.ds(t * P, P), :], x[:, q, :]).then_inc(x_stored[q], 16)

                load(0, 0)
                load(1, 1)
                for k in range(KT):
                    wait(sp, w_lo_done, k + 1 - W_SLOTS)
                    sp.dma_start(w_in[:, k % W_SLOTS, :], d["w_out"][k * P:(k + 1) * P, :]).then_inc(w_loaded[k % W_SLOTS], 16)
                for t in range(2):
                    load_h(t, t)
                for t in range(2, 6):
                    load(t, t % 2)
                    if t == 5:
                        load_h(2, 0)
                        store(0, 0)
                with sp.Fori(3, NT // 2) as i:
                    for q in range(2):
                        load(2 * i + q, q)
                        load_h(2 * i + q - 3, 1 - q)
                        store(2 * i + q - 5, 1 - q)
                for t in range(NT, NT + 5):
                    if t < NT + 3:
                        load_h(t - 3, (t - 3) % 2)
                    store(t - 5, (t - 5) % 2)
                for q in range(2):
                    sp.wait_ge(x_stored[q], 16 * (NT // 2))

            @block.gpsimd
            def _(pool):
                nc.gpsimd.memset(neg_half[:, :], -0.5).then_inc(half_made, 1)
                pool.wait_ge(half_made, 1)
                pool.wait_ge(const_loaded, 16 * 6)
                def combine(t, q, i, k):
                    if k == 0:
                        pool.wait_ge(in_loaded[q], 80 * (i + 1))
                        pool.wait_ge(centred, t + 1)
                        nc.gpsimd.tensor_tensor(heads(vb[:, :]), heads(v[:, q, :]), spread(o[:, RW:RW + RH]), ALU.mult).then_inc(pool_step, 1)
                    elif k == 1:
                        pool.wait_ge(var_done, t + 1)
                        nc.gpsimd.tensor_tensor(rstd[:, :], var[:, :], neg_half[:, :], ALU.pow).then_inc(rstd_done, 1)
                        pool.wait_ge(pool_step, 4 * t + 1)
                        nc.gpsimd.tensor_tensor(vb[:, :], vb[:, :], gn_b[:, :], ALU.add).then_inc(pool_step, 1)
                    elif k == 2:
                        pool.wait_ge(scaled, t + 1)
                        nc.gpsimd.tensor_tensor(o[:, 0:RW], o[:, 0:RW], gn_g[:, :], ALU.mult).then_inc(pool_step, 1)
                        pool.wait_ge(pool_step, 4 * t + 3)
                        nc.gpsimd.tensor_tensor(o[:, 0:RW], o[:, 0:RW], vb[:, :], ALU.add).then_inc(pool_step, 1)

                def finish(t, q, i, k):
                    if k == 0:
                        pool.wait_ge(l_var_done, t + 1)
                        nc.gpsimd.tensor_tensor(l_rstd[:, :], mv[:, 1:2], neg_half[:, 0:1], ALU.pow).then_inc(l_rstd_done, 1)
                    elif k == 2:
                        pool.wait_ge(gained, t + 1)
                        nc.gpsimd.tensor_tensor(x[:, q, :], x[:, q, :], bias[:, :], ALU.add).then_inc(x_done, 1)

                run(pool, combine=combine, finish=finish)

            @block.scalar
            def _(act):
                def split(t):
                    for k in split_before(t):
                        act.wait_ge(w_loaded[k % W_SLOTS], 16 * (k // W_SLOTS + 1))
                        nc.scalar.activation(w_hi[:, k, :], w_in[:, k % W_SLOTS, :], ACT.Copy).then_inc(w_hi_done, 1)

                def combine(t, q, i, k):
                    if k == 0:
                        act.wait_ge(centred, t + 1)
                        nc.scalar.activation(square[:, :], o[:, 0:RW], ACT.Square).then_inc(squared, 1)

                def turn(t, q, i):
                    for b in range(2):
                        act.wait_ge(tp_done, 2 * t + b + 1)
                        wait(act, product_done, t - 1)
                        nc.scalar.activation(m_hi[:, q, 4 * b:4 * b + 4, :], tp[:, b, :].rearrange("p (k c) -> p k c", k=4), ACT.Copy).then_inc(hi_done, 1)

                def finish(t, q, i, k):
                    if k == 1:
                        act.wait_ge(nmr_done, t + 1)
                        nc.scalar.activation(x[:, q, :], x[:, q, :], ACT.Identity, bias=nmr[:, :], scale=l_rstd[:, :]).then_inc(normed, 1)

                run(act, combine=combine, turn=turn, finish=finish, enter=split)

            @block.vector
            def _(dve):
                dve.wait_ge(const_loaded, 16 * 6)
                step = Tally(vec)

                def then(ins):
                    dve.wait_ge(vec, step.inc(ins))

                def combine(t, q, i, k):
                    if k == 0:
                        dve.wait_ge(in_loaded[q], 80 * (i + 1))
                        wait(dve, mix_done, t)
                        then(nc.vector.tensor_tensor(o[:, :], sc[:, q, 0, :], sc[:, q, 1, :], ALU.add))
                        then(nc.vector.tensor_reduce(mean[:, :], heads(o[:, 0:RW]), AX.X, ALU.add))
                        nc.vector.scalar_tensor_tensor(out=heads(o[:, 0:RW]), in0=spread(mean[:, :]), scalar=-1.0 / HEAD, in1=heads(o[:, 0:RW]),
                                                       op0=ALU.mult, op1=ALU.add).then_inc(centred, 1)
                    elif k == 1:
                        dve.wait_ge(squared, t + 1)
                        then(nc.vector.tensor_reduce(var[:, :], heads(square[:, :]), AX.X, ALU.add))
                        nc.vector.tensor_scalar(var[:, :], var[:, :], 1.0 / HEAD, GN_EPS, ALU.mult, ALU.add).then_inc(var_done, 1)
                    elif k == 2:
                        dve.wait_ge(rstd_done, t + 1)
                        nc.vector.tensor_tensor(heads(o[:, 0:RW]), heads(o[:, 0:RW]), spread(rstd[:, :]), ALU.mult).then_inc(scaled, 1)
                    else:
                        dve.wait_ge(pool_step, 4 * (t + 1))
                        dve.wait_ge(gate_done, t + 1)
                        wait(dve, tp_done, 2 * (t - 1))
                        nc.vector.tensor_tensor(mix[:, q, 0:RW], G[:, :], o[:, 0:RW], ALU.mult).then_inc(mix_done, 1)

                def turn(t, q, i):
                    for b in range(2):
                        dve.wait_ge(hi_done, 2 * t + b + 1)
                        nc.vector.tensor_tensor(m_lo[:, q, 4 * b:4 * b + 4, :], tp[:, b, :].rearrange("p (k c) -> p k c", k=4),
                                                m_hi[:, q, 4 * b:4 * b + 4, :].bitcast(F32), ALU.subtract).then_inc(lo_done, 1)

                def finish(t, q, i, k):
                    if k == 0:
                        dve.wait_ge(product_done, t + 1)
                        dve.wait_ge(h_loaded[q], 16 * (i + 1))
                        wait(dve, x_stored[q], 16 * i)
                        for b in range(2):
                            cols = slice(b * 512, (b + 1) * 512)
                            nc.vector.scalar_tensor_tensor(out=x[:, q, cols], in0=h[:, q, cols], scalar=ALPHA, in1=mm[:, q, b, :],
                                                           op0=ALU.mult, op1=ALU.add).then_inc(res_done, 1)
                        for b in range(2):
                            cols = slice(b * 512, (b + 1) * 512)
                            dve.wait_ge(res_done, 2 * t + b + 1)
                            last = nc.vector.bn_stats(stats[:, 6 * b:6 * b + 6], x[:, q, cols])
                        step.inc(last)
                        wait(dve, l_rstd_done, t)
                        hold(dve, vec, step.now(), passed)
                        then(nc.vector.bn_aggr(mv[:, :], stats[:, :]))
                        nc.vector.tensor_scalar(mv[:, 1:2], mv[:, 1:2], LN_EPS, None, ALU.add).then_inc(l_var_done, 1)
                    elif k == 1:
                        dve.wait_ge(l_rstd_done, t + 1)
                        wait(dve, normed, t)
                        nc.vector.scalar_tensor_tensor(out=nmr[:, :], in0=mv[:, 0:1], scalar=-1.0, in1=l_rstd[:, :],
                                                       op0=ALU.mult, op1=ALU.mult).then_inc(nmr_done, 1)
                    else:
                        dve.wait_ge(normed, t + 1)
                        nc.vector.tensor_tensor(x[:, q, :], x[:, q, :], gain[:, :], ALU.mult).then_inc(gained, 1)

                COMBINE, FINISH = 3, 2

                def enter(t):
                    for k in split_before(t):
                        dve.wait_ge(w_hi_done, k + 1)
                        nc.vector.tensor_tensor(w_lo[:, k, :], w_in[:, k % W_SLOTS, :], w_hi[:, k, :].bitcast(F32), ALU.subtract).then_inc(w_lo_done, 1)
                    if isinstance(t, int):
                        step.enter(min(t + 3, NT) * COMBINE + max(t - 1, 0) * FINISH)
                    else:
                        step.enter((t + 3) * COMBINE + (t - 1) * FINISH)

                run(dve, combine=combine, turn=turn, finish=finish, enter=enter)

            @block.tensor
            def _(pe):
                pe.wait_ge(const_loaded, 16 * 6)

                def combine(t, q, i, k):
                    if k == 2:
                        pe.wait_ge(in_loaded[q], 80 * (i + 1))
                        wait(pe, mix_done, t)
                        nc.tensor.matmul(G[:, :], gate[64:128, q, :], gate_up[64:128, :], start=True, stop=True).then_inc(gate_done, 1)

                def turn(t, q, i):
                    pe.wait_ge(mix_done, t + 1)
                    wait(pe, lo_done, 2 * t)
                    for b in range(2):
                        for k in range(4):
                            last = nc.tensor.transpose(tp[:, b, k * P:(k + 1) * P], mix[:, q, (4 * b + k) * P:(4 * b + k + 1) * P], ident[:, :])
                        last.then_inc(tp_done, 1)

                def product(t, q, i):
                    if isinstance(t, int) and t == 0:
                        pe.wait_ge(w_lo_done, KT)
                    pe.wait_ge(lo_done, 2 * t + 2)
                    wait(pe, res_done, 2 * (t - 1))
                    for b in range(2):
                        parts = [(m, w, k) for k in range(KT) for m, w in ((m_hi, w_hi), (m_hi, w_lo), (m_lo, w_hi))]
                        for j, (m, w, k) in enumerate(parts):
                            last = nc.tensor.matmul(mm[:, q, b, :], m[:, q, k, :], w[:, k, b * 512:(b + 1) * 512],
                                                    start=(j == 0), stop=(j == len(parts) - 1))
                    last.then_inc(product_done, 1)

                run(pe, combine=combine, turn=turn, product=product)


def ffn(nc, d):
    for part in range(2):
        ffn_part(nc, d, part)


def ffn_part(nc, d, part):
    TILES = NT // 2
    TOK = TILES * P
    GRP = TOK // 2
    FB = D_FF // P
    NAME = f"ff{part}_"
    with ExitStack() as ctx:
        sb, ps, sem = alloc(ctx, nc)
        ident = sb(NAME + "ident", [P, P])
        gain = sb(NAME + "gain", [P, D])
        bias = sb(NAME + "bias", [P, D])
        neg_half = sb(NAME + "neg_half", [P, 1])
        x = sb(NAME + "x", [P, 2, D])
        x_hi = sb(NAME + "x_hi", [P, KT, TOK], F32R)
        x_lo = sb(NAME + "x_lo", [P, KT, TOK], F32R)
        y = sb(NAME + "y", [P, TILES, D])
        w = sb(NAME + "w", [P, 2, 3, D])
        w_hi = sb(NAME + "w_hi", [P, 2, 3, D], F32R)
        w_lo = sb(NAME + "w_lo", [P, 2, 3, D], F32R)
        th = sb(NAME + "th", [P, GRP])
        a = sb(NAME + "a", [P, GRP])
        a_hi = sb(NAME + "a_hi", [P, 2, TOK], F32R)
        a_lo = sb(NAME + "a_lo", [P, 2, TOK], F32R)
        stats = sb(NAME + "stats", [P, TILES, 12])
        mv = sb(NAME + "mv", [P, TILES, 2])
        rstd = sb(NAME + "rstd", [P, TILES])
        nmr = sb(NAME + "nmr", [P, TILES])
        gu = ps(NAME + "gu", [P, 2, 2, 512])
        dn = ps(NAME + "dn", [P, 4, 512])
        const_loaded = sem(NAME + "const")
        half_made = sem(NAME + "half_made")
        x_loaded = [sem(NAME + "x0"), sem(NAME + "x1")]
        tp_done = sem(NAME + "tp_done")
        x_hi_done = sem(NAME + "x_hi_done")
        x_lo_done = sem(NAME + "x_lo_done")
        y_started = sem(NAME + "y_started")
        win_loaded = [sem(NAME + "win0"), sem(NAME + "win1")]
        win_hi_done = sem(NAME + "win_hi_done")
        win_lo_done = sem(NAME + "win_lo_done")
        wout_loaded = [sem(NAME + "wout0"), sem(NAME + "wout1")]
        wout_hi_done = sem(NAME + "wout_hi_done")
        wout_lo_done = sem(NAME + "wout_lo_done")
        gu_done = sem(NAME + "gu_done")
        th_done = sem(NAME + "th_done")
        a_done = sem(NAME + "a_done")
        a_hi_done = sem(NAME + "a_hi_done")
        a_lo_done = sem(NAME + "a_lo_done")
        dn_done = sem(NAME + "dn_done")
        y_added = sem(NAME + "y_added")
        var_done = sem(NAME + "var_done")
        rstd_done = sem(NAME + "rstd_done")
        nmr_done = sem(NAME + "nmr_done")
        normed = sem(NAME + "normed")
        gained = sem(NAME + "gained")
        out_done = sem(NAME + "out_done")
        out_by_vec = sem(NAME + "out_by_vec")
        stored = sem(NAME + "stored")
        vec = sem(NAME + "vec")
        w_view = d["w_ffn_in"].rearrange("(k p) n -> p k n", p=P)
        block3 = lambda ap: ap.rearrange("p (k c) -> p k c", k=KT)
        first_row = part * TOK
        POOL_TILES = [t for t in range(TILES) if t % 2 == 0]

        with nc.Block() as block:
            @block.sync
            def _(sp):
                for to, of in ((ident[:, :], d["ident"]), (gain[:, :], d["ln2_g"].partition_broadcast(P)), (bias[:, :], d["ln2_b"].partition_broadcast(P))):
                    sp.dma_start(to, of).then_inc(const_loaded, 16)

                def weights_in(f, q):
                    wait(sp, win_lo_done, 2 * (f - 1))
                    sp.dma_start(block3(w[:, q, 0, :]), w_view[:, :, bass.ds(f * P, P)]).then_inc(win_loaded[q], 16)
                    sp.dma_start(block3(w[:, q, 1, :]), w_view[:, :, bass.ds(f * P + D_FF, P)]).then_inc(win_loaded[q], 16)

                def weights_out(f, q):
                    wait(sp, wout_lo_done, f - 1)
                    sp.dma_start(w[:, q, 2, :], d["w_ffn_out"][bass.ds(f * P, P), :]).then_inc(wout_loaded[q], 16)

                for t in range(TILES):
                    wait(sp, tp_done, 2 * (t - 1))
                    wait(sp, y_started, t - 1)
                    sp.dma_start(x[:, t % 2, :], d["x1"][first_row + t * P:first_row + (t + 1) * P, :]).then_inc(x_loaded[t % 2], 16)
                    if t < 2:
                        weights_in(t, t)
                for q in range(2):
                    weights_out(q, q)
                with sp.Fori(1, FB // 2) as i:
                    for q in range(2):
                        weights_in(2 * i + q, q)
                    for q in range(2):
                        weights_out(2 * i + q, q)
                for t in range(TILES):
                    if t in POOL_TILES:
                        sp.wait_ge(out_done, 1 + POOL_TILES.index(t))
                    else:
                        sp.wait_ge(out_by_vec, t - len([u for u in POOL_TILES if u < t]) + 1)
                    sp.dma_start(d["y"][first_row + t * P:first_row + (t + 1) * P, :], y[:, t, :]).then_inc(stored, 16)
                sp.wait_ge(stored, 16 * TILES)

            @block.gpsimd
            def _(pool):
                nc.gpsimd.memset(neg_half[:, :], -0.5).then_inc(half_made, 1)
                pool.wait_ge(half_made, 1)
                pool.wait_ge(const_loaded, 48)

                def lo(x, q, hi_done, count, done):
                    pool.wait_ge(hi_done, count)
                    nc.gpsimd.tensor_tensor(w_lo[:, q, x, :], w[:, q, x, :], w_hi[:, q, x, :].bitcast(F32), ALU.subtract).then_inc(done, 1)

                def pair(i):
                    for q in range(2):
                        for x in range(2):
                            lo(x, q, win_hi_done, 2 * (2 * i + q) + x + 1, win_lo_done)
                    for q in range(2):
                        lo(2, q, wout_hi_done, 2 * i + q + 1, wout_lo_done)

                pair(0)
                with pool.Fori(1, FB // 2) as i:
                    pair(i)
                for t in range(TILES):
                    pool.wait_ge(var_done, t + 1)
                    nc.gpsimd.tensor_tensor(rstd[:, t:t + 1], mv[:, t, 1:2], neg_half[:, :], ALU.pow).then_inc(rstd_done, 1)
                for t in range(TILES):
                    if t in POOL_TILES:
                        pool.wait_ge(gained, t + 1)
                        nc.gpsimd.tensor_tensor(y[:, t, :], y[:, t, :], bias[:, :], ALU.add).then_inc(out_done, 1)

            @block.scalar
            def _(act):
                def split_in(f, q, i):
                    act.wait_ge(win_loaded[q], 32 * (i + 1))
                    wait(act, gu_done, 2 * (f - 1))
                    for x in range(2):
                        nc.scalar.activation(w_hi[:, q, x, :], w[:, q, x, :], ACT.Copy).then_inc(win_hi_done, 1)

                def split_out(q, i):
                    act.wait_ge(wout_loaded[q], 16 * (i + 1))
                    wait(act, dn_done, 12 * i)
                    nc.scalar.activation(w_hi[:, q, 2, :], w[:, q, 2, :], ACT.Copy).then_inc(wout_hi_done, 1)

                def silu(f, q):
                    for g in range(2):
                        n = 2 * f + g
                        act.wait_ge(gu_done, n + 1)
                        wait(act, a_done, n)
                        nc.scalar.activation(th[:, :], gu[:, g, 0, 0:GRP], ACT.Tanh, scale=0.5).then_inc(th_done, 1)
                        act.wait_ge(a_done, n + 1)
                        nc.scalar.activation(a_hi[:, q, g * GRP:(g + 1) * GRP], a[:, :], ACT.Copy).then_inc(a_hi_done, 1)

                split_in(0, 0, 0)
                for t in range(TILES):
                    for b in range(2):
                        act.wait_ge(tp_done, 2 * t + b + 1)
                        nc.scalar.activation(x_hi[:, 4 * b:4 * b + 4, t * P:(t + 1) * P],
                                             dn[:, 2 * (t % 2) + b, :].rearrange("p (k c) -> p k c", k=4), ACT.Copy).then_inc(x_hi_done, 1)
                split_in(1, 1, 0)
                split_out(0, 0)
                split_out(1, 0)

                def pair(i):
                    for q in range(2):
                        silu(2 * i + q, q)
                        split_in(2 * i + 2 + q, q, i + 1)
                    for q in range(2):
                        split_out(q, i + 1)

                pair(0)
                with act.Fori(1, FB // 2 - 1) as i:
                    pair(i)
                for q in range(2):
                    silu(FB - 2 + q, q)
                for t in range(TILES):
                    act.wait_ge(nmr_done, t + 1)
                    nc.scalar.activation(y[:, t, :], y[:, t, :], ACT.Identity, bias=nmr[:, t:t + 1], scale=rstd[:, t:t + 1]).then_inc(normed, 1)

            @block.vector
            def _(dve):
                dve.wait_ge(const_loaded, 48)
                for t in range(TILES):
                    dve.wait_ge(x_loaded[t % 2], 16 * (t // 2 + 1))
                    nc.vector.tensor_scalar(y[:, t, :], x[:, t % 2, :], ALPHA, None, ALU.mult).then_inc(y_started, 1)
                    for b in range(2):
                        dve.wait_ge(x_hi_done, 2 * t + b + 1)
                        at = x_hi[:, 4 * b:4 * b + 4, t * P:(t + 1) * P]
                        nc.vector.tensor_tensor(x_lo[:, 4 * b:4 * b + 4, t * P:(t + 1) * P],
                                                dn[:, 2 * (t % 2) + b, :].rearrange("p (k c) -> p k c", k=4), at.bitcast(F32), ALU.subtract).then_inc(x_lo_done, 1)
                dve.wait_ge(y_started, TILES)
                step = Tally(vec)

                def silu(f, q):
                    for g in range(2):
                        n = 2 * f + g
                        dve.wait_ge(th_done, n + 1)
                        wait(dve, a_hi_done, n)
                        v = step.inc(nc.vector.scalar_tensor_tensor(out=th[:, :], in0=th[:, :], scalar=1.0, in1=gu[:, g, 0, 0:GRP], op0=ALU.add, op1=ALU.mult))
                        dve.wait_ge(vec, v)
                        nc.vector.scalar_tensor_tensor(out=a[:, :], in0=th[:, :], scalar=0.5, in1=gu[:, g, 1, 0:GRP],
                                                       op0=ALU.mult, op1=ALU.mult).then_inc(a_done, 1)
                        dve.wait_ge(a_hi_done, n + 1)
                        cols = slice(g * GRP, (g + 1) * GRP)
                        nc.vector.tensor_tensor(a_lo[:, q, cols], a[:, :], a_hi[:, q, cols].bitcast(F32), ALU.subtract).then_inc(a_lo_done, 1)

                def add(i):
                    for n in range(12):
                        t, c = n // 2, slice(n % 2 * 512, (n % 2 + 1) * 512)
                        dve.wait_ge(dn_done, 12 * i + n + 1)
                        wait(dve, y_added, 12 * (i - 1) + n + 1)
                        nc.vector.tensor_tensor(y[:, t, c], dn[:, n % 4, :], y[:, t, c], ALU.add).then_inc(y_added, 1)

                def pair(i):
                    step.enter(4 * i)
                    silu(2 * i, 0)
                    silu(2 * i + 1, 1)
                    add(i)
                    assert step.k == 4

                pair(0)
                with dve.Fori(1, FB // 2) as i:
                    pair(i)
                step.enter(4 * (FB // 2))
                dve.wait_ge(y_added, 12 * (FB // 2))
                for t in range(TILES):
                    nc.vector.bn_stats(stats[:, t, 0:6], y[:, t, 0:512])
                    v = step.inc(nc.vector.bn_stats(stats[:, t, 6:12], y[:, t, 512:1024]))
                for t in range(TILES):
                    dve.wait_ge(vec, v - TILES + 1 + t)
                    w = step.inc(nc.vector.bn_aggr(mv[:, t, :], stats[:, t, :]))
                for t in range(TILES):
                    dve.wait_ge(vec, w - TILES + 1 + t)
                    nc.vector.tensor_scalar(mv[:, t, 1:2], mv[:, t, 1:2], LN_EPS, None, ALU.add).then_inc(var_done, 1)
                for t in range(TILES):
                    dve.wait_ge(rstd_done, t + 1)
                    nc.vector.scalar_tensor_tensor(out=nmr[:, t:t + 1], in0=mv[:, t, 0:1], scalar=-1.0, in1=rstd[:, t:t + 1],
                                                   op0=ALU.mult, op1=ALU.mult).then_inc(nmr_done, 1)
                for t in range(TILES):
                    dve.wait_ge(normed, t + 1)
                    nc.vector.tensor_tensor(y[:, t, :], y[:, t, :], gain[:, :], ALU.mult).then_inc(gained, 1)
                    if t not in POOL_TILES:
                        dve.wait_ge(gained, t + 1)
                        nc.vector.tensor_tensor(y[:, t, :], y[:, t, :], bias[:, :], ALU.add).then_inc(out_by_vec, 1)

            @block.tensor
            def _(pe):
                pe.wait_ge(const_loaded, 48)
                for t in range(TILES):
                    pe.wait_ge(x_loaded[t % 2], 16 * (t // 2 + 1))
                    wait(pe, x_lo_done, 2 * (t - 1))
                    for b in range(2):
                        for k in range(4):
                            last = nc.tensor.transpose(dn[:, 2 * (t % 2) + b, k * P:(k + 1) * P], x[:, t % 2, (4 * b + k) * P:(4 * b + k + 1) * P], ident[:, :])
                        last.then_inc(tp_done, 1)
                pe.wait_ge(x_lo_done, 2 * TILES)

                def gate_up(f, q):
                    pe.wait_ge(win_lo_done, 2 * (f + 1))
                    for g in range(2):
                        wait(pe, a_done, 2 * (f - 1) + g + 1)
                        for m in range(2):
                            parts = [(ww, xx, k) for k in range(KT) for ww, xx in ((w_hi, x_hi), (w_lo, x_hi), (w_hi, x_lo))]
                            for j, (ww, xx, k) in enumerate(parts):
                                last = nc.tensor.matmul(gu[:, g, m, 0:GRP], ww[:, q, m, k * P:(k + 1) * P], xx[:, k, g * GRP:(g + 1) * GRP],
                                                        start=(j == 0), stop=(j == len(parts) - 1))
                        last.then_inc(gu_done, 1)

                def down(i):
                    pe.wait_ge(wout_lo_done, 2 * (i + 1))
                    for n in range(12):
                        t, c = n // 2, slice(n % 2 * 512, (n % 2 + 1) * 512)
                        pe.wait_ge(a_lo_done, 4 * i + (3 if t < TILES // 2 else 4))
                        wait(pe, y_added, 12 * i + n - 3)
                        parts = [(aa, ww, q) for q in range(2) for aa, ww in ((a_hi, w_hi), (a_hi, w_lo), (a_lo, w_hi))]
                        for j, (aa, ww, q) in enumerate(parts):
                            last = nc.tensor.matmul(dn[:, n % 4, :], aa[:, q, t * P:(t + 1) * P], ww[:, q, 2, c],
                                                    start=(j == 0), stop=(j == len(parts) - 1))
                        last.then_inc(dn_done, 1)

                def pair(i):
                    gate_up(2 * i, 0)
                    gate_up(2 * i + 1, 1)
                    down(i)

                pair(0)
                with pe.Fori(1, FB // 2) as i:
                    pair(i)


def build(nc, d, upto=99):
    with ExitStack() as keep:
        h_hi = keep.enter_context(nc.sbuf_tensor("h_hi", [P, KT, (NT + 1) * P], F32R))
        h_lo = keep.enter_context(nc.sbuf_tensor("h_lo", [P, KT, (NT + 1) * P], F32R))
        project(nc, d, (h_hi, h_lo))
        if upto >= 2:
            columns(nc, d, (h_hi, h_lo))
        if upto >= 3:
            qkv(nc, d, (h_hi, h_lo))
    if upto >= 4:
        attend(nc, d)
    if upto >= 5:
        scan(nc, d)
    if upto >= 7:
        mixout(nc, d)
    if upto >= 8:
        ffn(nc, d)


SCRATCH = {"h": (T_REAL, D), "rkv": (T_REAL + 2 * N_META, 3 * RW), "lora": (P, T_REAL + 2 * N_META),
           "qkv": ((NT + 1) * P, QKV), "mix": (T_REAL, D), "scan": (2, T_REAL, RW + RH), "x1": (T_REAL, D)}


def layout(inputs, np):
    f = lambda n: np.ascontiguousarray(inputs[n])
    a = {}
    a["x"] = np.concatenate([f("x_prompt")[0], f("x_sample")[0], f("meta_tokens"),
                             np.zeros((P - N_META, D), np.float32)], axis=0)
    a["w_in"] = f("w_in")[0]
    a["mu"] = np.ascontiguousarray(f("shift_mu")[0].reshape(2, MB, P).transpose(2, 0, 1))
    for n in ("ln_in_g", "ln_in_b", "q_gain", "k_gain", "ln1_g", "ln1_b", "ln2_g", "ln2_b", "k_k", "k_a", "gn_g", "gn_b"):
        a[n] = f(n).reshape(-1)
    a["r_k"] = f("r_k").reshape(-1)
    a["lora_up"] = np.ascontiguousarray(np.stack([np.concatenate([f(w)[0], f(b)[0][:, None]], axis=1).transpose(1, 0, 2)
                                                  for w, b in (("decay_up", "decay_w0"), ("iclr_up", "iclr_a0"))], axis=2))
    a["gate_up"] = f("gate_up")[0]
    a["w_out"], a["w_ffn_in"], a["w_ffn_out"] = f("w_out")[0], f("w_ffn_in")[0], f("w_ffn_out")[0]
    a["ident"] = np.eye(P, dtype=np.float32)
    a.update(tables(np))
    return a


def tables(np):
    freqs = HEAD // 4
    grid = 64
    pos = np.arange(max(SEQS))
    inv = 10000.0 ** (-np.arange(freqs, dtype=np.float64) / freqs)
    cos, sin = np.ones((NT + 1, P, HEAD)), np.zeros((NT + 1, P, HEAD))
    for t in range(NT):
        p = pos[(t if t < 4 else t - 4) * P:][:P]
        for axis, at in enumerate((p // grid, p % grid)):
            ang = at[:, None] * inv
            for half in range(2):
                c = slice(axis * 32 + half * 16, axis * 32 + half * 16 + 16)
                cos[t, :, c] = np.cos(ang)
                sin[t, :, c] = np.sin(ang) * (-1 if half == 0 else 1)
    i = np.arange(P)
    same = i[:, None] // CHUNK == i[None, :] // CHUNK
    tri = np.stack([same & (i[:, None] <= i[None, :]), same & (i[:, None] >= i[None, :])], axis=1)
    c = np.tile(np.arange(CHUNK), 2)[:, None]
    t = np.arange(CHUNK)[None, :]
    gram = np.stack([np.stack([c < t, c <= t], axis=1), np.stack([c > t, c >= t], axis=1)], axis=1)
    level = np.stack([np.stack([(c >> l ^ 1 == t >> l) & (after if z == 0 else before)
                                for l in range(LEVELS)], axis=1) for z, (after, before) in enumerate(((c > t, c < t),) * 2)], axis=1)
    keep = np.ones((P, 3, STEPS))
    first = SEQS[0] // P
    keep[:, 0, first - 1] = 0
    keep[:, 1, STEPS - first - 1] = 0
    keep[:, 2] = 1 - keep[:, 0]
    masks = {"eye": c == t, "tri": tri, "halves": i[:, None] // CHUNK == np.arange(2)[None, :], "gram_mask": gram,
             "level_mask": level, "keep": keep}
    out = {"cos": cos, "sin": sin, **masks}
    return {n: np.ascontiguousarray(v.astype(np.float32)) for n, v in out.items()}


def declare(nc, arrays, scratch_kind=None):
    d = {n: nc.dram_tensor(f"in_{n}", a.shape, mybir.dt.from_np(a.dtype), kind="ExternalInput").ap() for n, a in arrays.items()}
    for n, shape in SCRATCH.items():
        d[n] = nc.dram_tensor(f"scratch_{n}", shape, F32, kind=scratch_kind or "Internal").ap()
    d["y"] = nc.dram_tensor("out_y", (T_REAL, D), F32, kind="ExternalOutput").ap()
    return d


def kernel(**inputs):
    import numpy as np
    import concourse.bacc as bacc
    from concourse.bass_utils import run_bass_kernel_spmd

    nc = bacc.Bacc("TRN2", target_bir_lowering=False, num_devices=1)
    arrays = layout(inputs, np)
    build(nc, declare(nc, arrays))
    r = run_bass_kernel_spmd(nc, [{f"in_{n}": a for n, a in arrays.items()}], core_ids=[0])
    y = r.results[0]["out_y"]
    return y[0:SEQS[0]][None], y[SEQS[0]:][None]
```
